# Optimizing a Trainium2 kernel written in Bass

```python
import jax
import jax.numpy as jnp
from jax import lax
import numpy as np
import jax, jax.numpy as jnp

D_MODEL = 1024
BATCH = 1
SEQ = 256
DEPTH = 2

GRID_W = 64
CTX_LEN = 256

N_HEADS = 8
N_KV_HEADS = 2
HEAD_DIM = 128
Q_PER_KV = N_HEADS // N_KV_HEADS
ROPE_THETA = 10000.0
Q_BLOCK = 128

GLA_HEADS = 4
GLA_DK = D_MODEL // 2 // GLA_HEADS
GLA_DV = D_MODEL // GLA_HEADS
GLA_RANK = 16
GLA_TAU = 16.0
GLA_CHUNK = 64

CONV_CH = D_MODEL
CONV_WIDTH = 31

D_FF = -(-8 * D_MODEL // (3 * 256)) * 256

ALPHA = (2.0 * DEPTH) ** 0.25
BETA = (8.0 * DEPTH) ** -0.25
NORM_EPS = 1e-6

ATT_Q = N_HEADS * HEAD_DIM
ATT_KV = N_KV_HEADS * HEAD_DIM
GLA_K = GLA_HEADS * GLA_DK
GLA_V = GLA_HEADS * GLA_DV
N_BRANCH = 3
MEM_SPLITS = (ATT_KV, ATT_KV, GLA_K, GLA_V, 2 * GLA_RANK)
REST_SPLITS = (ATT_Q, GLA_K, GLA_V, 2 * CONV_CH, N_BRANCH * D_MODEL)
MEM_COLS = sum(MEM_SPLITS)
IN_COLS = MEM_COLS + sum(REST_SPLITS)


def _split(a, sizes):
    return jnp.split(a, np.cumsum(sizes)[:-1].tolist(), axis=-1)

def _layernorm(x, g=None, b=None):
    xf = x.astype(jnp.float32)
    xc = xf - jnp.mean(xf, -1, keepdims=True)
    y = xc * lax.rsqrt(jnp.mean(xc * xc, -1, keepdims=True) + NORM_EPS)
    if g is not None:
        y = y * g.astype(jnp.float32) + b.astype(jnp.float32)
    return y.astype(x.dtype)

def _rmsnorm(x, g):
    xf = x.astype(jnp.float32)
    y = xf * lax.rsqrt(jnp.mean(xf * xf, -1, keepdims=True) + NORM_EPS)
    return (y * g.astype(jnp.float32)).astype(x.dtype)

def _modulate(x, shift, scale):
    return _layernorm(x) * (1.0 + scale) + shift

def _post(x, f, gate, g, b):
    return _layernorm(ALPHA * x + gate * f, g, b)

def _heads(a, n):
    B, L, _ = a.shape
    return a.reshape(B, L, n, -1).transpose(0, 2, 1, 3)

def _flip(a):
    return a[:, :, ::-1]

def _axial_rope(rows):
    t = jnp.arange(rows * GRID_W)
    row = (t // GRID_W).astype(jnp.float32)
    col = (t % GRID_W).astype(jnp.float32)
    half = HEAD_DIM // 2
    inv = ROPE_THETA ** (-jnp.arange(0, half, 2, dtype=jnp.float32) / half)
    ang = jnp.concatenate([row[:, None] * inv, col[:, None] * inv], axis=-1)
    return jnp.cos(ang), jnp.sin(ang)

def _apply_rope(x, cos, sin):
    xf = x.astype(jnp.float32)
    x1, x2 = xf[..., 0::2], xf[..., 1::2]
    y = jnp.stack([x1 * cos - x2 * sin, x1 * sin + x2 * cos], axis=-1)
    return y.reshape(x.shape).astype(x.dtype)

def _sdpa(q, k, v):
    s = jnp.einsum('bkgqd,bkld->bkgql', q, k, preferred_element_type=jnp.float32) * (HEAD_DIM ** -0.5)
    p = jax.nn.softmax(s, axis=-1)
    return jnp.einsum('bkgql,bkld->bkgqd', p.astype(v.dtype), v)

def _attend_blocks(q, k_all, v_all):
    B, Hk, G, S, Dh = q.shape
    nb = S // Q_BLOCK
    qb = jnp.moveaxis(q.reshape(B, Hk, G, nb, Q_BLOCK, Dh), 3, 0)
    o = lax.map(lambda blk: _sdpa(blk, k_all, v_all), qb)
    return jnp.moveaxis(o, 0, 3).reshape(B, Hk, G, S, Dh)

def _gla_log_gates(glr, w_a2, b_a):
    B, L, _ = glr.shape
    z = jnp.einsum('blnr,nrk->nblk', glr.reshape(B, L, 2, GLA_RANK), w_a2) + b_a[:, None, None, :]
    lg = jax.nn.log_sigmoid(z.astype(jnp.float32)) / GLA_TAU
    lg = lg.reshape(2, B, L, GLA_HEADS, GLA_DK).transpose(0, 1, 3, 2, 4)
    return lg[0], lg[1]

def _gla_scan(q, k, v, logg, s0):
    B, H, L, dk = q.shape
    dv = v.shape[-1]
    n = L // GLA_CHUNK

    def chunks(a):
        a = a.astype(jnp.float32)
        return a.reshape(B, H, n, GLA_CHUNK, a.shape[-1]).transpose(2, 0, 1, 3, 4)

    lower = jnp.tril(jnp.ones((GLA_CHUNK, GLA_CHUNK), dtype=bool))[:, :, None]

    def step(s, inp):
        qc, kc, vc, gc = inp
        b = jnp.cumsum(gc, axis=2)
        rel = jnp.where(lower, b[:, :, :, None, :] - b[:, :, None, :, :], -jnp.inf)
        a = jnp.einsum('bhid,bhjd,bhijd->bhij', qc, kc, jnp.exp(rel))
        o = jnp.einsum('bhid,bhde->bhie', qc * jnp.exp(b), s) + jnp.einsum('bhij,bhje->bhie', a, vc)
        b_end = b[:, :, -1:, :]
        s = jnp.exp(b_end[:, :, 0, :, None]) * s + jnp.einsum('bhjd,bhje->bhde', kc * jnp.exp(b_end - b), vc)
        return s, o

    s_end, o = lax.scan(step, s0, (chunks(q), chunks(k), chunks(v), chunks(logg)))
    return o.transpose(1, 2, 0, 3, 4).reshape(B, H, L, dv).astype(v.dtype), s_end

def _gla_final_state(k, v, logg):
    b = jnp.cumsum(logg, axis=2)
    w = jnp.exp(b[:, :, -1:, :] - b)
    return jnp.einsum('bhld,bhle->bhde', k.astype(jnp.float32) * w, v.astype(jnp.float32))

def _gla_bidir(qg, kg, vg, gf, gb, s_f, s_b):
    o_f, s_f_end = _gla_scan(qg, kg, vg, gf, s_f)
    o_b, s_b_end = _gla_scan(_flip(qg), _flip(kg), _flip(vg), _flip(gb), s_b)
    return o_f + _flip(o_b), s_f_end, s_b_end

def _mem_parts(pm, p):
    k, v, kg, vg, glr = _split(pm, MEM_SPLITS)
    k = _rmsnorm(_heads(k, N_KV_HEADS), p['k_norm'])
    v = _heads(v, N_KV_HEADS)
    gf, gb = _gla_log_gates(glr, p['gla_w_a2'], p['gla_b_a'])
    return k, v, _heads(kg, GLA_HEADS), _heads(vg, GLA_HEADS), gf, gb

def _rest_parts(pr, p):
    q, qg, r, glu, gates = _split(pr, REST_SPLITS)
    B, L, _ = q.shape
    q = _rmsnorm(q.reshape(B, L, N_KV_HEADS, Q_PER_KV, HEAD_DIM), p['q_norm']).transpose(0, 2, 3, 1, 4)
    qg = _heads(qg, GLA_HEADS) * (GLA_DK ** -0.5)
    return q, qg, r, glu, gates

def _conv_module(glu, p):
    a, g = jnp.split(glu, 2, axis=-1)
    y = a * jax.nn.sigmoid(g)
    pad = CONV_WIDTH // 2
    y = lax.conv_general_dilated(y, p['conv_w_dw'].astype(y.dtype), (1,), [(pad, pad)],
                                 dimension_numbers=('NWC', 'WIO', 'NWC'),
                                 feature_group_count=CONV_CH) + p['conv_b_dw']
    y = jax.nn.silu(_layernorm(y, p['conv_ln_g'], p['conv_ln_b']))
    return y @ p['w_conv_o']

def _merge(o_att, o_gla, r, glu, gates, p):
    B, L, _ = r.shape
    y_att = o_att.transpose(0, 3, 1, 2, 4).reshape(B, L, ATT_Q) @ p['w_att_o']
    o_gla = _rmsnorm(o_gla, p['gla_norm']).transpose(0, 2, 1, 3).reshape(B, L, GLA_V)
    y_gla = (o_gla * jax.nn.silu(r)) @ p['w_gla_o']
    y_conv = _conv_module(glu, p)
    g_att, g_gla, g_conv = jnp.split(jax.nn.sigmoid(gates), N_BRANCH, axis=-1)
    return (g_att * y_att + g_gla * y_gla + g_conv * y_conv) @ p['w_out']

def _context_mixer(h, p):
    proj = h @ p['w_in']
    k, v, kg, vg, gf, gb = _mem_parts(proj[..., :MEM_COLS], p)
    q, qg, r, glu, gates = _rest_parts(proj[..., MEM_COLS:], p)
    o_att = _sdpa(q, k, v)
    zero = jnp.zeros(kg.shape[:2] + (GLA_DK, GLA_DV), jnp.float32)
    o_gla, s_f, s_b = _gla_bidir(qg, kg, vg, gf, gb, zero, zero)
    return _merge(o_att, o_gla, r, glu, gates, p), (k, v, s_f, s_b)

def _context_memory(h, p):
    k, v, kg, vg, gf, gb = _mem_parts(h @ p['w_in'][:, :MEM_COLS], p)
    s_f = _gla_final_state(kg, vg, gf)
    s_b = _gla_final_state(_flip(kg), _flip(vg), _flip(gb))
    return k, v, s_f, s_b

def _latent_mixer(h, mem, cos, sin, p):
    proj = h @ p['w_in']
    k, v, kg, vg, gf, gb = _mem_parts(proj[..., :MEM_COLS], p)
    q, qg, r, glu, gates = _rest_parts(proj[..., MEM_COLS:], p)
    k_ctx, v_ctx, s_f, s_b = mem
    k_all = jnp.concatenate([_apply_rope(k, cos, sin), k_ctx], axis=2)
    v_all = jnp.concatenate([v, v_ctx], axis=2)
    o_att = _attend_blocks(_apply_rope(q, cos, sin), k_all, v_all)
    o_gla, _, _ = _gla_bidir(qg, kg, vg, gf, gb, s_f, s_b)
    return _merge(o_att, o_gla, r, glu, gates, p)

def _ffn(h, p):
    return (jax.nn.silu(h @ p['w_ff_gate']) * (h @ p['w_ff_up'])) @ p['w_ff_down']

def first_inputs(seed: int = 0) -> dict:
    key = jax.random.key(seed)
    ks = jax.random.split(key, 27)

    def nrm(i, shape, scale):
        return jax.random.normal(ks[i], shape, jnp.float32) * scale

    D = D_MODEL
    L = DEPTH
    return {
        'x': nrm(0, (BATCH, SEQ, D), 1.0),
        'c': nrm(1, (BATCH, D), 1.0),
        'ctx': nrm(2, (BATCH, CTX_LEN, D), 1.0),
        'c_ctx': nrm(3, (D,), 1.0),
        'w_ada': nrm(4, (L, D, 6 * D), 0.3 * D ** -0.5),
        'b_ada': nrm(5, (L, 6 * D), 0.02),
        'w_in': nrm(6, (L, D, IN_COLS), D ** -0.5),
        'q_norm': 1.0 + nrm(7, (L, HEAD_DIM), 0.02),
        'k_norm': 1.0 + nrm(8, (L, HEAD_DIM), 0.02),
        'w_att_o': nrm(9, (L, ATT_Q, D), ATT_Q ** -0.5),
        'gla_w_a2': nrm(10, (L, 2, GLA_RANK, GLA_K), GLA_RANK ** -0.5),
        'gla_b_a': nrm(11, (L, 2, GLA_K), 0.5),
        'gla_norm': 1.0 + nrm(12, (L, GLA_DV), 0.02),
        'w_gla_o': nrm(13, (L, GLA_V, D), GLA_V ** -0.5),
        'conv_w_dw': nrm(14, (L, CONV_WIDTH, 1, CONV_CH), CONV_WIDTH ** -0.5),
        'conv_b_dw': nrm(15, (L, CONV_CH), 0.02),
        'conv_ln_g': 1.0 + nrm(16, (L, CONV_CH), 0.02),
        'conv_ln_b': nrm(17, (L, CONV_CH), 0.02),
        'w_conv_o': nrm(18, (L, CONV_CH, D), CONV_CH ** -0.5),
        'w_out': nrm(19, (L, D, D), BETA * D ** -0.5),
        'ln1_g': 1.0 + nrm(20, (L, D), 0.02),
        'ln1_b': nrm(21, (L, D), 0.02),
        'w_ff_gate': nrm(22, (L, D, D_FF), D ** -0.5),
        'w_ff_up': nrm(23, (L, D, D_FF), D ** -0.5),
        'w_ff_down': nrm(24, (L, D_FF, D), BETA * D_FF ** -0.5),
        'ln2_g': 1.0 + nrm(25, (L, D), 0.02),
        'ln2_b': nrm(26, (L, D), 0.02),
    }

def first_block(x, c, ctx, c_ctx, w_ada, b_ada, w_in, q_norm, k_norm, w_att_o, gla_w_a2, gla_b_a,
              gla_norm, w_gla_o, conv_w_dw, conv_b_dw, conv_ln_g, conv_ln_b, w_conv_o, w_out,
              ln1_g, ln1_b, w_ff_gate, w_ff_up, w_ff_down, ln2_g, ln2_b):
    rows = x.shape[1] // GRID_W
    cos, sin = _axial_rope(rows)
    silu_c = jax.nn.silu(c)
    silu_cc = jax.nn.silu(c_ctx)
    xc = ctx
    for l in range(DEPTH):
        p = {'w_in': w_in[l], 'q_norm': q_norm[l], 'k_norm': k_norm[l], 'w_att_o': w_att_o[l],
             'gla_w_a2': gla_w_a2[l], 'gla_b_a': gla_b_a[l], 'gla_norm': gla_norm[l],
             'w_gla_o': w_gla_o[l], 'conv_w_dw': conv_w_dw[l], 'conv_b_dw': conv_b_dw[l],
             'conv_ln_g': conv_ln_g[l], 'conv_ln_b': conv_ln_b[l], 'w_conv_o': w_conv_o[l],
             'w_out': w_out[l], 'w_ff_gate': w_ff_gate[l], 'w_ff_up': w_ff_up[l],
             'w_ff_down': w_ff_down[l]}
        last = l == DEPTH - 1
        mod = (silu_c @ w_ada[l] + b_ada[l])[:, None, :]
        sh1, sc1, g1, sh2, sc2, g2 = jnp.split(mod, 6, axis=-1)
        n_cm = 2 if last else 6
        mod_c = jnp.split(silu_cc @ w_ada[l][:, :n_cm * D_MODEL] + b_ada[l][:n_cm * D_MODEL], n_cm)
        hc = _modulate(xc, mod_c[0], mod_c[1])
        if last:
            mem = _context_memory(hc, p)
        else:
            yc, mem = _context_mixer(hc, p)
            xc = _post(xc, yc, mod_c[2], ln1_g[l], ln1_b[l])
            xc = _post(xc, _ffn(_modulate(xc, mod_c[3], mod_c[4]), p), mod_c[5], ln2_g[l], ln2_b[l])
        x = _post(x, _latent_mixer(_modulate(x, sh1, sc1), mem, cos, sin, p), g1, ln1_g[l], ln1_b[l])
        x = _post(x, _ffn(_modulate(x, sh2, sc2), p), g2, ln2_g[l], ln2_b[l])
    return x


HEAD_DIM_2 = 64
FOX_HEADS = 4
NSA_HEADS = 8
NSA_KV_GROUPS = 2
DIL_HEADS = 4
MIX_WIDTH = (FOX_HEADS + NSA_HEADS + DIL_HEADS) * HEAD_DIM_2
DIL_PATTERNS = ((128, 1), (512, 4), (2048, 16))
ROPE_THETA_2 = 500000.0
ROPE_DIM = HEAD_DIM_2 // 4
CMP_BLOCK = 32
CMP_STRIDE = 16
CMP_HIDDEN = 4 * HEAD_DIM_2
SEL_BLOCK = 64
SEL_TOPK = 16
NSA_WINDOW = 512
D_FF_2 = 2816
CONV_WIDTH_2 = 3
RMS_EPS = 1e-6
NEG_INF = -1e30
FORCE_SCORE = 1e9
ATTN_SCALE = HEAD_DIM_2 ** -0.5
KV_W = NSA_KV_GROUPS * HEAD_DIM_2
IN_SPLITS = (FOX_HEADS * HEAD_DIM_2,) * 3 + (FOX_HEADS,) + (NSA_HEADS * HEAD_DIM_2,) + (KV_W,) * 6 + (3 * NSA_HEADS,) + (DIL_HEADS * HEAD_DIM_2,) * 3
N_IN = sum(IN_SPLITS)


def rms_norm(x, g):
    xf = x.astype(jnp.float32)
    y = xf * lax.rsqrt(jnp.mean(xf * xf, axis=-1, keepdims=True) + RMS_EPS)
    return (y * g.astype(jnp.float32)).astype(x.dtype)

def rope_tables(positions):
    half = ROPE_DIM // 2
    inv_freq = ROPE_THETA_2 ** (-2.0 * jnp.arange(half, dtype=jnp.float32) / ROPE_DIM)
    ang = positions.astype(jnp.float32)[..., None] * inv_freq
    return jnp.cos(ang)[:, :, None, :], jnp.sin(ang)[:, :, None, :]

def partial_rope(x, cos, sin):
    half = ROPE_DIM // 2
    cos = cos.astype(x.dtype)
    sin = sin.astype(x.dtype)
    x1 = x[..., :half]
    x2 = x[..., half:ROPE_DIM]
    return jnp.concatenate([x1 * cos - x2 * sin, x2 * cos + x1 * sin, x[..., ROPE_DIM:]], axis=-1)

def masked_softmax(scores, mask):
    s = jnp.where(mask, scores, NEG_INF)
    m = jnp.max(s, axis=-1, keepdims=True)
    e = jnp.where(mask, jnp.exp(s - m), 0.0)
    den = jnp.maximum(jnp.sum(e, axis=-1, keepdims=True), 1e-30)
    return e / den, m + jnp.log(den)

def sweep_query_blocks(fn, seq):
    out = lax.map(fn, jnp.arange(seq // Q_BLOCK, dtype=jnp.int32) * Q_BLOCK)
    out = jnp.moveaxis(out, 0, 1)
    return out.reshape((out.shape[0], seq) + out.shape[3:])

def fox_attention(q, k, v, log_f):
    S = q.shape[1]
    c = jnp.cumsum(log_f, axis=1)
    c_k = jnp.transpose(c, (0, 2, 1))[:, :, None, :]
    kpos = jnp.arange(S)

    def block(start):
        qb = lax.dynamic_slice_in_dim(q, start, Q_BLOCK, axis=1)
        cb = lax.dynamic_slice_in_dim(c, start, Q_BLOCK, axis=1)
        qpos = start + jnp.arange(Q_BLOCK)
        s = jnp.einsum('bqhd,bkhd->bhqk', qb, k, preferred_element_type=jnp.float32) * ATTN_SCALE
        s = s + jnp.transpose(cb, (0, 2, 1))[..., None] - c_k
        p, _ = masked_softmax(s, kpos[None, :] <= qpos[:, None])
        return jnp.einsum('bhqk,bkhd->bqhd', p.astype(v.dtype), v)

    return sweep_query_blocks(block, S)

def dilated_attention(q, k, v):
    S = q.shape[1]

    def block(start):
        qb = lax.dynamic_slice_in_dim(q, start, Q_BLOCK, axis=1)
        qpos = start + jnp.arange(Q_BLOCK)
        outs, lses = [], []
        for window, dilation in DIL_PATTERNS:
            offs = jnp.arange(window // dilation + 1) * dilation
            idx = qpos[:, None] - offs[None, :]
            valid = idx >= 0
            idx = jnp.maximum(idx, 0)
            kg = jnp.take(k, idx, axis=1)
            vg = jnp.take(v, idx, axis=1)
            s = jnp.einsum('bqhd,bqjhd->bhqj', qb, kg, preferred_element_type=jnp.float32) * ATTN_SCALE
            p, lse = masked_softmax(s, valid[None, None])
            outs.append(jnp.einsum('bhqj,bqjhd->bqhd', p.astype(v.dtype), vg))
            lses.append(lse[..., 0])
        w = jax.nn.softmax(jnp.stack(lses, 0), axis=0)
        w = jnp.transpose(w, (0, 1, 3, 2))[..., None].astype(v.dtype)
        return jnp.sum(w * jnp.stack(outs, 0), axis=0)

    return sweep_query_blocks(block, S)

def nsa_compress(kv, pos_emb, w1, w2):
    S = kv.shape[1]
    n_cmp = (S - CMP_BLOCK) // CMP_STRIDE + 1
    idx = jnp.arange(n_cmp)[:, None] * CMP_STRIDE + jnp.arange(CMP_BLOCK)[None, :]
    win = jnp.take(kv, idx, axis=1) + pos_emb[None, None, :, None, :]
    B, N, L, G, hd = win.shape
    win = jnp.transpose(win, (0, 1, 3, 2, 4)).reshape(B, N, G, L * hd)
    return jax.nn.gelu(win @ w1) @ w2

def nsa_attention(q, kc, vc, ks, vs, kw, vw, gates, cmp_pos_k, cmp_w1_k, cmp_w2_k, cmp_pos_v, cmp_w1_v, cmp_w2_v):
    B, S, H, hd = q.shape
    G = NSA_KV_GROUPS
    R = H // G
    k_cmp = nsa_compress(kc, cmp_pos_k, cmp_w1_k, cmp_w2_k)
    v_cmp = nsa_compress(vc, cmp_pos_v, cmp_w1_v, cmp_w2_v)
    n_cmp = k_cmp.shape[1]
    cmp_start = jnp.arange(n_cmp) * CMP_STRIDE
    cmp_end = cmp_start + CMP_BLOCK - 1
    n_sel = S // SEL_BLOCK
    top_k = min(SEL_TOPK, n_sel)
    sel_start = jnp.arange(n_sel) * SEL_BLOCK
    overlap = ((cmp_start[:, None] < sel_start[None, :] + SEL_BLOCK) & (cmp_start[:, None] + CMP_BLOCK > sel_start[None, :])).astype(jnp.float32)
    ks_blk = jnp.transpose(ks.reshape(B, n_sel, SEL_BLOCK, G, hd), (0, 3, 1, 2, 4))
    vs_blk = jnp.transpose(vs.reshape(B, n_sel, SEL_BLOCK, G, hd), (0, 3, 1, 2, 4))
    pad = ((0, 0), (NSA_WINDOW, 0), (0, 0), (0, 0))
    kw_pad = jnp.pad(kw, pad)
    vw_pad = jnp.pad(vw, pad)
    gather_blocks = jax.vmap(jax.vmap(lambda blocks, idx: blocks[idx]))
    blk_id = jnp.arange(n_sel)[None, :]

    def block(start):
        qb = lax.dynamic_slice_in_dim(q, start, Q_BLOCK, axis=1).reshape(B, Q_BLOCK, G, R, hd)
        gb = lax.dynamic_slice_in_dim(gates, start, Q_BLOCK, axis=1).reshape(B, Q_BLOCK, G, R, 3)
        qpos = start + jnp.arange(Q_BLOCK)
        s_c = jnp.einsum('bqgrd,bngd->bgrqn', qb, k_cmp, preferred_element_type=jnp.float32) * ATTN_SCALE
        p_c, _ = masked_softmax(s_c, cmp_end[None, :] <= qpos[:, None])
        o_c = jnp.einsum('bgrqn,bngd->bqgrd', p_c.astype(v_cmp.dtype), v_cmp)
        imp = jnp.einsum('bgrqn,nj->bgqj', p_c, overlap)
        cur = (qpos // SEL_BLOCK)[:, None]
        forced = (blk_id == 0) | (blk_id == cur) | (blk_id == cur - 1)
        future = sel_start[None, :] > qpos[:, None]
        imp = jnp.where(future, NEG_INF, jnp.where(forced, FORCE_SCORE, imp))
        _, sel = lax.top_k(imp, top_k)
        k_sel = gather_blocks(ks_blk, sel).reshape(B, G, Q_BLOCK, top_k * SEL_BLOCK, hd)
        v_sel = gather_blocks(vs_blk, sel).reshape(B, G, Q_BLOCK, top_k * SEL_BLOCK, hd)
        kpos_sel = (sel[..., None] * SEL_BLOCK + jnp.arange(SEL_BLOCK)).reshape(B, G, Q_BLOCK, top_k * SEL_BLOCK)
        mask_s = (kpos_sel <= qpos[None, None, :, None])[:, :, None]
        s_s = jnp.einsum('bqgrd,bgqkd->bgrqk', qb, k_sel, preferred_element_type=jnp.float32) * ATTN_SCALE
        p_s, _ = masked_softmax(s_s, mask_s)
        o_s = jnp.einsum('bgrqk,bgqkd->bqgrd', p_s.astype(v_sel.dtype), v_sel)
        kwb = lax.dynamic_slice_in_dim(kw_pad, start, Q_BLOCK + NSA_WINDOW, axis=1)
        vwb = lax.dynamic_slice_in_dim(vw_pad, start, Q_BLOCK + NSA_WINDOW, axis=1)
        kpos_w = (start - NSA_WINDOW + jnp.arange(Q_BLOCK + NSA_WINDOW))[None, :]
        mask_w = (kpos_w <= qpos[:, None]) & (kpos_w > qpos[:, None] - NSA_WINDOW) & (kpos_w >= 0)
        s_w = jnp.einsum('bqgrd,bkgd->bgrqk', qb, kwb, preferred_element_type=jnp.float32) * ATTN_SCALE
        p_w, _ = masked_softmax(s_w, mask_w)
        o_w = jnp.einsum('bgrqk,bkgd->bqgrd', p_w.astype(vwb.dtype), vwb)
        o = gb[..., 0:1] * o_c + gb[..., 1:2] * o_s + gb[..., 2:3] * o_w
        return o.reshape(B, Q_BLOCK, H, hd)

    return sweep_query_blocks(block, S)

def hybrid_mixer(h, cos, sin, w_in, b_forget, b_nsa_gate, cmp_pos_k, cmp_w1_k, cmp_w2_k, cmp_pos_v, cmp_w1_v, cmp_w2_v, w_out):
    B, S, _ = h.shape
    proj = h @ w_in
    splits = np.cumsum(IN_SPLITS)[:-1].tolist()
    (fq, fk, fv, ff, nq, kc, vc, ks, vs, kw, vw, ng, dq, dk, dv) = jnp.split(proj, splits, axis=-1)

    def heads(t, n):
        return t.reshape(B, S, n, HEAD_DIM_2)

    log_f = jax.nn.log_sigmoid(ff.astype(jnp.float32) + b_forget.astype(jnp.float32))
    o_fox = fox_attention(heads(fq, FOX_HEADS), heads(fk, FOX_HEADS), heads(fv, FOX_HEADS), log_f)
    rope = lambda t, n: partial_rope(heads(t, n), cos, sin)
    gates = jax.nn.sigmoid(ng + b_nsa_gate).reshape(B, S, NSA_HEADS, 3)
    o_nsa = nsa_attention(rope(nq, NSA_HEADS), rope(kc, NSA_KV_GROUPS), heads(vc, NSA_KV_GROUPS),
                          rope(ks, NSA_KV_GROUPS), heads(vs, NSA_KV_GROUPS),
                          rope(kw, NSA_KV_GROUPS), heads(vw, NSA_KV_GROUPS), gates,
                          cmp_pos_k, cmp_w1_k, cmp_w2_k, cmp_pos_v, cmp_w1_v, cmp_w2_v)
    o_dil = dilated_attention(rope(dq, DIL_HEADS), rope(dk, DIL_HEADS), heads(dv, DIL_HEADS))
    mix = jnp.concatenate([o_fox.reshape(B, S, -1), o_nsa.reshape(B, S, -1), o_dil.reshape(B, S, -1)], axis=-1)
    return mix @ w_out

def conv_ffn(h, w_up, conv_w, conv_b, w_down):
    S = h.shape[1]
    u = h @ w_up
    u_pad = jnp.pad(u, ((0, 0), (CONV_WIDTH_2 - 1, 0), (0, 0)))
    c = conv_b + u_pad[:, 0:S] * conv_w[0]
    for j in range(1, CONV_WIDTH_2):
        c = c + u_pad[:, j:j + S] * conv_w[j]
    a, b = jnp.split(c, 2, axis=-1)
    return (jax.nn.silu(a) * b) @ w_down

def second_inputs(seed: int = 0) -> dict:
    key = jax.random.key(seed)
    k = jax.random.split(key, 24)
    nrm = lambda kk, shape, scale: jax.random.normal(kk, shape, jnp.float32) * scale
    x = nrm(k[0], (BATCH, SEQ, D_MODEL), 1.0)
    offset = jax.random.randint(k[1], (BATCH, 1), 0, 1024, dtype=jnp.int32)
    positions = offset + jnp.arange(SEQ, dtype=jnp.int32)[None, :]
    return {
        'x': x,
        'positions': positions,
        'attn_pre_norm': 1.0 + nrm(k[2], (DEPTH, D_MODEL), 0.05),
        'attn_post_norm': 1.0 + nrm(k[3], (DEPTH, D_MODEL), 0.05),
        'ffn_pre_norm': 1.0 + nrm(k[4], (DEPTH, D_MODEL), 0.05),
        'ffn_post_norm': 1.0 + nrm(k[5], (DEPTH, D_MODEL), 0.05),
        'w_in': nrm(k[6], (DEPTH, D_MODEL, N_IN), D_MODEL ** -0.5),
        'b_forget': jax.random.uniform(k[7], (DEPTH, FOX_HEADS), jnp.float32, 1.0, 5.0),
        'b_nsa_gate': nrm(k[8], (DEPTH, 3 * NSA_HEADS), 0.01),
        'cmp_pos_k': nrm(k[9], (DEPTH, CMP_BLOCK, HEAD_DIM_2), 0.1),
        'cmp_w1_k': nrm(k[10], (DEPTH, CMP_BLOCK * HEAD_DIM_2, CMP_HIDDEN), (CMP_BLOCK * HEAD_DIM_2) ** -0.5),
        'cmp_w2_k': nrm(k[11], (DEPTH, CMP_HIDDEN, HEAD_DIM_2), CMP_HIDDEN ** -0.5),
        'cmp_pos_v': nrm(k[12], (DEPTH, CMP_BLOCK, HEAD_DIM_2), 0.1),
        'cmp_w1_v': nrm(k[13], (DEPTH, CMP_BLOCK * HEAD_DIM_2, CMP_HIDDEN), (CMP_BLOCK * HEAD_DIM_2) ** -0.5),
        'cmp_w2_v': nrm(k[14], (DEPTH, CMP_HIDDEN, HEAD_DIM_2), CMP_HIDDEN ** -0.5),
        'w_out': nrm(k[15], (DEPTH, MIX_WIDTH, D_MODEL), MIX_WIDTH ** -0.5),
        'w_up': nrm(k[16], (DEPTH, D_MODEL, 2 * D_FF_2), D_MODEL ** -0.5),
        'conv_w': nrm(k[17], (DEPTH, CONV_WIDTH_2, 2 * D_FF_2), CONV_WIDTH_2 ** -0.5),
        'conv_b': nrm(k[18], (DEPTH, 2 * D_FF_2), 0.01),
        'w_down': nrm(k[19], (DEPTH, D_FF_2, D_MODEL), D_FF_2 ** -0.5),
    }

def second_block(x, positions, attn_pre_norm, attn_post_norm, ffn_pre_norm, ffn_post_norm, w_in, b_forget, b_nsa_gate,
              cmp_pos_k, cmp_w1_k, cmp_w2_k, cmp_pos_v, cmp_w1_v, cmp_w2_v, w_out, w_up, conv_w, conv_b, w_down):
    cos, sin = rope_tables(positions)
    for l in range(DEPTH):
        h = rms_norm(x, attn_pre_norm[l])
        mix = hybrid_mixer(h, cos, sin, w_in[l], b_forget[l], b_nsa_gate[l], cmp_pos_k[l], cmp_w1_k[l], cmp_w2_k[l],
                           cmp_pos_v[l], cmp_w1_v[l], cmp_w2_v[l], w_out[l])
        x = x + rms_norm(mix, attn_post_norm[l])
        h = rms_norm(x, ffn_pre_norm[l])
        x = x + rms_norm(conv_ffn(h, w_up[l], conv_w[l], conv_b[l], w_down[l]), ffn_post_norm[l])
    return x


def setup_inputs(seed=0):
    out = dict(first_inputs(seed))
    for name, value in second_inputs(seed + 1).items():
        if name != "x":
            out[name + "_2"] = value
    return out


def reference(
    x, c, ctx, c_ctx, w_ada, b_ada, w_in, q_norm, k_norm, w_att_o, gla_w_a2, gla_b_a, gla_norm,
    w_gla_o, conv_w_dw, conv_b_dw, conv_ln_g, conv_ln_b, w_conv_o, w_out, ln1_g, ln1_b,
    w_ff_gate, w_ff_up, w_ff_down, ln2_g, ln2_b, positions_2, attn_pre_norm_2, attn_post_norm_2,
    ffn_pre_norm_2, ffn_post_norm_2, w_in_2, b_forget_2, b_nsa_gate_2, cmp_pos_k_2, cmp_w1_k_2,
    cmp_w2_k_2, cmp_pos_v_2, cmp_w1_v_2, cmp_w2_v_2, w_out_2, w_up_2, conv_w_2, conv_b_2,
    w_down_2,
):
    x = first_block(
        x, c, ctx, c_ctx, w_ada, b_ada, w_in, q_norm, k_norm, w_att_o, gla_w_a2, gla_b_a,
        gla_norm, w_gla_o, conv_w_dw, conv_b_dw, conv_ln_g, conv_ln_b, w_conv_o, w_out, ln1_g,
        ln1_b, w_ff_gate, w_ff_up, w_ff_down, ln2_g, ln2_b,
    )
    return second_block(
        x, positions_2, attn_pre_norm_2, attn_post_norm_2, ffn_pre_norm_2, ffn_post_norm_2,
        w_in_2, b_forget_2, b_nsa_gate_2, cmp_pos_k_2, cmp_w1_k_2, cmp_w2_k_2, cmp_pos_v_2,
        cmp_w1_v_2, cmp_w2_v_2, w_out_2, w_up_2, conv_w_2, conv_b_2, w_down_2,
    )


_drawn_inputs = setup_inputs


def setup_inputs(seed=0):
    import zlib

    import numpy as np

    out = dict(_drawn_inputs(seed))
    spreads = {}
    factors = {'ctx': 3.836,
     'c_ctx': 3.323,
     'b_ada': 3.673,
     'q_norm': 39.428,
     'k_norm': 42.207,
     'gla_w_a2': 8.0,
     'gla_b_a': 5.391,
     'gla_norm': 60.843,
     'conv_b_dw': 8.0,
     'conv_ln_g': 31.841,
     'conv_ln_b': 28.435,
     'b_nsa_gate_2': 8.0,
     'cmp_pos_k_2': 4.086,
     'conv_b_2': 4.732}
    for name, (base, spread) in spreads.items():
        noise = np.random.default_rng([zlib.crc32(name.encode()), seed]).standard_normal(out[name].shape)
        drawn = base * np.exp(spread * noise) if base else spread * noise
        out[name] = jnp.asarray(drawn.astype(out[name].dtype))
    for name, factor in factors.items():
        out[name] = (out[name] * factor).astype(out[name].dtype)
    return out
```

```python
from contextlib import ExitStack

import numpy as np

import concourse.bass as bass
from concourse import mybir

ALU = mybir.AluOpType
ACT = mybir.ActivationFunctionType
AXX = mybir.AxisListType.X
F32 = mybir.dt.float32
BF16 = mybir.dt.bfloat16
I32 = mybir.dt.int32

P = 128
DEPTH = 2
EPS = 1e-6
ALPHA = (2.0 * DEPTH) ** 0.25
NSLOT = 9
NFF = 22
SCALE1 = 128.0 ** -0.5
SCALE2 = 0.125
MASKED = -(2.0 ** 100)

COLS = [
    ("b_ada", 48), ("q_norm", 1), ("k_norm", 1), ("gla_norm", 2), ("conv_b_dw", 8),
    ("conv_ln_g", 8), ("conv_ln_b", 8), ("ln1_g", 8), ("ln1_b", 8), ("ln2_g", 8), ("ln2_b", 8),
    ("attn_pre_norm_2", 8), ("attn_post_norm_2", 8), ("ffn_pre_norm_2", 8), ("ffn_post_norm_2", 8),
    ("conv_b_2", 44),
]
COL_AT = {}
_at = 0
for _name, _n in COLS:
    for _l in range(DEPTH):
        COL_AT[_name, _l] = _at
        _at += _n
NCOL = _at


class Engine:

    def __init__(self, name):
        self.name, self.queue, self.count, self.seen = name, [], 0, {}
        self.sem = None

    def wait(self, *tokens):
        for t in tokens:
            if t is None:
                continue
            if isinstance(t, list):
                self.wait(*t)
                continue
            sem, value = t
            if self.seen.get(id(sem), 0) < value:
                self.seen[id(sem)] = value
                self.queue.append(lambda e, sem=sem, value=value: e.wait_ge(sem, value))

    def do(self, make, *tokens):
        self.wait(*tokens)
        self.count += 1
        self.queue.append(lambda e: make(e).then_inc(self.sem, 1))
        return (self.sem, self.count)

    def quiet(self, make, *tokens):
        self.wait(*tokens)
        self.queue.append(make)

    def dma(self, out, in_, sem, *tokens):
        self.wait(*tokens)
        self.queue.append(lambda e: e.dma_start(out, in_).then_inc(sem, 16))

    def now(self):
        return (self.sem, self.count)


class Bank:
    def __init__(self, ap):
        self.ap, self.free = ap, None


def bc(ap, axis, n):
    a = ap.unsqueeze(axis)
    shape = list(a.shape)
    shape[axis] = n
    return a.to_broadcast(shape)


def program(nc, A, out):
    with ExitStack() as ctx:
        def sb(name, shape, dt=F32):
            return ctx.enter_context(nc.sbuf_tensor(name, shape, dt))

        def sem(name):
            return ctx.enter_context(nc.semaphore(name))

        pe, dve, act, pool, sp = (Engine(n) for n in ("pe", "dve", "act", "pool", "sp"))
        for e in (pe, dve, act, pool):
            e.sem = sem("s_" + e.name)
        s_const = sem("s_const")
        s_copy = sem("s_copy")
        s_out = sem("s_out")
        slot_sem = [sem(f"s_w{i}") for i in range(NSLOT)]

        XT = sb("XT", [P, 8, 512])
        HT = sb("HT", [P, 8, 512])
        MG = sb("MG", [P, 8, 512])
        MGF = MG[:, :, :].rearrange("p a b -> p (a b)")
        RING = sb("RING", [P, NSLOT, 1024])
        AR = sb("AR", [P, 20480])
        CM = sb("CM", [P, 8, P])
        CG = sb("CG", [P, 5120])
        ROPE = sb("ROPE", [P, 2, 256])
        COL = sb("COL", [P, NCOL + 1])
        MOD = sb("MOD", [P, 2, 48, 2])
        WA = sb("WA", [33, 2, 512])
        CVW = sb("CVW", [P, 248])
        SM = sb("SM", [P, 256])
        NM = sb("NM", [32, 256])
        RS = sb("RS", [P, 3, 512])
        banks = [Bank(ctx.enter_context(nc.psum_tensor(f"PS{i}", [P, 512], F32))) for i in range(8)]
        turn = [0]

        def ps():
            b = banks[turn[0] % 8]
            turn[0] += 1
            return b

        ONES, M1024, M256, M128, IDENT, R1, R2, ZERO = (CM[:, i, :] for i in range(8))

        def mm(out_, lhsT, rhs, start, stop, *tokens):
            pe.quiet(lambda e: e.matmul(out_, lhsT, rhs, start=start, stop=stop), *tokens)

        def mmt(out_, lhsT, rhs, start, stop, *tokens):
            return pe.do(lambda e: e.matmul(out_, lhsT, rhs, start=start, stop=stop), *tokens)

        def transpose(out_, in_, n, *tokens):
            return pe.do(lambda e: e.transpose(out_, in_, IDENT[0:n, 0:n]), *tokens)

        def tt(eng, out_, a, b, op, *tokens):
            return eng.do(lambda e: e.tensor_tensor(out_, a, b, op), *tokens)

        def ts(eng, out_, a, s1, s2, op0, op1, *tokens):
            if op1 is None:
                return eng.do(lambda e: e.tensor_scalar(out_, a, s1, None, op0), *tokens)
            return eng.do(lambda e: e.tensor_scalar(out_, a, s1, s2, op0, op1), *tokens)

        def stt(out_, a, s, b, op0, op1, *tokens):
            return dve.do(lambda e: e.scalar_tensor_tensor(out=out_, in0=a, scalar=s, in1=b, op0=op0, op1=op1),
                          *tokens)

        def copy(out_, a, *tokens):
            return dve.do(lambda e: e.tensor_copy(out_, a), *tokens)

        def recip(out_, a, *tokens):
            return dve.do(lambda e: e.reciprocal(out_, a), *tokens)

        def rmax(out_, a, *tokens):
            return dve.do(lambda e: e.tensor_reduce(out_, a, AXX, ALU.max), *tokens)

        def af(out_, a, f, *tokens, bias=0.0, scale=1.0):
            return act.do(lambda e: e.activation(out_, a, f, bias=bias, scale=scale), *tokens)

        def fence():
            now = [e.now() for e in (pe, dve, act, pool) if e.count]
            for e in (pe, dve, act, pool):
                e.wait(now)
            return now

        def col(name, l, i=0, rows=P):
            c = COL_AT[name, l] + i
            return COL[0:rows, c:c + 1]

        slot_free = [None] * NSLOT
        slot_uses = [0] * NSLOT
        nload = [0]

        def load(src, width=1024):
            i = nload[0] % NSLOT
            nload[0] += 1
            slot_uses[i] += 1
            sp.dma(RING[:, i, 0:width], src, slot_sem[i], slot_free[i])
            return i, (slot_sem[i], 16 * slot_uses[i])

        def blocks(name, l, ct, kt_total=8):
            n = (kt_total + 7) // 8
            found = []
            for j in range(n):
                k = min(8, kt_total - 8 * j)
                i, t = load(A[name][l, ct, :, 8 * j * P:(8 * j + k) * P], k * P)
                found.append((i, t, 8 * j, k))
            return found

        def project(name, l, ct, src, cols, kt_total=8, width=P, after=None):
            b = ps()
            n = cols.stop - cols.start
            pe.wait(b.free, after)
            for i, t, k0, k in blocks(name, l, ct, kt_total):
                pe.wait(t)
                for j in range(k):
                    kt = k0 + j
                    tok = (mmt if j == k - 1 else mm)(
                        b.ap[0:width, 0:n], RING[:, i, j * P:j * P + width], src[:, kt, cols],
                        kt == 0, kt == kt_total - 1)
                slot_free[i] = pe.now()
            return b, pe.now()

        def project_tok(name, l, g, tiles, width, per, emit, after=None):
            bs = [ps() for _ in tiles]
            pe.wait([b.free for b in bs], after)
            for q in range(8 // per):
                i, t = load(A[name][l, g * (8 // per) + q, :, 0:per * width], per * width)
                pe.wait(t)
                for b, tile in zip(bs, tiles):
                    for j in range(per):
                        kt = per * q + j
                        (mmt if j == per - 1 else mm)(
                            b.ap[:, 0:width], HT[:, kt, tile * P:tile * P + P],
                            RING[:, i, j * width:(j + 1) * width], kt == 0, kt == 7)
                slot_free[i] = pe.now()
            tok = pe.now()
            for n, b in enumerate(bs):
                b.free = emit(n, b, tok)

        nconst = [0]

        def const(dst, src):
            sp.dma(dst, src, s_const)
            nconst[0] += 16

        const(CM[:, :, :], A["cm"])
        const(COL[:, :], A["cols"])
        const(XT[:, :, 0:256], A["x"])
        const(XT[:, :, 256:512], A["ctx"])
        const(CG[:, :], A["cg"])
        const(ROPE[:, :, :], A["rope1"])
        const(SM[:, 0:16], A["cc"])
        for e in (pe, dve, act, pool):
            e.wait((s_const, nconst[0]))

        late = []

        def reload(dst, src, *tokens):
            late.append((sem(f"s_late{len(late)}"), 16))
            sp.dma(dst, src, late[-1][0], *tokens)
            return late[-1]

        XA, CA = slice(0, 256), slice(256, 512)
        BOTH = slice(0, 512)

        def silu_of(eng_out, in_, *tokens):
            return af(eng_out, in_, ACT.Silu, *tokens)

        SC = SM[:, 16:32].rearrange("p (k n) -> p k n", n=2)
        t_sc = silu_of(SC, SM[:, 0:16].rearrange("p (n k) -> p k n", n=2))

        def over_features(src, nk, mean, n, *tokens):
            b = ps()
            pe.wait(b.free, *tokens)
            for kt in range(nk):
                (mmt if kt == nk - 1 else mm)(b.ap[:, 0:n], mean, src(kt), kt == 0, kt == nk - 1)
            return b, pe.now()

        def rstd_of(b, t, n, i, *tokens):
            r = RS[:, i, 0:n]
            b.free = af(r, b.ap[:, 0:n], ACT.Sqrt, t, dve.now(), *tokens, bias=COL[:, NCOL:NCOL + 1])
            return r, recip(r, r, b.free)

        def center_scale(src, dst, sq, cols, t_in):
            n = cols.stop - cols.start
            b, t = over_features(lambda k: src[:, k, cols], 8, M1024, n, t_in)
            b2 = ps()
            pe.wait(b2.free)
            tx = []
            for h in range(2):
                ks = slice(4 * h, 4 * h + 4)
                t1 = tt(dve, dst[:, ks, cols], src[:, ks, cols], bc(b.ap[:, 0:n], 1, 4), ALU.subtract, t)
                t2 = af(sq[:, ks, 0:n], dst[:, ks, cols], ACT.Square, t1)
                pe.wait(t2)
                for k in range(4 * h, 4 * h + 4):
                    (mmt if k % 4 == 3 else mm)(b2.ap[:, 0:n], M1024, sq[:, k, 0:n], k == 0, k == 7)
            b.free = t1
            r, t3 = rstd_of(b2, pe.now(), n, 0)
            out_t = []
            for h in range(2):
                ks = slice(4 * h, 4 * h + 4)
                out_t.append(tt(dve, dst[:, ks, cols], dst[:, ks, cols], bc(r, 1, 4), ALU.mult, t3))
            return out_t

        def modulate(l, cols, shift, scale, t_in):
            sq = AR[:, 0:4096].rearrange("p (k n) -> p k n", k=8)
            ts_ = center_scale(XT, HT, sq, cols, t_in)
            for k in range(8):
                for s, c in ((0, XA), (1, CA)):
                    if c.start >= cols.start and c.stop <= cols.stop:
                        af(HT[:, k, c], HT[:, k, c], ACT.Identity, ts_[k // 4],
                           bias=MOD[:, l, 8 * shift + k, s:s + 1], scale=MOD[:, l, 8 * scale + k, s:s + 1])
            return act.now()

        def post(cols, g, b, l, t_in):
            sq = AR[:, 0:4096].rearrange("p (k n) -> p k n", k=8)
            ts_ = center_scale(XT, XT, sq, cols, t_in)
            for k in range(8):
                af(XT[:, k, cols], XT[:, k, cols], ACT.Identity, ts_[k // 4],
                   bias=col(b, l, k), scale=col(g, l, k))
            return act.now()

        def residual(l, name, ct, src, cols, kt_total, gate, tmp, after):
            n = cols.stop - cols.start
            b, t = project(name, l, ct, src, cols, kt_total, after=after)
            for s, c in ((0, XA), (1, CA)):
                if c.start < cols.stop:
                    w = slice(c.start - cols.start, c.stop - cols.start)
                    t1 = af(tmp[:, w], b.ap[:, w], ACT.Copy, t, dve.now(),
                            scale=MOD[:, l, 8 * gate + ct, s:s + 1])
            b.free = t1
            return stt(XT[:, ct, cols], XT[:, ct, cols], ALPHA, tmp[:, 0:n], ALU.mult, ALU.add, t1)

        def pipe(stages, n):
            for i in range(n + len(stages) - 1):
                for s, stage in enumerate(stages):
                    if 0 <= i - s < n:
                        stage(i - s)

        def ada(l, lo, hi):
            b = ps()
            pe.wait(b.free, t_sc)
            for ct in range(lo, hi):
                i, t = load(A["w_ada"][l, ct, :, :])
                pe.wait(t)
                for kt in range(8):
                    (mmt if kt == 7 else mm)(b.ap[:, 2 * ct:2 * ct + 2], RING[:, i, kt * P:kt * P + P],
                                             SC[:, kt, :], kt == 0, kt == 7)
                slot_free[i] = pe.now()
            v = b.ap[:, 2 * lo:2 * hi].rearrange("p (c n) -> p c n", n=2)
            c = COL_AT["b_ada", l]
            b.free = tt(dve, MOD[:, l, lo:hi, :], v, bc(COL[:, c + lo:c + hi], 2, 2), ALU.add, pe.now())
            for s in (8, 32):
                if lo <= s < hi:
                    ts(dve, MOD[:, l, s:s + 8, :], MOD[:, l, s:s + 8, :], 1.0, None, ALU.add, None, dve.now())

        def view(a, n, m, src=None):
            return (AR if src is None else src)[:, a:a + n * m].rearrange("p (k n) -> p k n", k=n)

        OG = view(0, 8, 512)
        QG = view(4096, 4, 512)
        KG = view(6144, 4, 512)
        VG = view(8192, 4, 1024)
        LG = view(12288, 4, 512)
        ST = view(14336, 8, 256)
        KGT = view(16384, 2, 512)
        GLRT = AR[:, 17408:17920]
        XE = view(17920, 8, 128)
        QST = view(18944, 2, 256)
        ATB = [view(19456 + 512 * i, 2, 256) for i in range(2)]
        EX = [view(1792 * i, 14, 128, MGF) for i in range(2)]
        KW = view(0, 4, 512, MGF)
        GT = MGF[:, 3584:4096]
        LM = CG[:, 0:896].rearrange("p (k n) -> p k n", k=7)
        DIAG2 = CG[:, 896:1024]
        CF = CG[:, 1024:2816]
        CB = CG[:, 2816:4608]
        INP, INS, EXS, EXP = (CG[:, 4608 + 128 * i:4736 + 128 * i] for i in range(4))

        QT = view(4096, 8, 512)
        KT = view(12288, 2, 512)
        VT = view(13312, 4, 256)
        PT = [view(14336 + 1024 * i, 4, 256) for i in range(3)]
        SQ = [AR[:, 17408 + 512 * i:17920 + 512 * i] for i in range(6)]

        def gla_projections(l, qcols):
            def keep(dst, scale=1.0):
                def f(b, t):
                    b.free = af(dst, b.ap[:, 0:dst.shape[-1]], ACT.Copy, t, scale=scale)
                return f

            for ct in range(4):
                keep(KG[:, ct, :])(*project("w_kg", l, ct, HT, BOTH))
            for ct in range(4):
                keep(QG[:, ct, qcols], SCALE1)(*project("w_qg", l, ct, HT, qcols))
            b = ps()
            pe.wait(b.free)
            i, t = load(A["w_glr"][l], 256)
            pe.wait(t)
            for kt in range(8):
                (mmt if kt == 7 else mm)(b.ap[0:32, :], RING[:, i, kt * 32:kt * 32 + 32], HT[:, kt, :],
                                         kt == 0, kt == 7)
            slot_free[i] = pe.now()
            b.free = af(GLRT[0:32, :], b.ap[0:32, :], ACT.Copy, pe.now())
            pool.do(lambda e: e.memset(GLRT[32:33, :], 1.0))
            for g in range(2):
                def emit(n, b, tok, g=g):
                    return af(VG[:, n, g * 512:g * 512 + 512], b.ap[:, :], ACT.Copy, tok)
                project_tok("w_vg", l, g, range(4), 512, 2, emit)

        def gla_gates(seq):
            for tile in range(2):
                for d in range(2):
                    b = ps()
                    q = 256 * seq + 128 * tile
                    t = mmt(b.ap[:, :], GLRT[0:33, q:q + 128], WA[0:33, d, :], True, True,
                            b.free, act.now(), pool.now(), t_wa[0])
                    t1 = af(GT, b.ap[:, :], ACT.Abs, t, dve.now())
                    t2 = af(GT, GT, ACT.Exp, t1, scale=-1.0)
                    t3 = af(GT, GT, ACT.Ln, t2, bias=1.0)
                    b.free = stt(LG[:, 2 * tile + d, :], b.ap[:, :], 0.0, GT, ALU.min, ALU.subtract, t3)

        def gla_states():
            for tile in range(2):
                b = ps()
                pe.wait(b.free, act.now())
                for h in range(4):
                    transpose(b.ap[:, h * P:h * P + P], KG[:, h, 256 + tile * P:384 + tile * P], P)
                b.free = af(KGT[:, tile, :], b.ap[:, :], ACT.Copy, pe.now())
            for d in range(2):
                for tile in range(2):
                    b = ps()
                    far = tile == (0 if d == 0 else 1)
                    mmt(b.ap[:, :], (EXS, EXP)[d], LG[:, 2 * tile + d, :], True, not far, b.free, dve.now())
                    if far:
                        mmt(b.ap[:, :], ONES, LG[:, 2 * (1 - tile) + d, :], False, True)
                    w = KW[:, 2 * d + tile, :]
                    b.free = af(w, b.ap[:, :], ACT.Exp, pe.now(), scale=1.0 / 16)
                    tt(dve, w, w, KGT[:, tile, :], ALU.mult, act.now())
            for h in range(4):
                b = ps()
                pe.wait(b.free, dve.now())
                for d in range(2):
                    for tile in range(2):
                        mmt(b.ap[:, d * 256:d * 256 + 256], KW[:, 2 * d + tile, h * P:h * P + P],
                            VG[:, 2 + tile, h * 256:h * 256 + 256], tile == 0, tile == 1)
                b.free = af(ST[:, 2 * h:2 * h + 2, :], b.ap[:, :].rearrange("p (d n) -> p d n", d=2),
                            ACT.Copy, pe.now())

        def gla_outputs(l, seq, states):
            c0 = 256 * seq
            lt = [dve.now()]
            pend = []

            def weights(h):
                at = ATB[h % 2]
                tx = []
                for tile in range(2):
                    b = ps()
                    pe.wait(b.free, lt)
                    lf = LG[:, 2 * tile, h * P:h * P + P]
                    lb = LG[:, 2 * tile + 1, h * P:h * P + P]
                    for n, (g, m) in enumerate(((lf, INP), (lb, INS), (lf, EXS), (lb, EXP))):
                        mmt(b.ap[:, n * P:n * P + P], g, m, True, True)
                    b.free = af(XE[:, 4 * tile:4 * tile + 4, :], b.ap[:, :].rearrange("p (k n) -> p k n", k=4),
                                ACT.Exp, pe.now(), xe_free[0], scale=1.0 / 16)
                tx = act.now()
                t0 = copy(SM[:, 32:33], XE[:, 0, 127:128], tx)
                t0 = copy(SM[:, 33:34], XE[:, 5, 0:1], tx)
                for tile in range(2):
                    q = QG[:, h, c0 + tile * P:c0 + tile * P + P]
                    k = KG[:, h, c0 + tile * P:c0 + tile * P + P]
                    tt(dve, XE[:, 4 * tile:4 * tile + 2, :], XE[:, 4 * tile:4 * tile + 2, :], bc(q, 1, 2),
                       ALU.mult, t0)
                    tt(dve, XE[:, 4 * tile + 2:4 * tile + 4, :], XE[:, 4 * tile + 2:4 * tile + 4, :],
                       bc(k, 1, 2), ALU.mult, t0)
                t_xe = dve.now()
                if states:
                    copy(QST[:, 0, 0:128], XE[:, 0, :], t_xe, qst_free[0])
                    copy(QST[:, 1, 128:256], XE[:, 5, :])
                    ts(dve, QST[:, 0, 128:256], XE[:, 4, :], SM[:, 32:33], None, ALU.mult, None)
                    ts(dve, QST[:, 1, 0:128], XE[:, 1, :], SM[:, 33:34], None, ALU.mult, None)
                b = ps()
                mm(b.ap[:, 0:128], XE[:, 2, :], XE[:, 4, :], True, True, b.free, dve.now())
                xe_free[0] = mmt(b.ap[:, 128:256], XE[:, 7, :], XE[:, 1, :], True, True)
                copy(at[:, 0, 128:256], b.ap[:, 0:128], pe.now(), at_free[h % 2])
                b.free = copy(at[:, 1, 0:128], b.ap[:, 128:256])
                for tile in range(2):
                    q = QG[:, h, c0 + tile * P:c0 + tile * P + P]
                    k = KG[:, h, c0 + tile * P:c0 + tile * P + P]
                    ex = EX[tile]
                    lf = LG[:, 2 * tile, h * P:h * P + P]
                    lb = LG[:, 2 * tile + 1, h * P:h * P + P]
                    for c in range(4):
                        n = 448
                        b = ps()
                        mm(b.ap[:, 0:n], lf, CF[:, c * n:c * n + n], True, False, b.free)
                        mmt(b.ap[:, 0:n], lb, CB[:, c * n:c * n + n], False, True)
                        flat = MGF[:, 1792 * tile + c * n:1792 * tile + c * n + n]
                        b.free = af(flat, b.ap[:, 0:n], ACT.Exp, pe.now(), ex_free[tile], scale=1.0 / 16)
                    t = act.now()
                    tt(dve, ex[:, 0:7, :], ex[:, 0:7, :], bc(q, 1, 7), ALU.mult, t)
                    tt(dve, ex[:, 7:14, :], ex[:, 7:14, :], bc(k, 1, 7), ALU.mult, t)

            def grams(h):
                at = ATB[h % 2]
                for tile in range(2):
                    q = QG[:, h, c0 + tile * P:c0 + tile * P + P]
                    k = KG[:, h, c0 + tile * P:c0 + tile * P + P]
                    ex = EX[tile]
                    b1, b2 = ps(), ps()
                    pe.wait(b1.free, b2.free, gram_in[tile])
                    for n in range(4):
                        (mmt if n == 3 else mm)(b1.ap[:, n * P:n * P + P], ex[:, 7 + n, :], ex[:, n, :], True, True)
                    for n in range(4, 7):
                        mm(b2.ap[:, (n - 4) * P:(n - 3) * P], ex[:, 7 + n, :], ex[:, n, :], True, True)
                    t = mmt(b2.ap[:, 384:512], k, q, True, True)
                    ex_free[tile] = t
                    dst = at[:, tile, tile * P:tile * P + P]
                    tt(dve, dst, b2.ap[:, 384:512], DIAG2, ALU.mult, t)
                    for n in range(7):
                        src = (b1 if n < 4 else b2).ap[:, (n % 4) * P:(n % 4) * P + P]
                        mk = LM[:, n, :].bitcast(I32)
                        dve.do(lambda e, src=src, mk=mk, dst=dst: e.copy_predicated(dst, mk, src), dve.now())
                    b1.free = b2.free = dve.now()

            def values(h):
                at = ATB[h % 2]
                b = ps()
                pe.wait(b.free, dve.now())
                for et in range(2):
                    o = b.ap[:, et * 256:et * 256 + 256]
                    e0 = h * 256 + et * P
                    mm(o, VG[:, 2 * seq, e0:e0 + P], at[:, 0, :], True, False)
                    mmt(o, VG[:, 2 * seq + 1, e0:e0 + P], at[:, 1, :], False, not states)
                    if states:
                        mm(o, ST[:, 2 * h, et * P:et * P + P], QST[:, 0, :], False, False)
                        mmt(o, ST[:, 2 * h + 1, et * P:et * P + P], QST[:, 1, :], False, True)
                at_free[h % 2] = qst_free[0] = pe.now()
                o = OG[:, 2 * h:2 * h + 2, c0:c0 + 256]
                t = af(o, b.ap[:, :].rearrange("p (k n) -> p k n", k=2), ACT.Copy, pe.now())
                b.free = t
                t = af(GT.rearrange("p (k n) -> p k n", k=2), o, ACT.Square, t, gt_free[0])
                b2, t = over_features(lambda k: GT[:, k * 256:k * 256 + 256], 2, M256, 256, t)
                gt_free[0] = t
                r, t = rstd_of(b2, t, 256, h % 2)
                for et in range(2):
                    o = OG[:, 2 * h + et, c0:c0 + 256]
                    stt(o, o, col("gla_norm", l, et), r, ALU.mult, ALU.mult, t)

            xe_free, qst_free, at_free, ex_free, gt_free = [None], [None], [None, None], [None, None], [None]
            gram_in = [None, None]
            for h in range(4):
                weights(h)
                gram_in[0] = gram_in[1] = dve.now()
                grams(h)
                values(h)

        def att_projections(l, qcols):
            items = [("w_k", ct, KT[:, ct, :], BOTH, "k_norm") for ct in range(2)]
            items += [("w_q", ct, QT[:, ct, qcols], qcols, "q_norm") for ct in range(8)]
            done = {}

            def raw(i):
                name, ct, dst, cols, _ = items[i]
                n = cols.stop
                b, t = project(name, l, ct, HT, cols)
                t = af(dst, b.ap[:, 0:n], ACT.Copy, t)
                b.free = t
                done["raw", i] = af(SQ[i % 3][:, 0:n], dst, ACT.Square, t, done.get(("norm", i - 3)))

            def norm(i):
                _, _, dst, cols, g = items[i]
                n = cols.stop
                b, t = over_features(lambda k: SQ[i % 3][:, 0:n], 1, M128, n, done["raw", i])
                done["norm", i] = t
                r, t = rstd_of(b, t, n, i % 3)
                done["scaled", i] = stt(dst, dst, col(g, l), r, ALU.mult, ALU.mult, t)

            def rotate(i):
                dst = items[i][2][:, 0:256]
                b = ps()
                t = mmt(b.ap[:, 0:256], R1, dst, True, True, b.free, done["scaled", i])
                tmp = SQ[3 + i % 3][:, 0:256]
                b.free = tt(dve, tmp, b.ap[:, 0:256], ROPE[:, 1, :], ALU.mult, t, dve.now())
                t = tt(dve, dst, dst, ROPE[:, 0, :], ALU.mult)
                tt(dve, dst, dst, tmp, ALU.add, t)

            pipe([raw, norm, rotate], len(items))

            def emit(n, b, tok):
                return af(VT[:, n, :], b.ap[:, 0:256], ACT.Copy, tok)
            project_tok("w_v", l, 0, range(4), 256, 4, emit)

        def attend(q0, k0, nk):
            pe.wait(dve.now(), act.now())
            for h in range(8):
                for qt in range(2):
                    b = ps()
                    t = mmt(b.ap[:, 0:nk * P], QT[:, h, q0 + qt * P:q0 + qt * P + P],
                            KT[:, h // 4, k0:k0 + nk * P], True, True, b.free)
                    b.free = rmax(SM[:, 64 + 8 * qt + h:65 + 8 * qt + h], b.ap[:, 0:nk * P], t)
            for qt in range(2):
                b = ps()
                t = transpose(b.ap[0:8, 0:P], SM[:, 64 + 8 * qt:72 + 8 * qt], P, b.free, dve.now())
                b.free = af(NM[0:8, qt * P:qt * P + P], b.ap[0:8, 0:P], ACT.Copy, t, scale=-1.0)
            t_nm = act.now()
            done = {}

            def weigh(h):
                pt = PT[h % 3]
                for kp in range(nk // 2):
                    b = ps()
                    pe.wait(b.free, t_nm)
                    for j in range(2):
                        kc = k0 + (2 * kp + j) * P
                        o = b.ap[:, j * 256:j * 256 + 256]
                        mm(o, KT[:, h // 4, kc:kc + P], QT[:, h, q0:q0 + 256], True, False)
                        mmt(o, IDENT[0:8, h:h + 1].to_broadcast([8, P]), NM[0:8, :], False, True)
                    b.free = af(pt[:, 2 * kp:2 * kp + 2, :], b.ap[:, :].rearrange("p (k n) -> p k n", k=2),
                                ACT.Exp, pe.now(), done.get(("values", h - 3)), scale=SCALE1)
                done["weigh", h] = act.now()

            def values(h):
                pt = PT[h % 3]
                b = ps()
                pe.wait(b.free, done["weigh", h])
                for j in range(nk):
                    mm(b.ap[:, 0:256], VT[:, k0 // P + j, (h // 4) * P:(h // 4) * P + P], pt[:, j, :],
                       j == 0, j == nk - 1)
                for j in range(nk):
                    mm(b.ap[:, 256:512], ONES, pt[:, j, :], j == 0, j == nk - 1) if j < nk - 1 else \
                        mmt(b.ap[:, 256:512], ONES, pt[:, j, :], j == 0, True)
                t = done["values", h] = pe.now()
                r = RS[:, h % 3, 0:256]
                t = recip(r, b.ap[:, 256:512], t)
                b.free = tt(dve, QT[:, h, q0:q0 + 256], b.ap[:, 0:256], r, ALU.mult, t)

            pipe([weigh, values], 8)

        def merge(l, cols, branch, name, src):
            n = cols.stop
            tmp = [AR[:, 17408 + 512 * i:17408 + 512 * i + n] for i in range(2)]
            t_in = [dve.now(), act.now()]
            used = [dve.now()] * 2
            for ct in range(8):
                bg, tg = project("w_gates", l, 8 * branch + ct, HT, cols)
                by, ty = project(name, l, ct, src, cols, after=t_in)
                tp = tmp[ct % 2]
                bg.free = af(tp, bg.ap[:, 0:n], ACT.Sigmoid, tg, used[ct % 2])
                m = MG[:, ct, cols]
                if branch == 0:
                    by.free = used[ct % 2] = tt(dve, m, tp, by.ap[:, 0:n], ALU.mult, bg.free, ty)
                else:
                    by.free = tt(dve, tp, tp, by.ap[:, 0:n], ALU.mult, bg.free, ty)
                    used[ct % 2] = tt(dve, m, m, tp, ALU.add, by.free)

        def gla_gated(l, cols):
            n = cols.stop
            tmp = [AR[:, 17408 + 512 * i:17408 + 512 * i + n] for i in range(2)]
            used = [dve.now()] * 2
            for ct in range(8):
                b, t = project("w_r", l, ct, HT, cols)
                b.free = af(tmp[ct % 2], b.ap[:, 0:n], ACT.Silu, t, used[ct % 2])
                used[ct % 2] = tt(dve, OG[:, ct, cols], OG[:, ct, cols], tmp[ct % 2], ALU.mult, b.free)

        YP = AR[:, 4096:8672].rearrange("p (k s n) -> p k s n", k=8, s=2)
        ZC = view(8704, 8, 512)
        CSQ = view(12800, 8, 512)

        def conv(l, cols):
            n = cols.stop
            ns = n // 256
            tmp = [AR[:, 17408 + 512 * i:17408 + 512 * i + n] for i in range(2)]
            used = [dve.now()] * 2
            t0 = pool.do(lambda e: e.memset(AR[:, 4096:8672], 0.0))
            t_y = []
            for ct in range(8):
                ba, ta = project("w_glu", l, ct, HT, cols)
                bg, tg = project("w_glu", l, 8 + ct, HT, cols)
                tp = tmp[ct % 2]
                bg.free = af(tp, bg.ap[:, 0:n], ACT.Sigmoid, tg, used[ct % 2])
                v = lambda a: a.rearrange("p (s n) -> p s n", s=ns)
                ba.free = used[ct % 2] = tt(dve, YP[:, ct, 0:ns, 15:271], v(ba.ap[:, 0:n]), v(tp), ALU.mult,
                                            t0, bg.free, ta)
                t_y.append(dve.now())
            last = {}
            for c0 in range(0, 8, 4):
                for tap in range(31):
                    for ct in range(c0, c0 + 4):
                        z = ZC[:, ct, cols].rearrange("p (s n) -> p s n", s=ns)
                        y = YP[:, ct, 0:ns, tap:tap + 256]
                        w = CVW[:, ct * 31 + tap:ct * 31 + tap + 1]
                        if tap == 0:
                            last[ct] = ts(dve, z, y, w, col("conv_b_dw", l, ct), ALU.mult, ALU.add, t_y[ct], t_cv[0])
                        else:
                            last[ct] = stt(z, y, w, z, ALU.mult, ALU.add, last[ct])
            t = center_scale(ZC, ZC, CSQ, cols, dve.now())
            for k in range(8):
                af(ZC[:, k, cols], ZC[:, k, cols], ACT.Silu, t[k // 4],
                   bias=col("conv_ln_b", l, k), scale=col("conv_ln_g", l, k))

        FF = view(0, NFF, 512)

        def ffn(l, cols):
            n = cols.stop
            tmp = [AR[:, 12288 + 512 * i:12288 + 512 * i + n] for i in range(3)]
            used = [dve.now()] * 3
            for j in range(NFF):
                bg, tg = project("w_ff_gate", l, j, HT, cols)
                bu, tu = project("w_ff_up", l, j, HT, cols)
                bg.free = af(tmp[j % 3], bg.ap[:, 0:n], ACT.Silu, tg, used[j % 3])
                bu.free = used[j % 3] = tt(dve, FF[:, j, cols], tmp[j % 3], bu.ap[:, 0:n], ALU.mult, bg.free, tu)
            for ct in range(8):
                residual(l, "w_ff_down", ct, FF, cols, NFF, 5, AR[:, 16384 + 512 * (ct % 2):16896 + 512 * (ct % 2)],
                         dve.now() if ct == 0 else None)

        t_wa, t_cv = [None], [None]
        ada(0, 0, 16)
        for l in range(DEPTH):
            last = l == DEPTH - 1
            cols = XA if last else BOTH
            now = fence()
            t_wa[0] = reload(WA[:, :, :], A["wa"][l], now)
            t_cv[0] = reload(CVW[:, :], A["cvw"][l], now)
            modulate(l, BOTH, 0, 1, now)
            fence()
            gla_projections(l, cols)
            ada(l, 16, 48)
            fence()
            gla_gates(1)
            fence()
            gla_states()
            fence()
            if not last:
                gla_outputs(l, 1, False)
                fence()
            gla_gates(0)
            fence()
            gla_outputs(l, 0, True)
            fence()
            att_projections(l, cols)
            fence()
            if not last:
                attend(256, 256, 2)
                fence()
            attend(0, 0, 4)
            fence()
            merge(l, cols, 0, "w_att_o", QT)
            gla_gated(l, cols)
            merge(l, cols, 1, "w_gla_o", OG)
            fence()
            conv(l, cols)
            fence()
            merge(l, cols, 2, "w_conv_o", ZC)
            fence()
            for ct in range(8):
                residual(l, "w_out", ct, MG, cols, 8, 2, AR[:, 16384 + 512 * (ct % 2):16896 + 512 * (ct % 2)], None)
            fence()
            post(cols, "ln1_g", "ln1_b", l, None)
            fence()
            modulate(l, cols, 3, 4, None)
            fence()
            ffn(l, cols)
            if not last:
                ada(l + 1, 0, 16)
            fence()
            post(cols, "ln2_g", "ln2_b", l, None)

        X = slice(0, 256)
        QK = view(0, 16, 256)
        VX = AR[:, 4096:7168].rearrange("p (t h n) -> p t h n", t=2, h=12)
        TK = AR[:, 7168:8192].rearrange("p (a g n) -> p a g n", a=2, g=2)
        XW = AR[:, 8192:9152].rearrange("p (a k g n) -> p a k g n", a=2, k=16, g=2)
        HID = AR[:, 9152:9272].rearrange("p (a j n) -> p a j n", a=2, j=2)
        KCMP = AR[:, 9280:9296]
        VC = AR[0:15, 9296:9552].rearrange("p (g n) -> p g n", g=2)
        W2 = AR[:, 9600:9984].rearrange("p (j n) -> p j n", j=2)
        MIX = view(10240, 8, 256)
        PB = [AR[:, 12288 + 384 * i:12672 + 384 * i] for i in range(4)]
        GB = view(13824, 12, 256)
        RT = [AR[:, 16896 + 256 * i:17152 + 256 * i] for i in range(4)]
        TB = [AR[:, 17920 + 512 * i:18432 + 512 * i] for i in range(4)]
        G24 = AR[0:24, 19968:20224]
        CT8 = AR[0:4, 20224:20480]
        CNT = CG[:, 0:384]
        C01 = CG[0:15, 384:640]
        SELG = CG[0:24, 640:2176]
        TRI = CG[:, 2176:2304]
        INVF = CG[:, 2304:2305]
        POSE = CG[:, 2320:2384].rearrange("p (l a k) -> p l a k", l=2, a=2)
        BNG = CG[0:24, 2384:2386]
        BFG = CG[:, 2400:2408].rearrange("p (l h) -> p l h", l=2)
        CBF = CG[:, 2560:3648].bitcast(BF16)
        IDB, MQ, MK = CBF[:, 0:128], CBF[:, 128:512], CBF[:, 512:896]
        DQ, DK = CBF[:, 896:1280], CBF[:, 1280:1664]
        CQM, CKM = CBF[:, 1664:1792], CBF[0:15, 1920:2176]
        LFT = SM[:, 160:192].rearrange("p (a t h) -> p a t h", a=4, t=2)
        NC = SM[:, 192:200].rearrange("p (t h) -> p t h", t=2)
        MX = SM[:, 64:128].rearrange("p (q u) -> p q u", q=2)


        def tables(now):
            posi = TB[0][:, 0:256].bitcast(I32)
            t = reload(posi, A["pos"].partition_broadcast(P), now)
            ang, k, r, pf = TB[1][:, 0:256], TB[2][:, 0:256], TB[3][:, 0:256], TB[0][:, 256:512]
            t = copy(pf, posi, t)
            t = ts(dve, ang, pf, INVF, None, ALU.mult, None, t)
            big = 1.5 * 2.0 ** 23
            c1 = 6.28125
            c2 = float(np.round(1.9353071795864769e-3 * 2.0 ** 20) / 2.0 ** 20)
            c3 = 1.9353071795864769e-3 - c2
            for n, shift in ((1, 0.0), (0, 0.25)):
                t = ts(dve, k, ang, 1.0 / (2.0 * np.pi), shift, ALU.mult, ALU.add, dve.now(), act.now())
                t = ts(dve, k, k, big, None, ALU.add, None, t)
                t = ts(dve, k, k, -big, None, ALU.add, None, t)
                t = stt(r, k, -c1, ang, ALU.mult, ALU.add, t)
                t = stt(r, k, -c2, r, ALU.mult, ALU.add, t)
                t = stt(r, k, -c3, r, ALU.mult, ALU.add, t)
                t = ts(dve, r, r, float(2.0 * np.pi * shift), 3.1415925, ALU.add, ALU.min, t)
                t = ts(dve, r, r, -3.1415925, None, ALU.max, None, t)
                af(ROPE[:, n, :], r, ACT.Sin, t)

        def rms(l, name, src_of, dst_of):
            sq = view(10240, 8, 256)
            for h in range(2):
                ks = slice(4 * h, 4 * h + 4)
                t = af(sq[:, ks, :], src_of(ks), ACT.Square, dve.now(), act.now())
            b, t = over_features(lambda k: sq[:, k, :], 8, M1024, 256, t)
            r, t = rstd_of(b, t, 256, 0)
            for k in range(8):
                stt(dst_of(k), src_of(slice(k, k + 1)).rearrange("p a n -> p (a n)"), col(name, l, k), r,
                    ALU.mult, ALU.mult, t)

        def projections2(l):
            rope = {4, 5, 6, 7, 8, 9, 10, 12, 13, 14, 15}
            done = {}

            def raw(i):
                b, t = project("w_in2", l, i, HT, X)
                b.free = done[i] = af(QK[:, i, :], b.ap[:, 0:256], ACT.Copy, t)

            def rotate(i):
                if i not in rope:
                    return
                dst = QK[:, i, :]
                b = ps()
                t = mmt(b.ap[:, 0:256], R2, dst, True, True, b.free, done[i])
                tmp = TB[i % 2][:, 0:256]
                b.free = tt(dve, tmp, b.ap[:, 0:256], ROPE[:, 1, :], ALU.mult, t, dve.now())
                t = tt(dve, dst, dst, ROPE[:, 0, :], ALU.mult)
                tt(dve, dst, dst, tmp, ALU.add, t)

            t1 = pool.do(lambda e: e.memset(AR[:, 4096:7168], 1.0))
            t1 = pool.do(lambda e: e.memset(VC, 1.0))
            pipe([raw, rotate], 16)
            b = ps()
            pe.wait(b.free)
            i, t = load(A["w_ng"][l], 192)
            pe.wait(t)
            for kt in range(8):
                (mmt if kt == 7 else mm)(b.ap[0:24, 0:256], RING[:, i, kt * 24:kt * 24 + 24], HT[:, kt, X],
                                         kt == 0, kt == 7)
            slot_free[i] = pe.now()
            b.free = af(G24, b.ap[0:24, 0:256], ACT.Sigmoid, pe.now(), bias=BNG[:, l:l + 1])

            def emit(n, b, tok, h0):
                nh = 8 if h0 == 0 else 4
                v = b.ap[:, 0:64 * nh].rearrange("p (h two d) -> p h two d", two=2, d=64)
                o = VX[:, n, h0:h0 + nh, :].rearrange("p (h two) d -> p h two d", two=2)
                act.wait(t1)
                t = af(o[:, :, 0, 0:64], v[:, :, 0, :], ACT.Copy, tok)
                t = af(o[:, :, 1, 64:128], v[:, :, 1, :], ACT.Copy, tok)
                if h0 == 8:
                    t = tt(dve, LFT[:, 0, n, :], b.ap[:, 256:260], BFG[:, l, :], ALU.add, t)
                return t
            project_tok("w_t0", l, 0, range(2), 512, 2, lambda n, b, tok: emit(n, b, tok, 0))
            project_tok("w_t1", l, 0, range(2), 260, 2, lambda n, b, tok: emit(n, b, tok, 8))
            t = af(LFT[:, 1], LFT[:, 0], ACT.Abs, dve.now())
            t = af(LFT[:, 1], LFT[:, 1], ACT.Exp, t, scale=-1.0)
            t = af(LFT[:, 1], LFT[:, 1], ACT.Ln, t, bias=1.0)
            t = stt(LFT[:, 2], LFT[:, 0], 0.0, LFT[:, 1], ALU.min, ALU.subtract, t)
            lf = LFT[:, 2]
            b = ps()
            mm(b.ap[:, 0:4], TRI, lf[:, 0, :], True, True, t, b.free)
            mm(b.ap[:, 4:8], ONES, lf[:, 0, :], True, False)
            mmt(b.ap[:, 4:8], TRI, lf[:, 1, :], False, True)
            b.free = af(NC.rearrange("p t h -> p (t h)"), b.ap[:, 0:8], ACT.Copy, pe.now(), scale=-1.0)
            b = ps()
            mm(b.ap[0:4, 0:128], lf[:, 0, :], TRI, True, True, b.free)
            mm(b.ap[0:4, 128:256], lf[:, 0, :], ONES, True, False)
            mmt(b.ap[0:4, 128:256], lf[:, 1, :], TRI, False, True)
            b.free = af(CT8, b.ap[0:4, 0:256], ACT.Copy, pe.now(), scale=-8.0)

        def compress(l, t_w2):
            dve.wait(act.now())
            for a, tile in ((0, 8), (1, 11)):
                for g in range(2):
                    src = QK[64 * g:64 * g + 64, tile, :]
                    copy(TK[0:64, a, g, :], src)
                    copy(TK[64:128, a, g, 0:255], src[:, 1:256])
            t = dve.now()
            for a in range(2):
                for g in range(2):
                    for h in range(2):
                        v = TK[:, a, g, 16 * h:16 * h + 240].rearrange("p (n k t) -> p k n t", k=8, t=2)[:, :, :, 0]
                        tt(dve, XW[:, a, 8 * h:8 * h + 8, g, :], v, bc(POSE[:, l, a, 8 * h:8 * h + 8], 2, 15),
                           ALU.add, t)
            t = dve.now()
            for a in range(2):
                b = [ps(), ps()]
                pe.wait(b[0].free, b[1].free, t)
                for c in range(4):
                    i, tw = load(A["w_cmp"][l, 4 * a + c], 1024)
                    pe.wait(tw)
                    for k in range(4):
                        for j in range(2):
                            (mmt if k == 3 else mm)(
                                b[j].ap[:, 0:30], RING[:, i, 256 * k + 128 * j:256 * k + 128 * j + 128],
                                XW[:, a, 4 * c + k, :, :], c == 0 and k == 0, c == 3 and k == 3)
                    slot_free[i] = pe.now()
                for j in range(2):
                    b[j].free = af(HID[:, a, j, :], b[j].ap[:, 0:30], ACT.Gelu_apprx_tanh, pe.now())
            b = ps()
            pe.wait(b.free, act.now(), t_w2)
            for j in range(2):
                (mmt if j else mm)(b.ap[:, 0:30], W2[:, j, 0:128], HID[:, 0, j, :], j == 0, j == 1)
            af(KCMP[0:64, 0:15], b.ap[0:64, 0:15], ACT.Copy, pe.now())
            b.free = af(KCMP[64:128, 0:15], b.ap[64:128, 15:30], ACT.Copy)
            b = ps()
            pe.wait(b.free)
            for g in range(2):
                for j in range(2):
                    mmt(b.ap[0:15, 64 * g:64 * g + 64], HID[:, 1, j, 15 * g:15 * g + 15], W2[:, j, 128:192],
                        j == 0, j == 1)
            act.wait(pool.now())
            af(VC[:, 0, 0:64], b.ap[0:15, 0:64], ACT.Copy, pe.now())
            b.free = af(VC[:, 1, 64:128], b.ap[0:15, 64:128], ACT.Copy)
            for i in range(12):
                if i % 2 == 0:
                    b = ps()
                    pe.wait(b.free)
                mmt(b.ap[:, 256 * (i % 2):256 * (i % 2) + 256], SELG[:, 128 * i:128 * i + 128], G24, True, True)
                if i % 2:
                    b.free = af(GB[:, i - 1:i + 1, :], b.ap[:, :].rearrange("p (k n) -> p k n", k=2),
                                ACT.Copy, pe.now())

        UNITS = [("fox", h % 2, h // 2, 2 + h // 2, h, h // 2, None) for h in range(4)]
        UNITS += [("sel", g, 4 + i, 9, 4 + g, 2 + i, 1) for i in range(4) for g in range(2)]
        UNITS += [("win", g, 4 + i, 10, 6 + g, 2 + i, 2) for i in range(4) for g in range(2)]
        UNITS += [("dil", h % 2, 12 + h // 2, 14 + h // 2, 8 + h, 6 + h // 2, None) for h in range(4)]
        UNITS += [("cmp", g, 4 + i, None, g, 2 + i, 0) for i in range(4) for g in range(2)]

        def attention2():
            def row(u, n):
                return IDENT[0:32, u:u + 1].to_broadcast([32, n])

            for u, (kind, par, q, k, v, o, br) in enumerate(UNITS[:24]):
                r = slice(64 * par, 64 * par + 64)
                b = ps()
                mm(b.ap[:, 0:384], IDB, DQ if kind == "dil" else MQ, True, False, b.free)
                if kind == "fox":
                    mm(b.ap[:, 0:128], IDENT[0:4, u:u + 1].to_broadcast([4, P]), CT8[:, 0:128], False, False)
                    mm(b.ap[:, 128:384], IDENT[0:4, u:u + 1].to_broadcast([4, P]), CT8[:, 0:256], False, False)
                mm(b.ap[:, 0:128], QK[r, q, 0:128], QK[r, k, 0:128], False, False)
                t = mmt(b.ap[:, 128:384], QK[r, q, 128:256], QK[r, k, 0:256], False, True)
                for qt, w in ((0, slice(0, 128)), (1, slice(128, 384))):
                    b.free = rmax(MX[:, qt, u:u + 1], b.ap[:, w], t)
            for par in range(2):
                r = slice(64 * par, 64 * par + 64)
                b = ps()
                mm(b.ap[:, 0:128], IDB, CQM, True, False, b.free)
                for i in range(4):
                    for qt in range(2):
                        c = 32 * i + 16 * qt
                        mmt(b.ap[:, c:c + 15], QK[r, 4 + i, 128 * qt:128 * qt + 128], KCMP[r, 0:15], False,
                            i == 3 and qt == 1)
                v = b.ap[:, 0:128].rearrange("p (u q n) -> p u q n", u=4, q=2)
                m = MX[:, :, 24:32].rearrange("p q (u two) -> p q u two", two=2)
                for qt in range(2):
                    b.free = rmax(m[:, qt, :, par], v[:, :, qt, 0:15], pe.now())
            for qt in range(2):
                b = ps()
                t = transpose(b.ap[0:32, 0:P], MX[:, qt, :], P, b.free, dve.now())
                b.free = af(NM[:, qt * P:qt * P + P], b.ap[0:32, 0:P], ACT.Copy, t, scale=-1.0)
            t_nm = act.now()
            done = {}

            def weigh(u):
                kind, par, q, k, v, o, br = UNITS[u]
                r = slice(64 * par, 64 * par + 64)
                pt = PB[u % 4]
                b = ps()
                old = done.get(("values", u - 4))
                if kind == "cmp":
                    mm(b.ap[0:15, 0:256], KCMP[r, 0:15], QK[r, q, 0:256], True, False, b.free, t_nm)
                    mm(b.ap[0:15, 0:256], IDB[0:15, 0:15], CKM, False, False)
                    t = mmt(b.ap[0:15, 0:256], row(u, 15), NM[:, 0:256], False, True)
                    b.free = af(pt[0:15, 0:256], b.ap[0:15, 0:256], ACT.Exp, t, old, scale=SCALE2)
                    done["weigh", u] = tt(dve, pt[0:15, 0:256], pt[0:15, 0:256], C01, ALU.mult, b.free)
                    return
                mm(b.ap[:, 0:384], IDB, DK if kind == "dil" else MK, True, False, b.free, t_nm)
                mm(b.ap[:, 0:256], QK[r, k, 0:128], QK[r, q, 0:256], False, False)
                mm(b.ap[:, 256:384], QK[r, k, 128:256], QK[r, q, 128:256], False, False)
                mm(b.ap[:, 0:256], row(u, P), NM[:, 0:256], False, False)
                if kind == "fox":
                    mm(b.ap[:, 0:256], CT8[:, 0:128], IDENT[0:4, u:u + 1].to_broadcast([4, 256]), False, False)
                    mm(b.ap[:, 256:384], CT8[:, 128:256], IDENT[0:4, u:u + 1].to_broadcast([4, 128]), False, False)
                t = mmt(b.ap[:, 256:384], row(u, P), NM[:, 128:256], False, True)
                b.free = t = af(pt, b.ap[:, 0:384], ACT.Exp, t, old, scale=SCALE2)
                if kind == "dil":
                    t = tt(dve, pt, pt, CNT, ALU.mult, t)
                done["weigh", u] = t

            def values(u):
                kind, par, q, k, v, o, br = UNITS[u]
                own = slice(64 * par, 64 * par + 64)
                den = slice(64 - 64 * par, 128 - 64 * par)
                pt = PB[u % 4]
                b = ps()
                pe.wait(b.free, done["weigh", u])
                if kind == "cmp":
                    mmt(b.ap[:, 0:256], VC[:, v, :], pt[0:15, 0:256], True, True)
                else:
                    mm(b.ap[:, 0:256], VX[:, 0, v, :], pt[:, 0:256], True, False)
                    mmt(b.ap[:, 128:256], VX[:, 1, v, :], pt[:, 256:384], False, True)
                t = done["values", u] = pe.now()
                rt = RT[u % 4][own, :]
                if kind == "cmp":
                    t = ts(dve, rt, b.ap[den, 0:256], 1e-30, None, ALU.max, None, t)
                    t = recip(rt, rt, t)
                else:
                    t = recip(rt, b.ap[den, 0:256], t)
                dst = MIX[own, o, :]
                if br is not None:
                    t = tt(dve, rt, rt, GB[own, 3 * (o - 2) + br, :], ALU.mult, t)
                if br in (None, 1):
                    b.free = tt(dve, dst, b.ap[own, 0:256], rt, ALU.mult, t)
                else:
                    b.free = t = tt(dve, rt, b.ap[own, 0:256], rt, ALU.mult, t)
                    tt(dve, dst, dst, rt, ALU.add, t)

            pipe([weigh, values], 32)

        def mix_out(l, name, src, kt_total, norm):
            f = view(12288, 8, 256)
            t_in = dve.now()
            for ct in range(8):
                b, t = project(name, l, ct, src, X, kt_total, after=t_in)
                b.free = af(f[:, ct, :], b.ap[:, 0:256], ACT.Copy, t)
            fence()
            rms(l, norm, lambda ks: f[:, ks, :], lambda k: f[:, k, :])
            tt(dve, XT[:, :, X], XT[:, :, X], f, ALU.add, dve.now())

        def ffn2(l):
            ffv = view(0, NFF, 256)
            ts_ = {}

            def one(j):
                b, t = project("w_up", l, j, HT, X)
                tp = TB[(j // NFF + 2 * (j % NFF)) % 4][:, 0:256]
                w = [CVW[:, 44 * n + j:44 * n + j + 1] for n in range(3)]
                t = af(tp, b.ap[:, 0:256], ACT.Identity, t, ts_.get((j % NFF) - 2), t_cv[0],
                       bias=col("conv_b_2", l, j), scale=w[2])
                t = stt(tp[:, 1:256], b.ap[:, 0:255], w[1], tp[:, 1:256], ALU.mult, ALU.add, t)
                b.free = stt(tp[:, 2:256], b.ap[:, 0:254], w[0], tp[:, 2:256], ALU.mult, ALU.add, t)
                return tp, b.free

            for j in range(NFF):
                ta, t1 = one(j)
                tb, t2 = one(j + NFF)
                t1 = af(ta, ta, ACT.Silu, t1)
                ts_[j] = tt(dve, ffv[:, j, :], ta, tb, ALU.mult, t1, t2)
            mix_out(l, "w_down", ffv, NFF, "ffn_post_norm_2")

        now = fence()
        t_c = reload(CG[:, 0:3648], A["cg2"], now)
        for e in (pe, dve, act, pool):
            e.wait(t_c)
        tables(now)
        fence()
        for l in range(DEPTH):
            now = fence()
            t_cv[0] = reload(CVW[:, 0:132], A["cvw2"][l], now)
            t_w2 = reload(AR[:, 9600:9984], A["w2"][l], now)
            rms(l, "attn_pre_norm_2", lambda ks: XT[:, ks, X], lambda k: HT[:, k, X])
            fence()
            projections2(l)
            fence()
            compress(l, t_w2)
            fence()
            attention2()
            fence()
            mix_out(l, "w_mix", MIX, 8, "attn_post_norm_2")
            fence()
            rms(l, "ffn_pre_norm_2", lambda ks: XT[:, ks, X], lambda k: HT[:, k, X])
            fence()
            ffn2(l)
        sp.dma(out, XT[:, :, X], s_out, dve.now())
        sp.queue.append(lambda e: e.wait_ge(s_out, 16))

        sp.wait(late, [e.now() for e in (pe, dve, act, pool) if e.count])
        sp.wait([(slot_sem[i], 16 * slot_uses[i]) for i in range(NSLOT)])

        block = ctx.enter_context(nc.Block())

        def run(queue, e):
            for f in queue:
                f(e)

        @block.sync
        def _(e):
            run(sp.queue, e)

        @block.tensor
        def _(e):
            run(pe.queue, e)

        @block.vector
        def _(e):
            run(dve.queue, e)

        @block.scalar
        def _(e):
            run(act.queue, e)

        @block.gpsimd
        def _(e):
            run(pool.queue, e)


def shape_constants():
    f = np.float32
    i = np.arange(128)
    cm = np.zeros((128, 8, 128), f)
    cm[:, 0] = 1.0
    cm[:, 1] = 1.0 / 1024
    cm[:, 2] = 1.0 / 256
    cm[:, 3] = 1.0 / 128
    cm[:, 4] = np.eye(128)
    for m in range(0, 128, 2):
        cm[m + 1, 5, m] = -1.0
        cm[m, 5, m + 1] = 1.0
    for h in (0, 64):
        for d in range(8):
            cm[h + d + 8, 6, h + d] = -1.0
            cm[h + d, 6, h + d + 8] = 1.0
    s, t = i[:, None], i[None, :]
    cg = np.zeros((128, 5120), f)
    for n, m in enumerate((64, 32, 16, 8, 4, 2, 1)):
        mid = (i // (2 * m)) * 2 * m + m
        same = (s // (2 * m)) == (t // (2 * m))
        up_s, up_t = s >= mid[:, None], t >= mid[None, :]
        cg[:, 128 * n:128 * n + 128] = same & (up_s != up_t)
        md = mid[None, :]
        qf = up_t & (s >= md) & (s <= t)
        qb = ~up_t & (s >= t) & (s < md)
        kf = ~up_t & (s > t) & (s < md)
        kb = up_t & (s >= md) & (s < t)
        for base, q, k in ((1024, qf, kf), (2816, qb, kb)):
            cg[:, base + 128 * n:base + 128 * n + 128] = q
            cg[:, base + 896 + 128 * n:base + 1024 + 128 * n] = k
    cg[:, 896:1024] = 2.0 * np.eye(128)
    for n, m in enumerate((s <= t, s >= t, s > t, s < t)):
        cg[:, 4608 + 128 * n:4736 + 128 * n] = m
    pos = np.arange(256)
    inv = (np.float32(10000.0) ** (-np.arange(0, 64, 2, dtype=f) / f(64))).astype(f)
    ang = np.concatenate([(pos // 64).astype(f)[:, None] * inv, (pos % 64).astype(f)[:, None] * inv], 1)
    rope1 = np.stack([np.repeat(np.cos(ang).T, 2, 0), np.repeat(np.sin(ang).T, 2, 0)], 1).astype(f)
    return cm, cg, rope1


def shape_constants_2():
    f = np.float32
    i = np.arange(128)
    s, t = i[:, None], i[None, :]
    c = np.zeros((128, 3648), f)
    k, q = s, t
    off = lambda k0, q0: (q0 + q) - (k0 + k)

    def count(o):
        ok = o >= 0
        return (ok & (o <= 128)).astype(f) + (ok & (o % 4 == 0)) + (ok & (o % 16 == 0))
    parts = ((0, 0), (0, 128), (128, 128))
    for n, (k0, q0) in enumerate(parts):
        c[:, 128 * n:128 * n + 128] = count(off(k0, q0))
    ends = np.arange(15) * 16 + 31
    seen = ends[:, None] <= np.arange(256)[None, :]
    c[0:15, 384:640] = seen
    for pair in range(4):
        for br in range(3):
            a = 640 + 128 * (3 * pair + br)
            c[pair * 3 + br, a:a + 64] = 1.0
            c[(4 + pair) * 3 + br, a + 64:a + 128] = 1.0
    c[:, 2176:2304] = s <= t
    inv = (f(500000.0) ** (f(-2.0) * np.arange(8, dtype=f) / f(16))).astype(f)
    c[:, 2304] = np.where(i % 64 < 16, inv[i % 8], 0.0)
    b = np.zeros((128, 2176), f)
    b[:, 0:128] = np.eye(128)
    for n, (k0, q0) in enumerate(parts):
        ok = off(k0, q0) >= 0
        dil = count(off(k0, q0)) > 0
        w = slice(512 + 128 * n, 640 + 128 * n)
        b[:, w] = np.where(ok, 0.0, MASKED)
        b[:, 1280 + 128 * n:1408 + 128 * n] = np.where(dil, 0.0, MASKED)
    for n, (q0, k0) in enumerate(((0, 0), (128, 0), (128, 128))):
        ok = (off(k0, q0) >= 0).T
        dil = (count(off(k0, q0)) > 0).T
        b[:, 128 + 128 * n:256 + 128 * n] = np.where(ok, 0.0, MASKED)
        b[:, 896 + 128 * n:1024 + 128 * n] = np.where(dil, 0.0, MASKED)
    for u in range(8):
        for qt in range(2):
            a = 1664 + 32 * u + 16 * qt
            b[:, a:a + 15] = np.where(seen[:, 128 * qt:128 * qt + 128].T, 0.0, MASKED)
    b[0:15, 1920:2176] = np.where(seen, 0.0, MASKED)
    c[:, 2560:3648] = (b.view(np.uint32) >> 16).astype(np.uint16).view(f)
    return c


def by_features(w):
    n, k, c = w.shape
    return np.ascontiguousarray(
        w.reshape(n, k // 128, 128, c // 128, 128).transpose(0, 3, 2, 1, 4)).reshape(n, c // 128, 128, k)


def by_tokens(w, width, per):
    n, k, c = w.shape
    return np.ascontiguousarray(
        w.reshape(n, 8 // per, per, 128, c // width, width).transpose(0, 4, 1, 3, 2, 5)
    ).reshape(n, c // width * (8 // per), 128, per * width)


def narrow(w):
    n, k, c = w.shape
    return np.ascontiguousarray(w.reshape(n, 8, 128, c).transpose(0, 2, 1, 3)).reshape(n, 128, 8 * c)


def columns(v):
    return v.reshape(-1, 128).T


def arrange(inp):
    f = np.float32
    a = {}
    a["cm"], a["cg"], a["rope1"] = shape_constants()
    a["cols"] = np.concatenate([columns(inp[name][l]) for name, _ in COLS for l in range(DEPTH)]
                               + [np.full((128, 1), EPS, f)], 1)
    feat = lambda x: np.ascontiguousarray(x[0].T.reshape(8, 128, 256).transpose(1, 0, 2))
    a["x"], a["ctx"] = feat(inp["x"]), feat(inp["ctx"])
    a["cc"] = np.concatenate([columns(inp["c"][0]), columns(inp["c_ctx"])], 1)
    a["w_ada"] = by_features(inp["w_ada"])
    w = inp["w_in"]
    cut = lambda lo, n: w[:, :, lo:lo + n]
    a["w_k"] = by_features(cut(0, 256))
    a["w_v"] = by_tokens(cut(256, 256), 256, 4)
    a["w_kg"] = by_features(cut(512, 512))
    a["w_vg"] = by_tokens(cut(1024, 1024), 512, 2)
    a["w_glr"] = narrow(cut(2048, 32))
    a["w_q"] = by_features(cut(2080, 1024))
    a["w_qg"] = by_features(cut(3104, 512))
    a["w_r"] = by_features(cut(3616, 1024))
    a["w_glu"] = by_features(cut(4640, 2048))
    a["w_gates"] = by_features(cut(6688, 3072))
    for name in ("w_att_o", "w_gla_o", "w_conv_o", "w_out", "w_ff_gate", "w_ff_up", "w_ff_down"):
        a[name] = by_features(inp[name])
    wa = np.zeros((DEPTH, 33, 2, 512), f)
    for d in range(2):
        wa[:, 16 * d:16 * d + 16, d] = inp["gla_w_a2"][:, d]
        wa[:, 32, d] = inp["gla_b_a"][:, d]
    a["wa"] = wa
    a["cvw"] = np.ascontiguousarray(inp["conv_w_dw"][:, :, 0].reshape(DEPTH, 31, 8, 128).transpose(0, 3, 2, 1)
                                    ).reshape(DEPTH, 128, 248)
    a["pos"] = np.ascontiguousarray(inp["positions_2"][0])
    w = inp["w_in_2"]
    nq = w[:, :, 772:1284].reshape(DEPTH, 1024, 2, 4, 64).transpose(0, 1, 3, 2, 4).reshape(DEPTH, 1024, 512)
    kv = [w[:, :, 1284 + 128 * n:1412 + 128 * n] for n in range(6)]
    kc, vc, ks, vs, kw, vw = kv
    a["w_in2"] = by_features(np.concatenate(
        [w[:, :, 0:512], nq, kc, ks, kw, vc, w[:, :, 2076:2588]], 2))
    a["w_ng"] = narrow(w[:, :, 2052:2076])
    a["w_t0"] = by_tokens(np.concatenate([w[:, :, 512:768], vs, vw], 2), 512, 2)
    a["w_t1"] = by_tokens(np.concatenate([w[:, :, 2588:2844], w[:, :, 768:772]], 2), 260, 2)
    w1 = np.stack([inp["cmp_w1_k_2"], inp["cmp_w1_v_2"]], 1)
    a["w_cmp"] = np.ascontiguousarray(
        w1.reshape(DEPTH, 2, 4, 4, 128, 256).transpose(0, 1, 2, 4, 3, 5)).reshape(DEPTH, 8, 128, 1024)
    w2k, w2v = (inp[n].reshape(DEPTH, 2, 128, 64).transpose(0, 2, 1, 3) for n in ("cmp_w2_k_2", "cmp_w2_v_2"))
    a["w2"] = np.ascontiguousarray(np.concatenate([w2k, w2k, w2v], 3)).reshape(DEPTH, 128, 384)
    cg2 = shape_constants_2()
    pe_ = np.stack([inp["cmp_pos_k_2"], inp["cmp_pos_v_2"]], 1)
    cg2[:, 2320:2384] = pe_.reshape(DEPTH, 2, 16, 128).transpose(3, 0, 1, 2).reshape(128, 64)
    cg2[0:24, 2384:2386] = inp["b_nsa_gate_2"].T
    cg2[:, 2400:2408] = np.broadcast_to(inp["b_forget_2"].reshape(1, 8), (128, 8))
    a["cg2"] = cg2
    wo = inp["w_out_2"]
    mid = wo[:, 256:768].reshape(DEPTH, 2, 4, 64, 1024).transpose(0, 2, 1, 3, 4).reshape(DEPTH, 512, 1024)
    a["w_mix"] = by_features(np.concatenate([wo[:, 0:256], mid, wo[:, 768:1024]], 1))
    a["w_up"] = by_features(inp["w_up_2"])
    a["w_down"] = by_features(inp["w_down_2"])
    a["cvw2"] = np.ascontiguousarray(inp["conv_w_2"].reshape(DEPTH, 3, 44, 128).transpose(0, 3, 1, 2)
                                     ).reshape(DEPTH, 128, 132)
    return a


def kernel(**inputs):
    import concourse.bacc as _bacc
    from concourse.bass_utils import run_bass_kernel_spmd as _run

    inp = {k: np.asarray(v) for k, v in inputs.items()}
    arrays = {k + "_in": np.ascontiguousarray(v) for k, v in arrange(inp).items()}
    nc = _bacc.Bacc("TRN2", target_bir_lowering=False, num_devices=1)
    args = {}
    for name, a in arrays.items():
        args[name[:-3]] = nc.dram_tensor(name, a.shape, mybir.dt.from_np(a.dtype), kind="ExternalInput").ap()
    out = nc.dram_tensor("out", (128, 8, 256), F32, kind="ExternalOutput").ap()
    program(nc, args, out)
    r = _run(nc, [arrays], core_ids=[0])
    y = r.results[0]["out"]
    return np.ascontiguousarray(y.transpose(1, 0, 2).reshape(1024, 256).T)[None]
```

```python
from contextlib import ExitStack

import numpy as np

import concourse.bass as bass
from concourse import mybir

ALU = mybir.AluOpType
ACT = mybir.ActivationFunctionType
AXX = mybir.AxisListType.X
F32 = mybir.dt.float32
F32R = mybir.dt.float32r
BF16 = mybir.dt.bfloat16
I32 = mybir.dt.int32

P = 128
DEPTH = 2
EPS = 1e-6
ALPHA = (2.0 * DEPTH) ** 0.25
NSLOT = 6
NFF = 22
SCALE1 = 128.0 ** -0.5
SCALE2 = 0.125
MASKED = -(2.0 ** 100)

COLS = [
    ("b_ada", 48), ("q_norm", 1), ("k_norm", 1), ("gla_norm", 2), ("conv_b_dw", 8),
    ("conv_ln_g", 8), ("conv_ln_b", 8), ("ln1_g", 8), ("ln1_b", 8), ("ln2_g", 8), ("ln2_b", 8),
    ("attn_pre_norm_2", 8), ("attn_post_norm_2", 8), ("ffn_pre_norm_2", 8), ("ffn_post_norm_2", 8),
    ("conv_b_2", 44),
]
COL_AT = {}
_at = 0
for _name, _n in COLS:
    for _l in range(DEPTH):
        COL_AT[_name, _l] = _at
        _at += _n
NCOL = _at


class Engine:

    def __init__(self, name):
        self.name, self.queue, self.count, self.seen = name, [], 0, {}
        self.sem = None
        self.early = []

    def wait(self, *tokens):
        for t in tokens:
            if t is None:
                continue
            if isinstance(t, list):
                self.wait(*t)
                continue
            sem, value = t
            if self.seen.get(id(sem), 0) < value:
                self.seen[id(sem)] = value
                self.queue.append(lambda e, sem=sem, value=value: e.wait_ge(sem, value))

    def do(self, make, *tokens):
        self.wait(*tokens)
        self.count += 1
        self.queue.append(lambda e: make(e).then_inc(self.sem, 1))
        return (self.sem, self.count)

    def quiet(self, make, *tokens):
        self.wait(*tokens)
        self.queue.append(make)

    def dma(self, out, in_, sem, *tokens):
        self.wait(*tokens)
        self.queue.append(lambda e: e.dma_start(out, in_).then_inc(sem, 16))

    def at(self, place, instructions):
        self.early.append((place, instructions))

    def whole(self):
        found, at = [], 0
        for place, instructions in self.early:
            found += self.queue[at:place] + instructions
            at = place
        return found + self.queue[at:]

    def now(self):
        return (self.sem, self.count)


class Bank:
    def __init__(self, ap):
        self.ap, self.free = ap, None


def bc(ap, axis, n):
    a = ap.unsqueeze(axis)
    shape = list(a.shape)
    shape[axis] = n
    return a.to_broadcast(shape)


def program(nc, A, out):
    with ExitStack() as ctx:
        def sb(name, shape, dt=F32):
            return ctx.enter_context(nc.sbuf_tensor(name, shape, dt))

        def sem(name):
            return ctx.enter_context(nc.semaphore(name))

        pe, dve, act, pool, sp = (Engine(n) for n in ("pe", "dve", "act", "pool", "sp"))
        for e in (pe, dve, act, pool):
            e.sem = sem("s_" + e.name)
        s_const = sem("s_const")
        s_copy = sem("s_copy")
        s_out = sem("s_out")
        slot_sem = [sem(f"s_w{i}") for i in range(NSLOT)]

        def placed(name, shape):
            at = (nc.sbuf_base + 31) // 32 * 32
            return sb(name, shape), at

        def over(name, shape, at):
            return nc.alloc_sbuf_tensor_at(name, shape, F32R, offset=at)

        XT = sb("XT", [P, 8, 512])
        HT, at_ht = placed("HT", [P, 8, 512])
        MG, at_mg = placed("MG", [P, 8, 512])
        MGF = MG[:, :, :].rearrange("p a b -> p (a b)")
        RING, at_ring = placed("RING", [P, NSLOT, 1024])
        AR = sb("AR", [P, 20480])
        CM = sb("CM", [P, 8, P])
        Z, at_z = placed("Z", [P, 7168])
        CG = Z[:, 0:5120]
        LGX = Z[:, 5120:7168].rearrange("p (k n) -> p k n", k=4)
        RINGL = over("RINGL", [P, NSLOT, 1024], at_ring)
        HTL = over("HTL", [P, 8, 512], at_ht)
        HTH = over("HTH", [P, 8, 512], at_z)
        WH1 = over("WH1", [P, 3, 1024], at_z + 4 * 4096)
        MGL = over("MGL", [P, 8, 512], at_mg)
        MGH = over("MGH", [P, 8, 512], at_ht)
        HTH2 = over("HTH2", [P, 8, 256], at_z + 4 * 3072)
        WH2 = over("WH2", [P, 4, 1024], at_mg)
        ROPE = sb("ROPE", [P, 2, 256])
        COL = sb("COL", [P, NCOL + 1])
        MOD = sb("MOD", [P, 2, 48, 2])
        WA = sb("WA", [33, 2, 512])
        CVW = sb("CVW", [P, 248])
        SM = sb("SM", [P, 320])
        ROWS = sb("ROWS", [2, 1024])
        RS = sb("RS", [P, 3, 512])
        banks = [Bank(ctx.enter_context(nc.psum_tensor(f"PS{i}", [P, 512], F32))) for i in range(8)]
        turn = [0]

        in_turn = [6]

        def ps():
            b = banks[turn[0] % in_turn[0]]
            turn[0] += 1
            return b

        ONES, M1024, M256, M128, IDENT, R1, R2, ZERO = (CM[:, i, :] for i in range(8))

        def mm(out_, lhsT, rhs, start, stop, *tokens):
            pe.quiet(lambda e: e.matmul(out_, lhsT, rhs, start=start, stop=stop), *tokens)

        def mmt(out_, lhsT, rhs, start, stop, *tokens):
            return pe.do(lambda e: e.matmul(out_, lhsT, rhs, start=start, stop=stop), *tokens)

        def transpose(out_, in_, n, *tokens):
            return pe.do(lambda e: e.transpose(out_, in_, IDENT[0:n, 0:n]), *tokens)

        def tt(eng, out_, a, b, op, *tokens):
            return eng.do(lambda e: e.tensor_tensor(out_, a, b, op), *tokens)

        def ts(eng, out_, a, s1, s2, op0, op1, *tokens):
            if op1 is None:
                return eng.do(lambda e: e.tensor_scalar(out_, a, s1, None, op0), *tokens)
            return eng.do(lambda e: e.tensor_scalar(out_, a, s1, s2, op0, op1), *tokens)

        def stt(out_, a, s, b, op0, op1, *tokens):
            return dve.do(lambda e: e.scalar_tensor_tensor(out=out_, in0=a, scalar=s, in1=b, op0=op0, op1=op1),
                          *tokens)

        def copy(out_, a, *tokens):
            return dve.do(lambda e: e.tensor_copy(out_, a), *tokens)

        def recip(out_, a, *tokens):
            return dve.do(lambda e: e.reciprocal(out_, a), *tokens)

        def rmax(out_, a, *tokens):
            return dve.do(lambda e: e.tensor_reduce(out_, a, AXX, ALU.max), *tokens)

        def af(out_, a, f, *tokens, bias=0.0, scale=1.0, total=None):
            if total is not None:
                return act.do(lambda e: e.activation(out_, a, f, bias=bias, scale=scale, accum_out=total), *tokens)
            return act.do(lambda e: e.activation(out_, a, f, bias=bias, scale=scale), *tokens)

        def fence(hold_pe=True):
            now = [e.now() for e in (pe, dve, act, pool) if e.count]
            for e in (pe, dve, act, pool):
                if e is not pe or hold_pe:
                    e.wait(now)
            return now

        def col(name, l, i=0, rows=P):
            c = COL_AT[name, l] + i
            return COL[0:rows, c:c + 1]

        slot_free = [None] * NSLOT
        slot_uses = [0] * NSLOT
        nload = [0]

        slot_place = [0] * NSLOT
        sp_place = [0]

        def used_up(i):
            slot_free[i], slot_place[i] = pe.now(), len(act.queue)

        def load(src, width=1024):
            i = nload[0] % NSLOT
            nload[0] += 1
            sp_place[0] = max(sp_place[0], slot_place[i])
            slot_uses[i] += 1
            sp.dma(RING[:, i, 0:width], src, slot_sem[i], slot_free[i])
            return i, (slot_sem[i], 16 * slot_uses[i])

        def blocks(name, l, ct, kt_total=8):
            n = (kt_total + 7) // 8
            found = []
            for j in range(n):
                k = min(8, kt_total - 8 * j)
                i, t = load(A[name][l, ct, :, 8 * j * P:(8 * j + k) * P], k * P)
                found.append((i, t, 8 * j, k))
            return found

        side = [None]

        def beside(n):
            for _ in range(n if side[0] is not None else 0):
                if next(side[0], 0) == 0:
                    side[0] = None
                    break

        s_wh, s_wl = sem("s_wh"), sem("s_wl")
        uppers = {"ring": WH1, "n": 3, "floor": 0, "marks": [], "free": {}, "first": 0}
        split_at = [0]

        def split_phase(ring):
            uppers.update(ring=ring, n=ring.shape[1], floor=len(act.queue), marks=[], free={}, first=split_at[0])

        def split(slot, t, width):
            n = split_at[0]
            split_at[0] += 1
            k = n - uppers["first"]
            j = k % uppers["n"]
            uppers["marks"].append(len(act.queue))
            place = max(uppers["marks"][max(0, k - 2)] if k else uppers["floor"], sp_place[0])
            ring, free = uppers["ring"], uppers["free"].get(j)
            wait = [lambda e, t=t: e.wait_ge(*t)] + ([lambda e, f=free: e.wait_ge(*f)] if free else [])
            act.at(place, wait + [lambda e: e.activation(ring[:, j, 0:width], RING[:, slot, 0:width], ACT.Copy)
                                  .then_inc(s_wh, 1)])
            pool.wait((s_wh, n + 1))
            pool.queue.append(lambda e: e.tensor_tensor(RINGL[:, slot, 0:width], RING[:, slot, 0:width],
                                                        ring[:, j, 0:width], ALU.subtract).then_inc(s_wl, 1))
            return j, (s_wl, n + 1)

        def project(name, l, ct, src, cols, kt_total=8, width=P, after=None):
            b = ps()
            n = cols.stop - cols.start
            pe.wait(b.free, after)
            for i, t, k0, k in blocks(name, l, ct, kt_total):
                if isinstance(src, tuple):
                    u, t = split(i, t, k * P)
                    w_up, w_lo = uppers["ring"][:, u, :], RINGL[:, i, :]
                    pe.wait(t)
                    for j in range(k):
                        kt = k0 + j
                        pe.wait(src[2][kt])
                        c = slice(j * P, j * P + width)
                        o = b.ap[0:width, 0:n]
                        mm(o, w_up[:, c], src[0][:, kt, cols], kt == 0, False)
                        mm(o, w_up[:, c], src[1][:, kt, cols], False, False)
                        (mmt if j == k - 1 else mm)(o, w_lo[:, c], src[0][:, kt, cols], False, kt == kt_total - 1)
                    uppers["free"][u] = pe.now()
                else:
                    pe.wait(t)
                    for j in range(k):
                        kt = k0 + j
                        (mmt if j == k - 1 else mm)(
                            b.ap[0:width, 0:n], RING[:, i, j * P:j * P + width], src[:, kt, cols],
                            kt == 0, kt == kt_total - 1)
                used_up(i)
            return b, pe.now()

        def project_tok(name, l, g, tiles, width, per, emit, src=None):
            bs = [ps() for _ in tiles]
            pe.wait([b.free for b in bs])
            for q in range(8 // per):
                i, t = load(A[name][l, g * (8 // per) + q, :, 0:per * width], per * width)
                if src is not None:
                    u, t = split(i, t, per * width)
                    pe.wait(src[2])
                pe.wait(t)
                for b, tile in zip(bs, tiles):
                    for j in range(per):
                        kt = per * q + j
                        x, w = slice(tile * P, tile * P + P), slice(j * width, (j + 1) * width)
                        o = b.ap[:, 0:width]
                        last = mmt if j == per - 1 else mm
                        if src is None:
                            last(o, HT[:, kt, x], RING[:, i, w], kt == 0, kt == 7)
                        else:
                            w_up, w_lo = uppers["ring"][:, u, w], RINGL[:, i, w]
                            mm(o, src[0][:, kt, x], w_up, kt == 0, False)
                            mm(o, src[1][:, kt, x], w_up, False, False)
                            last(o, src[0][:, kt, x], w_lo, False, kt == 7)
                used_up(i)
                if src is not None:
                    uppers["free"][u] = pe.now()
            tok = pe.now()
            for n, b in enumerate(bs):
                b.free = emit(n, b, tok)

        def parts(full, upper, lower, cols, *tokens):
            toks = []
            for k in range(8):
                t = act.do(lambda e, k=k: e.activation(upper[:, k, cols], full[:, k, cols], ACT.Copy), *tokens)
                toks.append(dve.do(lambda e, k=k: e.tensor_tensor(lower[:, k, cols], full[:, k, cols],
                                                                  upper[:, k, cols], ALU.subtract), t))
            return upper, lower, toks

        nconst = [0]

        def const(dst, src):
            sp.dma(dst, src, s_const)
            nconst[0] += 16

        const(CM[:, :, :], A["cm"])
        const(COL[:, :], A["cols"])
        const(XT[:, :, 0:256], A["x"])
        const(XT[:, :, 256:512], A["ctx"])
        const(CG[:, :], A["cg"])
        const(ROPE[:, :, :], A["rope1"])
        const(SM[:, 0:16], A["cc"])
        for e in (pe, dve, act, pool):
            e.wait((s_const, nconst[0]))

        late = []

        def reload(dst, src, *tokens):
            late.append((sem(f"s_late{len(late)}"), 16))
            sp_place[0] = len(act.queue)
            sp.dma(dst, src, late[-1][0], *tokens)
            return late[-1]

        XA, CA = slice(0, 256), slice(256, 512)
        BOTH = slice(0, 512)

        def silu_of(eng_out, in_, *tokens):
            return af(eng_out, in_, ACT.Silu, *tokens)

        SC = SM[:, 16:32].rearrange("p (k n) -> p k n", n=2)
        t_sc = silu_of(SC, SM[:, 0:16].rearrange("p (n k) -> p k n", n=2))

        def over_features(src, nk, mean, n, *tokens):
            b = ps()
            pe.wait(b.free, *tokens)
            for kt in range(nk):
                (mmt if kt == nk - 1 else mm)(b.ap[:, 0:n], mean, src(kt), kt == 0, kt == nk - 1)
            return b, pe.now()

        def rstd_of(b, t, n, i, *tokens):
            r = RS[:, i, 0:n]
            b.free = af(r, b.ap[:, 0:n], ACT.Sqrt, t, dve.now(), *tokens, bias=COL[:, NCOL:NCOL + 1])
            return r, recip(r, r, b.free)

        def center_scale(src, dst, sq, cols, t_in):
            n = cols.stop - cols.start
            b, t = over_features(lambda k: src[:, k, cols], 8, M1024, n, t_in)
            fill(1)
            b2 = ps()
            pe.wait(b2.free)
            for h in range(2):
                ks = slice(4 * h, 4 * h + 4)
                t1 = tt(dve, dst[:, ks, cols], src[:, ks, cols], bc(b.ap[:, 0:n], 1, 4), ALU.subtract, t)
                t2 = af(sq[:, ks, 0:n], dst[:, ks, cols], ACT.Square, t1)
                pe.wait(t2)
                for k in range(4 * h, 4 * h + 4):
                    (mmt if k % 4 == 3 else mm)(b2.ap[:, 0:n], M1024, sq[:, k, 0:n], k == 0, k == 7)
            b.free = t1
            t3 = pe.now()
            fill(1)
            r, t3 = rstd_of(b2, t3, n, 0)
            out_t = []
            for h in range(2):
                ks = slice(4 * h, 4 * h + 4)
                out_t.append(tt(dve, dst[:, ks, cols], dst[:, ks, cols], bc(r, 1, 4), ALU.mult, t3))
            return out_t

        def modulate(l, cols, shift, scale, t_in):
            sq = AR[:, 0:4096].rearrange("p (k n) -> p k n", k=8)
            ts_ = center_scale(XT, HT, sq, cols, t_in)
            for k in range(8):
                for s, c in ((0, XA), (1, CA)):
                    if c.start >= cols.start and c.stop <= cols.stop:
                        af(HT[:, k, c], HT[:, k, c], ACT.Identity, ts_[k // 4],
                           bias=MOD[:, l, 8 * shift + k, s:s + 1], scale=MOD[:, l, 8 * scale + k, s:s + 1])
            return act.now()

        def post(cols, g, b, l, t_in):
            sq = AR[:, 0:4096].rearrange("p (k n) -> p k n", k=8)
            ts_ = center_scale(XT, XT, sq, cols, t_in)
            for k in range(8):
                af(XT[:, k, cols], XT[:, k, cols], ACT.Identity, ts_[k // 4],
                   bias=col(b, l, k), scale=col(g, l, k))
            return act.now()

        def residual(l, name, ct, src, cols, kt_total, gate, tmp, after):
            n = cols.stop - cols.start
            b, t = project(name, l, ct, src, cols, kt_total, after=after)
            for s, c in ((0, XA), (1, CA)):
                if c.start < cols.stop:
                    w = slice(c.start - cols.start, c.stop - cols.start)
                    t1 = af(tmp[:, w], b.ap[:, w], ACT.Copy, t, dve.now(),
                            scale=MOD[:, l, 8 * gate + ct, s:s + 1])
            b.free = t1
            return stt(XT[:, ct, cols], XT[:, ct, cols], ALPHA, tmp[:, 0:n], ALU.mult, ALU.add, t1)

        def pipe(stages, n):
            for i in range(n + len(stages) - 1):
                for s, stage in enumerate(stages):
                    if 0 <= i - s < n:
                        stage(i - s)

        def ada(l, lo, hi):
            for g in range(2 * lo, 2 * hi):
                row_out()
                row_over()
                b = banks[6 + g % 2]
                pe.wait(b.free, t_sc)
                for q in range(4):
                    i, t = load(A["w_ada"][l, 4 * g + q, :, :])
                    pe.wait(t)
                    for j in range(2):
                        kt = 2 * q + j
                        (mmt if j else mm)(b.ap[0:2, :], SC[:, kt, :], RING[:, i, 512 * j:512 * j + 512],
                                           kt == 0, kt == 7)
                    used_up(i)
                rows_in.append((l, g, b, pe.now()))
                yield

        def row_out():
            if rows_in:
                l, g, b, t = rows_in.pop(0)
                b.free = af(ROW[g % 2], b.ap[0:2, :], ACT.Copy, t, row_free[g % 2])
                rows_out.append((l, g, b.free))

        def row_over():
            while len(rows_out) > (1 if rows_in or side_pe[0] is not None else 0):
                l, g, t = rows_out.pop(0)
                b = ps()
                pe.wait(b.free, t)
                for j in range(4):
                    row_free[g % 2] = transpose(b.ap[:, 2 * j:2 * j + 2], ROW[g % 2][:, 128 * j:128 * j + 128], 2)
                c = COL_AT["b_ada", l] + 4 * g
                v = b.ap[:, 0:8].rearrange("p (c n) -> p c n", n=2)
                t = pe.now()
                m = MOD[:, l, 4 * g:4 * g + 4, :]
                b.free = tt(dve, m, v, bc(COL[:, c:c + 4], 2, 2), ALU.add, t)
                if g // 2 in (1, 4):
                    ts(dve, m, m, 1.0, None, ALU.add, None, b.free)

        rows_in, rows_out, side_pe = [], [], [None]

        def fill(n):
            for _ in range(n):
                if side_pe[0] is not None and next(side_pe[0], 0) == 0:
                    side_pe[0] = None

        def fill_all():
            fill(100)
            while rows_in or rows_out:
                row_out()
                row_over()

        ROW = [ROWS[:, 0:512], ROWS[:, 512:1024]]
        row_free = [None, None]

        def view(a, n, m, src=None):
            return (AR if src is None else src)[:, a:a + n * m].rearrange("p (k n) -> p k n", k=n)

        OG = view(0, 8, 512)
        QG = view(4096, 4, 512)
        KG = view(6144, 4, 512)
        VG = view(8192, 4, 1024)
        LGS = [LGX, view(12288, 4, 512)]
        ST = view(14336, 8, 256)
        KGT = view(16384, 2, 512)
        GLRT = AR[:, 17408:17920]
        XE = view(17920, 8, 128)
        QSTB = [view(18944, 2, 256), view(3584, 2, 256, MGF)]
        ATB = [view(19456 + 512 * i, 2, 256) for i in range(2)]
        EX = [view(1792 * i, 14, 128, MGF) for i in range(2)]
        KW = view(0, 4, 512, MGF)
        GT = MGF[:, 3584:4096]
        LM = CG[:, 0:896].rearrange("p (k n) -> p k n", k=7)
        DIAG2 = CG[:, 896:1024]
        CF = CG[:, 1024:2816]
        CB = CG[:, 2816:4608]
        INP, INS, EXS, EXP = (CG[:, 4608 + 128 * i:4736 + 128 * i] for i in range(4))

        QT = view(4096, 8, 512)
        KT = view(12288, 2, 512)
        VT = view(13312, 4, 256)
        PT = [view(14336 + 1024 * i, 4, 256) for i in range(3)]
        SQ = [AR[:, 17408 + 512 * i:17920 + 512 * i] for i in range(6)]

        def gla_projections(l, qcols):
            def keep(dst, scale=1.0):
                def f(b, t):
                    b.free = af(dst, b.ap[:, 0:dst.shape[-1]], ACT.Copy, t, scale=scale)
                return f

            b = ps()
            pe.wait(b.free)
            i, t = load(A["w_glr"][l], 256)
            pe.wait(t)
            for kt in range(8):
                (mmt if kt == 7 else mm)(b.ap[0:32, :], RING[:, i, kt * 32:kt * 32 + 32], HT[:, kt, :],
                                         kt == 0, kt == 7)
            used_up(i)
            b.free = af(GLRT[0:32, :], b.ap[0:32, :], ACT.Copy, pe.now())
            pool.do(lambda e: e.memset(GLRT[32:33, :], 1.0))
            t_glr = [act.now(), pool.now()]
            for ct in range(4):
                keep(KG[:, ct, :])(*project("w_kg", l, ct, HT, BOTH))
            t_kg = act.now()
            for g in range(2):
                def emit(n, b, tok, g=g):
                    return af(VG[:, n, g * 512:g * 512 + 512], b.ap[:, :], ACT.Copy, tok)
                project_tok("w_vg", l, g, range(4), 512, 2, emit)
                gla_gates(1 - g, t_glr)
            for tile in range(2):
                b = ps()
                pe.wait(b.free, t_kg)
                for h in range(4):
                    transpose(b.ap[:, h * P:h * P + P], KG[:, h, 256 + tile * P:384 + tile * P], P)
                b.free = af(KGT[:, tile, :], b.ap[:, :], ACT.Copy, pe.now())
            for ct in range(4):
                keep(QG[:, ct, qcols], SCALE1)(*project("w_qg", l, ct, HT, qcols))

        def gla_gates(seq, t_in):
            LG = LGS[seq]
            for tile in range(2):
                for d in range(2):
                    b = ps()
                    q = 256 * seq + 128 * tile
                    t = mmt(b.ap[:, :], GLRT[0:33, q:q + 128], WA[0:33, d, :], True, True,
                            b.free, t_in, t_wa[0])
                    t1 = af(GT, b.ap[:, :], ACT.Abs, t, dve.now())
                    t2 = af(GT, GT, ACT.Exp, t1, scale=-1.0)
                    t3 = af(GT, GT, ACT.Ln, t2, bias=1.0)
                    b.free = stt(LG[:, 2 * tile + d, :], b.ap[:, :], 0.0, GT, ALU.min, ALU.subtract, t3)

        def gla_states():
            LG = LGS[1]
            for d in range(2):
                for tile in range(2):
                    b = ps()
                    far = tile == (0 if d == 0 else 1)
                    mmt(b.ap[:, :], (EXS, EXP)[d], LG[:, 2 * tile + d, :], True, not far, b.free, dve.now())
                    if far:
                        mmt(b.ap[:, :], ONES, LG[:, 2 * (1 - tile) + d, :], False, True)
                    w = KW[:, 2 * d + tile, :]
                    b.free = af(w, b.ap[:, :], ACT.Exp, pe.now(), scale=1.0 / 16)
                    tt(dve, w, w, KGT[:, tile, :], ALU.mult, act.now())
            fill(2)
            for h in range(4):
                b = ps()
                pe.wait(b.free, dve.now())
                for d in range(2):
                    for tile in range(2):
                        mmt(b.ap[:, d * 256:d * 256 + 256], KW[:, 2 * d + tile, h * P:h * P + P],
                            VG[:, 2 + tile, h * 256:h * 256 + 256], tile == 0, tile == 1)
                b.free = af(ST[:, 2 * h:2 * h + 2, :], b.ap[:, :].rearrange("p (d n) -> p d n", d=2),
                            ACT.Copy, pe.now())

        def gla_outputs(l, seq, states):
            c0 = 256 * seq
            LG = LGS[seq]
            lt = [dve.now()]

            def weights(h):
                at = ATB[h % 2]
                QST = QSTB[h % 2]
                tx = []
                for tile in range(2):
                    b = ps()
                    pe.wait(b.free, lt)
                    lf = LG[:, 2 * tile, h * P:h * P + P]
                    lb = LG[:, 2 * tile + 1, h * P:h * P + P]
                    for n, (g, m) in enumerate(((lf, INP), (lb, INS), (lf, EXS), (lb, EXP))):
                        mmt(b.ap[:, n * P:n * P + P], g, m, True, True)
                    b.free = af(XE[:, 4 * tile:4 * tile + 4, :], b.ap[:, :].rearrange("p (k n) -> p k n", k=4),
                                ACT.Exp, pe.now(), xe_free[0], scale=1.0 / 16)
                tx = act.now()
                t0 = copy(SM[:, 32:33], XE[:, 0, 127:128], tx)
                t0 = copy(SM[:, 33:34], XE[:, 5, 0:1], tx)
                for tile in range(2):
                    q = QG[:, h, c0 + tile * P:c0 + tile * P + P]
                    k = KG[:, h, c0 + tile * P:c0 + tile * P + P]
                    tt(dve, XE[:, 4 * tile:4 * tile + 2, :], XE[:, 4 * tile:4 * tile + 2, :], bc(q, 1, 2),
                       ALU.mult, t0)
                    tt(dve, XE[:, 4 * tile + 2:4 * tile + 4, :], XE[:, 4 * tile + 2:4 * tile + 4, :],
                       bc(k, 1, 2), ALU.mult, t0)
                t_xe = dve.now()
                if states:
                    copy(QST[:, 0, 0:128], XE[:, 0, :], t_xe, qst_free[h % 2])
                    copy(QST[:, 1, 128:256], XE[:, 5, :])
                    ts(dve, QST[:, 0, 128:256], XE[:, 4, :], SM[:, 32:33], None, ALU.mult, None)
                    ts(dve, QST[:, 1, 0:128], XE[:, 1, :], SM[:, 33:34], None, ALU.mult, None)
                t_cross[0] = dve.now()

            def cross(h):
                at = ATB[h % 2]
                b = ps()
                mm(b.ap[:, 0:128], XE[:, 2, :], XE[:, 4, :], True, True, b.free, t_cross[0])
                xe_free[0] = mmt(b.ap[:, 128:256], XE[:, 7, :], XE[:, 1, :], True, True)
                copy(at[:, 0, 128:256], b.ap[:, 0:128], pe.now(), at_free[h % 2])
                b.free = copy(at[:, 1, 0:128], b.ap[:, 128:256])

            def levels(u):
                h, tile = u // 2, u % 2
                if tile == 0:
                    weights(h)
                q = QG[:, h, c0 + tile * P:c0 + tile * P + P]
                k = KG[:, h, c0 + tile * P:c0 + tile * P + P]
                ex = EX[tile]
                lf = LG[:, 2 * tile, h * P:h * P + P]
                lb = LG[:, 2 * tile + 1, h * P:h * P + P]
                for c in range(4):
                    n = 448
                    b = ps()
                    mm(b.ap[:, 0:n], lf, CF[:, c * n:c * n + n], True, False, b.free)
                    mmt(b.ap[:, 0:n], lb, CB[:, c * n:c * n + n], False, True)
                    flat = MGF[:, 1792 * tile + c * n:1792 * tile + c * n + n]
                    b.free = af(flat, b.ap[:, 0:n], ACT.Exp, pe.now(), ex_free[tile], scale=1.0 / 16)
                    if c == 1:
                        tt(dve, ex[:, 0:7, :], ex[:, 0:7, :], bc(q, 1, 7), ALU.mult, act.now())
                tt(dve, ex[:, 7:14, :], ex[:, 7:14, :], bc(k, 1, 7), ALU.mult, act.now())
                gram_in[tile] = dve.now()

            def grams(u):
                h, tile = u // 2, u % 2
                if tile == 0:
                    cross(h)
                at = ATB[h % 2]
                q = QG[:, h, c0 + tile * P:c0 + tile * P + P]
                k = KG[:, h, c0 + tile * P:c0 + tile * P + P]
                ex = EX[tile]
                b1, b2 = ps(), ps()
                pe.wait(b1.free, b2.free, gram_in[tile])
                for n in range(4):
                    (mmt if n == 3 else mm)(b1.ap[:, n * P:n * P + P], ex[:, 7 + n, :], ex[:, n, :], True, True)
                for n in range(4, 7):
                    mm(b2.ap[:, (n - 4) * P:(n - 3) * P], ex[:, 7 + n, :], ex[:, n, :], True, True)
                t = mmt(b2.ap[:, 384:512], k, q, True, True)
                ex_free[tile] = t
                dst = at[:, tile, tile * P:tile * P + P]
                tt(dve, dst, b2.ap[:, 384:512], DIAG2, ALU.mult, t, at_free[h % 2])
                for n in range(7):
                    src = (b1 if n < 4 else b2).ap[:, (n % 4) * P:(n % 4) * P + P]
                    mk = LM[:, n, :].bitcast(I32)
                    dve.do(lambda e, src=src, mk=mk: e.copy_predicated(dst, mk, src), dve.now())
                b1.free = b2.free = at_done[h % 2] = dve.now()

            def outputs(u):
                if u % 2:
                    values(u // 2)

            def values(h):
                at = ATB[h % 2]
                QST = QSTB[h % 2]
                b = ps()
                pe.wait(b.free, at_done[h % 2])
                for et in range(2):
                    o = b.ap[:, et * 256:et * 256 + 256]
                    e0 = h * 256 + et * P
                    mm(o, VG[:, 2 * seq, e0:e0 + P], at[:, 0, :], True, False)
                    mmt(o, VG[:, 2 * seq + 1, e0:e0 + P], at[:, 1, :], False, not states)
                    if states:
                        mm(o, ST[:, 2 * h, et * P:et * P + P], QST[:, 0, :], False, False)
                        mmt(o, ST[:, 2 * h + 1, et * P:et * P + P], QST[:, 1, :], False, True)
                at_free[h % 2] = qst_free[h % 2] = pe.now()
                o = OG[:, 2 * h:2 * h + 2, c0:c0 + 256]
                t = af(o, b.ap[:, :].rearrange("p (k n) -> p k n", k=2), ACT.Copy, pe.now())
                b.free = t

            def norm(h):
                o = OG[:, 2 * h:2 * h + 2, c0:c0 + 256]
                t = act.now()
                t = af(GT.rearrange("p (k n) -> p k n", k=2), o, ACT.Square, t, gt_free[0])
                b2, t = over_features(lambda k: GT[:, k * 256:k * 256 + 256], 2, M256, 256, t)
                gt_free[0] = t
                r, t = rstd_of(b2, t, 256, h % 3)
                for et in range(2):
                    o = OG[:, 2 * h + et, c0:c0 + 256]
                    stt(o, o, col("gla_norm", l, et), r, ALU.mult, ALU.mult, t)

            xe_free, qst_free, at_free, ex_free, gt_free = [None], [None, None], [None, None], [None, None], [None]
            gram_in, at_done, t_cross = [None, None], [None, None], [None]
            pipe([levels, grams, outputs], 8)
            gt_free[0] = pe.now()
            for h in range(4):
                norm(h)

        def att_projections(l, qcols):
            H = hp[0]
            items = [("w_k", ct, KT[:, ct, :], BOTH, "k_norm") for ct in range(2)]
            items += [("w_q", ct, QT[:, ct, qcols], qcols, "q_norm") for ct in range(8)]
            done = {}

            def raw(i):
                name, ct, dst, cols, _ = items[i]
                n = cols.stop
                b, t = project(name, l, ct, H, cols)
                t = af(dst, b.ap[:, 0:n], ACT.Copy, t)
                b.free = t
                done["raw", i] = af(SQ[i % 3][:, 0:n], dst, ACT.Square, t, done.get(("norm", i - 3)))

            def norm(i):
                _, _, dst, cols, g = items[i]
                n = cols.stop
                b, t = over_features(lambda k: SQ[i % 3][:, 0:n], 1, M128, n, done["raw", i])
                done["norm", i] = t
                r, t = rstd_of(b, t, n, i % 3)
                done["scaled", i] = stt(dst, dst, col(g, l), r, ALU.mult, ALU.mult, t)

            def rotate(i):
                dst = items[i][2][:, 0:256]
                b = ps()
                t = mmt(b.ap[:, 0:256], R1, dst, True, True, b.free, done["scaled", i])
                tmp = SQ[3 + i % 3][:, 0:256]
                b.free = tt(dve, tmp, b.ap[:, 0:256], ROPE[:, 1, :], ALU.mult, t, dve.now())
                t = tt(dve, dst, dst, ROPE[:, 0, :], ALU.mult)
                tt(dve, dst, dst, tmp, ALU.add, t)

            pipe([raw, norm, rotate], len(items))

            def emit(n, b, tok):
                return af(VT[:, n, :], b.ap[:, 0:256], ACT.Copy, tok)
            project_tok("w_v", l, 0, range(4), 256, 4, emit, H)

        def attend(q0, k0, nk):
            n = nk * P
            MXC, NMC, DEN, REC = (SM[:, 64 + 16 * i:80 + 16 * i] for i in range(4))
            done = {}
            t_in = [dve.now(), act.now()]

            def weigh(u):
                h, qt = u // 2, u % 2
                c = slice(u, u + 1)
                pq = SQ[u % 5][:, 0:n]
                b = ps()
                t = mmt(b.ap[:, 0:n], QT[:, h, q0 + qt * P:q0 + qt * P + P],
                        KT[:, h // 4, k0:k0 + n], True, True, b.free, t_in)
                t = rmax(MXC[:, c], b.ap[:, 0:n], t)
                t = ts(dve, NMC[:, c], MXC[:, c], -SCALE1, None, ALU.mult, None, t)
                b.free = t = af(pq, b.ap[:, 0:n], ACT.Exp, t, done.get(("turned", u - 5)),
                                bias=NMC[:, c], scale=SCALE1, total=DEN[:, c])
                done["exp", u] = t

            def scale(u):
                c = slice(u, u + 1)
                pq = SQ[u % 5][:, 0:n]
                t = recip(REC[:, c], DEN[:, c], done["exp", u])
                done["weighed", u] = ts(dve, pq, pq, REC[:, c], None, ALU.mult, None, t)

            def turn_over(u):
                h, qt = u // 2, u % 2
                b = ps()
                pe.wait(b.free, done["weighed", u])
                for j in range(nk):
                    t = transpose(b.ap[:, j * P:j * P + P], SQ[u % 5][:, j * P:j * P + P], P)
                done["turned", u] = t
                dst = PT[h % 3][:, 0:nk, qt * P:qt * P + P]
                src = b.ap[:, 0:n].rearrange("p (k n) -> p k n", k=nk)
                old = done.get(("values", h - 3))
                b.free = copy(dst, src, t, old) if qt else af(dst, src, ACT.Copy, t, old)
                done["pt", u] = b.free

            def values(u):
                if u % 2 == 0:
                    return
                h = u // 2
                b = ps()
                pe.wait(b.free, done["pt", u], done["pt", u - 1])
                for j in range(nk):
                    (mmt if j == nk - 1 else mm)(b.ap[:, 0:256], VT[:, k0 // P + j, (h // 4) * P:(h // 4) * P + P],
                                                 PT[h % 3][:, j, :], j == 0, j == nk - 1)
                t = done["values", h] = pe.now()
                b.free = af(QT[:, h, q0:q0 + 256], b.ap[:, 0:256], ACT.Copy, t)

            pipe([weigh, scale, lambda u: None, turn_over, values], 16)

        def merge(l, cols, branch, name, src):
            n = cols.stop
            tmp = [AR[:, 17408 + 512 * i:17408 + 512 * i + n] for i in range(2)]
            t_in = [dve.now(), act.now()]
            used = [dve.now()] * 2
            for ct in range(8):
                bg, tg = project("w_gates", l, 8 * branch + ct, hp[0], cols)
                by, ty = project(name, l, ct, src, cols, after=t_in)
                tp = tmp[ct % 2]
                bg.free = af(tp, bg.ap[:, 0:n], ACT.Sigmoid, tg, used[ct % 2])
                m = MG[:, ct, cols]
                beside(12)
                if branch == 0:
                    by.free = used[ct % 2] = tt(dve, m, tp, by.ap[:, 0:n], ALU.mult, bg.free, ty)
                else:
                    by.free = tt(dve, tp, tp, by.ap[:, 0:n], ALU.mult, bg.free, ty)
                    used[ct % 2] = tt(dve, m, m, tp, ALU.add, by.free)

        def gla_gated(l, cols):
            n = cols.stop
            tmp = [AR[:, 17408 + 512 * i:17408 + 512 * i + n] for i in range(2)]
            used = [dve.now()] * 2
            for ct in range(8):
                b, t = project("w_r", l, ct, hp[0], cols)
                b.free = af(tmp[ct % 2], b.ap[:, 0:n], ACT.Silu, t, used[ct % 2])
                beside(8)
                used[ct % 2] = tt(dve, OG[:, ct, cols], OG[:, ct, cols], tmp[ct % 2], ALU.mult, b.free)

        YP = AR[:, 8192:12768].rearrange("p (k s n) -> p k s n", k=8, s=2)
        ZC = view(12800, 8, 512)
        CSQ = view(4096, 8, 512)

        def glu(l, cols):
            n = cols.stop
            ns = n // 256
            tmp = [AR[:, 17408 + 512 * i:17408 + 512 * i + n] for i in range(2)]
            used = [dve.now()] * 2
            t0 = pool.do(lambda e: e.memset(AR[:, 8192:12768], 0.0), dve.now())
            for ct in range(8):
                ba, ta = project("w_glu", l, ct, hp[0], cols)
                bg, tg = project("w_glu", l, 8 + ct, hp[0], cols)
                tp = tmp[ct % 2]
                bg.free = af(tp, bg.ap[:, 0:n], ACT.Sigmoid, tg, used[ct % 2])
                v = lambda a: a.rearrange("p (s n) -> p s n", s=ns)
                ba.free = used[ct % 2] = tt(dve, YP[:, ct, 0:ns, 15:271], v(ba.ap[:, 0:n]), v(tp), ALU.mult,
                                            t0, bg.free, ta)
                t_y[ct] = ba.free

        t_y = {}

        def taps(l, cols):
            ns = cols.stop // 256
            last = {}
            for c0 in range(0, 8, 4):
                for tap in range(31):
                    for ct in range(c0, c0 + 4):
                        z = ZC[:, ct, cols].rearrange("p (s n) -> p s n", s=ns)
                        y = YP[:, ct, 0:ns, tap:tap + 256]
                        w = CVW[:, ct * 31 + tap:ct * 31 + tap + 1]
                        if tap == 0:
                            last[ct] = ts(dve, z, y, w, col("conv_b_dw", l, ct), ALU.mult, ALU.add, t_y[ct], t_cv[0])
                        else:
                            last[ct] = stt(z, y, w, z, ALU.mult, ALU.add, last[ct])
                        yield

        def conv_norm(l, cols):
            t = center_scale(ZC, ZC, CSQ, cols, dve.now())
            for k in range(8):
                af(ZC[:, k, cols], ZC[:, k, cols], ACT.Silu, t[k // 4],
                   bias=col("conv_ln_b", l, k), scale=col("conv_ln_g", l, k))

        FF = view(0, NFF, 512)

        def ffn(l, cols):
            n = cols.stop
            tmp = [AR[:, 12288 + 512 * i:12288 + 512 * i + n] for i in range(3)]
            used = [dve.now()] * 3
            for j in range(NFF):
                bg, tg = project("w_ff_gate", l, j, hp[0], cols)
                bu, tu = project("w_ff_up", l, j, hp[0], cols)
                bg.free = af(tmp[j % 3], bg.ap[:, 0:n], ACT.Silu, tg, used[j % 3])
                bu.free = used[j % 3] = tt(dve, FF[:, j, cols], tmp[j % 3], bu.ap[:, 0:n], ALU.mult, bg.free, tu)
            for ct in range(8):
                residual(l, "w_ff_down", ct, FF, cols, NFF, 5, AR[:, 16384 + 512 * (ct % 2):16896 + 512 * (ct % 2)],
                         dve.now() if ct == 0 else None)

        t_wa, t_cv, hp = [None], [None], [None]
        t_cg = None
        side_pe[0] = ada(0, 0, 2)
        fill_all()
        for l in range(DEPTH):
            last = l == DEPTH - 1
            cols = XA if last else BOTH
            now = fence()
            t_wa[0] = reload(WA[:, :, :], A["wa"][l], now)
            t_cv[0] = reload(CVW[:, :], A["cvw"][l], now)
            if l == 0:
                modulate(l, BOTH, 0, 1, now)
                fence()
                side_pe[0] = ada(l, 2, 6)
            gla_projections(l, cols)
            fence(False)
            pe.wait(dve.now())
            for e in (pe, dve):
                e.wait(t_cg)
            gla_states()
            fence()
            if not last:
                gla_outputs(l, 1, False)
                fence()
            fill(1)
            gla_outputs(l, 0, True)
            fence(False)
            split_phase(WH1)
            hp[0] = parts(HT, HTH, HTL, BOTH)
            fill(1)
            att_projections(l, cols)
            fill(1)
            fence(False)
            if not last:
                attend(256, 256, 2)
                fill(1)
                fence(False)
            attend(0, 0, 4)
            fence(False)
            glu(l, cols)
            side[0] = taps(l, cols)
            merge(l, cols, 0, "w_att_o", QT)
            gla_gated(l, cols)
            merge(l, cols, 1, "w_gla_o", OG)
            beside(1000)
            conv_norm(l, cols)
            fill_all()
            fence()
            merge(l, cols, 2, "w_conv_o", ZC)
            fence()
            mp = parts(MG, MGH, MGL, cols)
            for ct in range(8):
                residual(l, "w_out", ct, mp, cols, 8, 2, AR[:, 16384 + 512 * (ct % 2):16896 + 512 * (ct % 2)], None)
            fence()
            if not last:
                side_pe[0] = ada(l + 1, 0, 6)
            post(cols, "ln1_g", "ln1_b", l, None)
            fence()
            modulate(l, cols, 3, 4, None)
            fence()
            hp[0] = parts(HT, HTH, HTL, cols)
            ffn(l, cols)
            now = fence()
            if not last:
                t_cg = reload(CG, A["cg"], now)
            post(cols, "ln2_g", "ln2_b", l, None)
            if not last:
                fence()
                fill_all()
                modulate(l + 1, BOTH, 0, 1, None)

        in_turn[0] = 8
        X = slice(0, 256)
        QK = view(0, 16, 256)
        VX = AR[:, 4096:5632].rearrange("p (t h n) -> p t h n", t=2, h=6)
        TK = AR[:, 7168:8192].rearrange("p (a g n) -> p a g n", a=2, g=2)
        XW = AR[:, 8192:9152].rearrange("p (a k g n) -> p a k g n", a=2, k=16, g=2)
        HID = AR[:, 9152:9272].rearrange("p (a j n) -> p a j n", a=2, j=2)
        KCMP = AR[:, 9280:9296]
        VC = AR[0:15, 9296:9424]
        W2 = AR[:, 9600:9984].rearrange("p (j n) -> p j n", j=2)
        MIX = view(10240, 8, 256)
        PB = [AR[:, 12288 + 384 * i:12672 + 384 * i] for i in range(4)]
        PQ = [AR[:, 13824 + 384 * i:14208 + 384 * i] for i in range(4)]
        GQ = AR[:, 15360:15408].rearrange("p (t n) -> p t n", t=2)
        PC = AR[:, 15424:15664].rearrange("p (u q n) -> p u q n", u=8, q=2)
        PCT = AR[0:15, 15872:17920].rearrange("p (u n) -> p u n", u=8)
        TB = [AR[:, 17920 + 512 * i:18432 + 512 * i] for i in range(4)]
        CT8 = AR[0:4, 20224:20480]
        CNT = CG[:, 0:384]
        C01 = CG[:, 384:414].rearrange("p (q n) -> p q n", q=2)
        BNG = CG[:, 416:464].rearrange("p (l n) -> p l n", l=2)
        TRI = CG[:, 2176:2304]
        INVF = CG[:, 2304:2305]
        POSE = CG[:, 2320:2384].rearrange("p (l a k) -> p l a k", l=2, a=2)
        BFG = CG[:, 2400:2408].rearrange("p (l h) -> p l h", l=2)
        CBF = CG[:, 2560:3072].bitcast(BF16)
        IDB, MQ = CBF[:, 0:128], CBF[:, 128:512]
        DQ, CQM = CBF[:, 512:896], CBF[:, 896:1024]
        LFT = SM[:, 272:296].rearrange("p (a t h) -> p a t h", a=3, t=2)
        MX, NMX, DN, RC = (SM[:, 32 + 48 * i:80 + 48 * i].rearrange("p (u q) -> p u q", q=2) for i in range(4))
        CM_ = [SM[:, 224 + 16 * i:240 + 16 * i].rearrange("p (u q) -> p u q", q=2) for i in range(3)]


        def tables(now):
            posi = TB[0][:, 0:256].bitcast(I32)
            t = reload(posi, A["pos"].partition_broadcast(P), now)
            ang, k, r, pf = TB[1][:, 0:256], TB[2][:, 0:256], TB[3][:, 0:256], TB[0][:, 256:512]
            t = copy(pf, posi, t)
            t = ts(dve, ang, pf, INVF, None, ALU.mult, None, t)
            big = 1.5 * 2.0 ** 23
            c1 = 6.28125
            c2 = float(np.round(1.9353071795864769e-3 * 2.0 ** 20) / 2.0 ** 20)
            c3 = 1.9353071795864769e-3 - c2
            for n, shift in ((1, 0.0), (0, 0.25)):
                t = ts(dve, k, ang, 1.0 / (2.0 * np.pi), shift, ALU.mult, ALU.add, dve.now(), act.now())
                t = ts(dve, k, k, big, None, ALU.add, None, t)
                t = ts(dve, k, k, -big, None, ALU.add, None, t)
                t = stt(r, k, -c1, ang, ALU.mult, ALU.add, t)
                t = stt(r, k, -c2, r, ALU.mult, ALU.add, t)
                t = stt(r, k, -c3, r, ALU.mult, ALU.add, t)
                t = ts(dve, r, r, float(2.0 * np.pi * shift), 3.1415925, ALU.add, ALU.min, t)
                t = ts(dve, r, r, -3.1415925, None, ALU.max, None, t)
                af(ROPE[:, n, :], r, ACT.Sin, t)

        def rms(l, name, src_of, dst_of):
            sq = view(10240, 8, 256)
            for h in range(2):
                ks = slice(4 * h, 4 * h + 4)
                t = af(sq[:, ks, :], src_of(ks), ACT.Square, dve.now(), act.now())
            b, t = over_features(lambda k: sq[:, k, :], 8, M1024, 256, t)
            r, t = rstd_of(b, t, 256, 0)
            for k in range(8):
                stt(dst_of(k), src_of(slice(k, k + 1)).rearrange("p a n -> p (a n)"), col(name, l, k), r,
                    ALU.mult, ALU.mult, t)

        def projections2(l):
            rope = {4, 5, 6, 7, 8, 9, 10, 12, 13, 14, 15}
            done = {}

            def raw(i):
                b, t = project("w_in2", l, i, hp[0], X)
                b.free = done[i] = af(QK[:, i, :], b.ap[:, 0:256], ACT.Copy, t)

            def rotate(i):
                if i not in rope:
                    return
                dst = QK[:, i, :]
                b = ps()
                t = mmt(b.ap[:, 0:256], R2, dst, True, True, b.free, done[i])
                tmp = TB[i % 2][:, 0:256]
                b.free = tt(dve, tmp, b.ap[:, 0:256], ROPE[:, 1, :], ALU.mult, t, dve.now())
                t = tt(dve, dst, dst, ROPE[:, 0, :], ALU.mult)
                tt(dve, dst, dst, tmp, ALU.add, t)

            def emit(n, b, tok, first):
                if first:
                    return af(VX[:, n, 0:4, :], b.ap[:, 0:512].rearrange("p (h n) -> p h n", h=4), ACT.Copy, tok)
                t = af(VX[:, n, 4:6, :], b.ap[:, 0:256].rearrange("p (h n) -> p h n", h=2), ACT.Copy, tok)
                t = tt(dve, LFT[:, 0, n, :], b.ap[:, 256:260], BFG[:, l, :], ALU.add, t)
                t = tt(dve, GQ[:, n, :], b.ap[:, 260:284], BNG[:, l, :], ALU.add, t)
                af(GQ[:, n, :], GQ[:, n, :], ACT.Sigmoid, t)
                return t
            project_tok("w_t1", l, 0, range(2), 284, 2, lambda n, b, tok: emit(n, b, tok, False), hp[0])
            project_tok("w_t0", l, 0, range(2), 512, 2, lambda n, b, tok: emit(n, b, tok, True), hp[0])
            pipe([raw, rotate], 16)
            t = af(LFT[:, 1], LFT[:, 0], ACT.Abs, dve.now())
            t = af(LFT[:, 1], LFT[:, 1], ACT.Exp, t, scale=-1.0)
            t = af(LFT[:, 1], LFT[:, 1], ACT.Ln, t, bias=1.0)
            t = stt(LFT[:, 2], LFT[:, 0], 0.0, LFT[:, 1], ALU.min, ALU.subtract, t)
            lf = LFT[:, 2]
            b = ps()
            mm(b.ap[0:4, 0:128], lf[:, 0, :], TRI, True, True, b.free, t)
            mm(b.ap[0:4, 128:256], lf[:, 0, :], ONES, True, False)
            mmt(b.ap[0:4, 128:256], lf[:, 1, :], TRI, False, True)
            b.free = af(CT8, b.ap[0:4, 0:256], ACT.Copy, pe.now(), scale=-8.0)

        def compress(l, t_w2):
            dve.wait(act.now())
            for a, tile in ((0, 8), (1, 11)):
                for g in range(2):
                    src = QK[64 * g:64 * g + 64, tile, :]
                    copy(TK[0:64, a, g, :], src)
                    copy(TK[64:128, a, g, 0:255], src[:, 1:256])
            t = dve.now()
            for a in range(2):
                for g in range(2):
                    for h in range(2):
                        v = TK[:, a, g, 16 * h:16 * h + 240].rearrange("p (n k t) -> p k n t", k=8, t=2)[:, :, :, 0]
                        tt(dve, XW[:, a, 8 * h:8 * h + 8, g, :], v, bc(POSE[:, l, a, 8 * h:8 * h + 8], 2, 15),
                           ALU.add, t)
            t = dve.now()
            for a in range(2):
                b = [ps(), ps()]
                pe.wait(b[0].free, b[1].free, t)
                for c in range(4):
                    i, tw = load(A["w_cmp"][l, 4 * a + c], 1024)
                    pe.wait(tw)
                    for k in range(4):
                        for j in range(2):
                            (mmt if k == 3 else mm)(
                                b[j].ap[:, 0:30], RING[:, i, 256 * k + 128 * j:256 * k + 128 * j + 128],
                                XW[:, a, 4 * c + k, :, :], c == 0 and k == 0, c == 3 and k == 3)
                    used_up(i)
                for j in range(2):
                    b[j].free = af(HID[:, a, j, :], b[j].ap[:, 0:30], ACT.Gelu_apprx_tanh, pe.now())
            b = ps()
            pe.wait(b.free, act.now(), t_w2)
            for j in range(2):
                (mmt if j else mm)(b.ap[:, 0:30], W2[:, j, 0:128], HID[:, 0, j, :], j == 0, j == 1)
            af(KCMP[0:64, 0:15], b.ap[0:64, 0:15], ACT.Copy, pe.now())
            b.free = af(KCMP[64:128, 0:15], b.ap[64:128, 15:30], ACT.Copy)
            b = ps()
            pe.wait(b.free)
            for g in range(2):
                for j in range(2):
                    mmt(b.ap[0:15, 64 * g:64 * g + 64], HID[:, 1, j, 15 * g:15 * g + 15], W2[:, j, 128:192],
                        j == 0, j == 1)
            b.free = af(VC, b.ap[0:15, 0:128], ACT.Copy, pe.now())

        ONE = (True, True)
        UNITS = [("fox", h % 2, h // 2, 2 + h // 2, h // 2, h // 2, None, ONE) for h in range(4)]
        UNITS += [("dil", h % 2, 12 + h // 2, 14 + h // 2, 4 + h // 2, 6 + h // 2, None, ONE) for h in range(4)]
        for i in range(4):
            for g in range(2):
                UNITS += [("sel", g, 4 + i, 9, 2, 2 + i, 1, (False, False)),
                          ("win", g, 4 + i, 10, 3, 2 + i, 2, (False, True))]

        def attention2():
            done = {}

            def weigh(u):
                kind, par, q, k, v, o, br, _ = UNITS[u]
                r = slice(64 * par, 64 * par + 64)
                pq = PQ[u % 4]
                b = ps()
                mm(b.ap[:, 0:384], IDB, DQ if kind == "dil" else MQ, True, False, b.free)
                if kind == "fox":
                    one = IDENT[0:4, u:u + 1].to_broadcast([4, P])
                    mm(b.ap[:, 0:128], one, CT8[:, 0:128], False, False)
                    mm(b.ap[:, 128:384], one, CT8[:, 0:256], False, False)
                mm(b.ap[:, 0:128], QK[r, q, 0:128], QK[r, k, 0:128], False, False)
                t = mmt(b.ap[:, 128:384], QK[r, q, 128:256], QK[r, k, 0:256], False, True)
                parts = ((0, slice(0, 128)), (1, slice(128, 384)))
                for qt, w in parts:
                    rmax(MX[:, u, qt:qt + 1], b.ap[:, w], t)
                t = ts(dve, NMX[:, u, :], MX[:, u, :], -SCALE2, None, ALU.mult, None, dve.now())
                for qt, w in parts:
                    b.free = t = af(pq[:, w], b.ap[:, w], ACT.Exp, t, done.get(("turned", u - 4)),
                                    bias=NMX[:, u, qt:qt + 1], scale=SCALE2, total=DN[:, u, qt:qt + 1])
                if kind == "dil":
                    for qt, w in parts:
                        x, c, d = pq[:, w], CNT[:, w], DN[:, u, qt:qt + 1]
                        t = dve.do(lambda e, x=x, c=c, d=d: e.scalar_tensor_tensor(
                            out=x, in0=x, scalar=1.0, in1=c, op0=ALU.mult, op1=ALU.mult, accum_out=d), b.free)
                done["exp", u] = t

            def scale(u):
                kind, par, q, k, v, o, br, _ = UNITS[u]
                pq = PQ[u % 4]
                parts = ((0, slice(0, 128)), (1, slice(128, 384)))
                t = recip(RC[:, u, :], DN[:, u, :], done["exp", u])
                if br is not None:
                    h = 4 * par + (o - 2)
                    t = tt(dve, RC[:, u, :], RC[:, u, :], GQ[:, :, 3 * h + br], ALU.mult, t)
                for qt, w in parts:
                    done["weighed", u] = ts(dve, pq[:, w], pq[:, w], RC[:, u, qt:qt + 1], None, ALU.mult, None, t)

            def turn_over(u):
                b = ps()
                pe.wait(b.free, done["weighed", u])
                for c, d in ((0, 0), (128, 128), (256, 256)):
                    t = transpose(b.ap[:, d:d + P], PQ[u % 4][:, c:c + P], P)
                done["turned", u] = t
                old = done.get(("values", u - 4))
                b.free = done["pb", u] = (copy(PB[u % 4], b.ap[:, 0:384], t, old) if u % 2 else
                                          af(PB[u % 4], b.ap[:, 0:384], ACT.Copy, t, old))

            def values(u):
                kind, par, q, k, v, o, br, (first, last) = UNITS[u]
                pt = PB[u % 4]
                b = banks[6 + o % 2]
                out_ = b.ap[:, 256 * par:256 * par + 256]
                pe.wait(b.free, done["pb", u])
                if kind == "sel":
                    mm(out_, VC, PCT[:, 2 * (o - 2) + par, :], True, False, t_cmp[0])
                mm(out_, VX[:, 0, v, :], pt[:, 0:256], first, False)
                t = done["values", u] = mmt(out_[:, 128:256], VX[:, 1, v, :], pt[:, 256:384], False, last)
                if last and par:
                    af(MIX[0:64, o, :], b.ap[0:64, 0:256], ACT.Copy, t)
                    b.free = af(MIX[64:128, o, :], b.ap[64:128, 256:512], ACT.Copy, t)

            t_cmp = [None]

            def compressed():
                m, d, r = CM_
                for par in range(2):
                    rows = slice(64 * par, 64 * par + 64)
                    b = ps()
                    mm(b.ap[:, 0:128], IDB, CQM, True, False, b.free, act.now())
                    for i in range(4):
                        for qt in range(2):
                            c = 32 * i + 16 * qt
                            mmt(b.ap[:, c:c + 15], QK[rows, 4 + i, 128 * qt:128 * qt + 128], KCMP[rows, 0:15], False,
                                i == 3 and qt == 1)
                    src = b.ap[:, 0:128].rearrange("p (u q n) -> p u q n", u=4, q=2)[:, :, :, 0:15]
                    pc = PC.rearrange("p (u two) q n -> p two u q n", two=2)[:, par]
                    b.free = dve.do(lambda e, pc=pc, src=src: e.tensor_copy(pc, src), pe.now())
                flat = PC.rearrange("p u q n -> p (u q) n")
                fm, fd, fr = (x.rearrange("p u q -> p (u q)") for x in (m, d, r))
                t = rmax(fm, flat, dve.now())
                t = tt(dve, flat, flat, bc(fm, 2, 15), ALU.subtract, t)
                t = af(flat, flat, ACT.Exp, t, scale=SCALE2)
                t = tt(dve, PC, PC, bc(C01, 1, 8), ALU.mult, t)
                t = dve.do(lambda e: e.tensor_reduce(fd, flat, AXX, ALU.add), t)
                t = ts(dve, fd, fd, 1e-30, None, ALU.max, None, t)
                t = recip(fr, fd, t)
                for u in range(8):
                    h = 4 * (u % 2) + u // 2
                    tt(dve, r[:, u, :], r[:, u, :], GQ[:, :, 3 * h], ALU.mult, t)
                t = tt(dve, flat, flat, bc(fr, 2, 15), ALU.mult, dve.now())

            def compressed_over():
                t = dve.now()
                for i in range(4):
                    b = ps()
                    pe.wait(b.free, t)
                    for j in range(4):
                        u, qt = 2 * i + j // 2, j % 2
                        transpose(b.ap[0:15, j * P:j * P + P], PC[:, u, qt, :], P)
                    b.free = t_cmp[0] = af(PCT[:, 2 * i:2 * i + 2, :],
                                           b.ap[0:15, :].rearrange("p (u n) -> p u n", u=2), ACT.Copy, pe.now())

            in_turn[0] = 6
            steps = [weigh, scale, lambda u: None, turn_over, values]
            for i in range(24 + len(steps) - 1):
                if i == 4:
                    compressed()
                if i == 7:
                    compressed_over()
                for n, f in enumerate(steps):
                    if 0 <= i - n < 24:
                        f(i - n)
            in_turn[0] = 8

        def mix_out(l, name, src, kt_total, norm):
            f = view(12288, 8, 256)
            t_in = dve.now()
            for ct in range(8):
                b, t = project(name, l, ct, src, X, kt_total, after=t_in)
                b.free = af(f[:, ct, :], b.ap[:, 0:256], ACT.Copy, t)
            fence()
            rms(l, norm, lambda ks: f[:, ks, :], lambda k: f[:, k, :])
            tt(dve, XT[:, :, X], XT[:, :, X], f, ALU.add, dve.now())

        def ffn2(l):
            ffv = view(0, NFF, 256)
            ts_ = {}

            def one(j):
                b, t = project("w_up", l, j, hp[0], X)
                tp = TB[(j // NFF + 2 * (j % NFF)) % 4][:, 0:256]
                w = [CVW[:, 44 * n + j:44 * n + j + 1] for n in range(3)]
                t = af(tp, b.ap[:, 0:256], ACT.Identity, t, ts_.get((j % NFF) - 2), t_cv[0],
                       bias=col("conv_b_2", l, j), scale=w[2])
                t = stt(tp[:, 1:256], b.ap[:, 0:255], w[1], tp[:, 1:256], ALU.mult, ALU.add, t)
                b.free = stt(tp[:, 2:256], b.ap[:, 0:254], w[0], tp[:, 2:256], ALU.mult, ALU.add, t)
                return tp, b.free

            for j in range(NFF):
                ta, t1 = one(j)
                tb, t2 = one(j + NFF)
                t1 = af(ta, ta, ACT.Silu, t1)
                ts_[j] = tt(dve, ffv[:, j, :], ta, tb, ALU.mult, t1, t2)
            mix_out(l, "w_down", ffv, NFF, "ffn_post_norm_2")

        now = fence()
        t_c = reload(CG[:, 0:3072], A["cg2"], now)
        for e in (pe, dve, act, pool):
            e.wait(t_c)
        tables(now)
        fence()
        split_phase(WH2)
        for l in range(DEPTH):
            now = fence()
            t_cv[0] = reload(CVW[:, 0:132], A["cvw2"][l], now)
            t_w2 = reload(AR[:, 9600:9984], A["w2"][l], now)
            rms(l, "attn_pre_norm_2", lambda ks: XT[:, ks, X], lambda k: HT[:, k, X])
            fence()
            hp[0] = parts(HT, HTH2, HTL, X)
            projections2(l)
            fence()
            compress(l, t_w2)
            fence()
            attention2()
            fence()
            mix_out(l, "w_mix", MIX, 8, "attn_post_norm_2")
            fence()
            rms(l, "ffn_pre_norm_2", lambda ks: XT[:, ks, X], lambda k: HT[:, k, X])
            fence()
            hp[0] = parts(HT, HTH2, HTL, X)
            ffn2(l)
        sp.dma(out, XT[:, :, X], s_out, dve.now())
        sp.queue.append(lambda e: e.wait_ge(s_out, 16))

        sp.wait(late, [e.now() for e in (pe, dve, act, pool) if e.count])
        sp.wait([(slot_sem[i], 16 * slot_uses[i]) for i in range(NSLOT)])

        block = ctx.enter_context(nc.Block())

        def run(queue, e):
            for f in queue.whole():
                f(e)

        @block.sync
        def _(e):
            run(sp, e)

        @block.tensor
        def _(e):
            run(pe, e)

        @block.vector
        def _(e):
            run(dve, e)

        @block.scalar
        def _(e):
            run(act, e)

        @block.gpsimd
        def _(e):
            run(pool, e)


def shape_constants():
    f = np.float32
    i = np.arange(128)
    cm = np.zeros((128, 8, 128), f)
    cm[:, 0] = 1.0
    cm[:, 1] = 1.0 / 1024
    cm[:, 2] = 1.0 / 256
    cm[:, 3] = 1.0 / 128
    cm[:, 4] = np.eye(128)
    for m in range(0, 128, 2):
        cm[m + 1, 5, m] = -1.0
        cm[m, 5, m + 1] = 1.0
    for h in (0, 64):
        for d in range(8):
            cm[h + d + 8, 6, h + d] = -1.0
            cm[h + d, 6, h + d + 8] = 1.0
    s, t = i[:, None], i[None, :]
    cg = np.zeros((128, 5120), f)
    for n, m in enumerate((64, 32, 16, 8, 4, 2, 1)):
        mid = (i // (2 * m)) * 2 * m + m
        same = (s // (2 * m)) == (t // (2 * m))
        up_s, up_t = s >= mid[:, None], t >= mid[None, :]
        cg[:, 128 * n:128 * n + 128] = same & (up_s != up_t)
        md = mid[None, :]
        qf = up_t & (s >= md) & (s <= t)
        qb = ~up_t & (s >= t) & (s < md)
        kf = ~up_t & (s > t) & (s < md)
        kb = up_t & (s >= md) & (s < t)
        for base, q, k in ((1024, qf, kf), (2816, qb, kb)):
            cg[:, base + 128 * n:base + 128 * n + 128] = q
            cg[:, base + 896 + 128 * n:base + 1024 + 128 * n] = k
    cg[:, 896:1024] = 2.0 * np.eye(128)
    for n, m in enumerate((s <= t, s >= t, s > t, s < t)):
        cg[:, 4608 + 128 * n:4736 + 128 * n] = m
    pos = np.arange(256)
    inv = (np.float32(10000.0) ** (-np.arange(0, 64, 2, dtype=f) / f(64))).astype(f)
    ang = np.concatenate([(pos // 64).astype(f)[:, None] * inv, (pos % 64).astype(f)[:, None] * inv], 1)
    rope1 = np.stack([np.repeat(np.cos(ang).T, 2, 0), np.repeat(np.sin(ang).T, 2, 0)], 1).astype(f)
    return cm, cg, rope1


def shape_constants_2():
    f = np.float32
    i = np.arange(128)
    s, t = i[:, None], i[None, :]
    c = np.zeros((128, 3072), f)
    k, q = s, t
    off = lambda k0, q0: (q0 + q) - (k0 + k)

    def count(o):
        ok = o >= 0
        return (ok & (o <= 128)).astype(f) + (ok & (o % 4 == 0)) + (ok & (o % 16 == 0))
    parts = ((0, 0), (128, 0), (128, 128))
    for n, (q0, k0) in enumerate(parts):
        c[:, 128 * n:128 * n + 128] = count(off(k0, q0)).T
    ends = np.arange(15) * 16 + 31
    seen = ends[:, None] <= np.arange(256)[None, :]
    c[:, 384:399] = seen[:, 0:128].T
    c[:, 399:414] = seen[:, 128:256].T
    c[:, 2176:2304] = s <= t
    inv = (f(500000.0) ** (f(-2.0) * np.arange(8, dtype=f) / f(16))).astype(f)
    c[:, 2304] = np.where(i % 64 < 16, inv[i % 8], 0.0)
    b = np.zeros((128, 1024), f)
    b[:, 0:128] = np.eye(128)
    for n, (q0, k0) in enumerate(parts):
        b[:, 128 + 128 * n:256 + 128 * n] = np.where(off(k0, q0).T >= 0, 0.0, MASKED)
        b[:, 512 + 128 * n:640 + 128 * n] = np.where(count(off(k0, q0)).T > 0, 0.0, MASKED)
    for u in range(4):
        for qt in range(2):
            a = 896 + 32 * u + 16 * qt
            b[:, a:a + 15] = np.where(seen[:, 128 * qt:128 * qt + 128].T, 0.0, MASKED)
    c[:, 2560:3072] = (b.view(np.uint32) >> 16).astype(np.uint16).view(f)
    return c


def by_features(w):
    n, k, c = w.shape
    return np.ascontiguousarray(
        w.reshape(n, k // 128, 128, c // 128, 128).transpose(0, 3, 2, 1, 4)).reshape(n, c // 128, 128, k)


def by_tokens(w, width, per):
    n, k, c = w.shape
    return np.ascontiguousarray(
        w.reshape(n, 8 // per, per, 128, c // width, width).transpose(0, 4, 1, 3, 2, 5)
    ).reshape(n, c // width * (8 // per), 128, per * width)


def narrow(w):
    n, k, c = w.shape
    return np.ascontiguousarray(w.reshape(n, 8, 128, c).transpose(0, 2, 1, 3)).reshape(n, 128, 8 * c)


def columns(v):
    return v.reshape(-1, 128).T


def arrange(inp):
    f = np.float32
    a = {}
    a["cm"], a["cg"], a["rope1"] = shape_constants()
    a["cols"] = np.concatenate([columns(inp[name][l]) for name, _ in COLS for l in range(DEPTH)]
                               + [np.full((128, 1), EPS, f)], 1)
    feat = lambda x: np.ascontiguousarray(x[0].T.reshape(8, 128, 256).transpose(1, 0, 2))
    a["x"], a["ctx"] = feat(inp["x"]), feat(inp["ctx"])
    a["cc"] = np.concatenate([columns(inp["c"][0]), columns(inp["c_ctx"])], 1)
    a["w_ada"] = by_tokens(inp["w_ada"], 512, 2)
    w = inp["w_in"]
    cut = lambda lo, n: w[:, :, lo:lo + n]
    a["w_k"] = by_features(cut(0, 256))
    a["w_v"] = by_tokens(cut(256, 256), 256, 4)
    a["w_kg"] = by_features(cut(512, 512))
    a["w_vg"] = by_tokens(cut(1024, 1024), 512, 2)
    a["w_glr"] = narrow(cut(2048, 32))
    a["w_q"] = by_features(cut(2080, 1024))
    a["w_qg"] = by_features(cut(3104, 512))
    a["w_r"] = by_features(cut(3616, 1024))
    a["w_glu"] = by_features(cut(4640, 2048))
    a["w_gates"] = by_features(cut(6688, 3072))
    for name in ("w_att_o", "w_gla_o", "w_conv_o", "w_out", "w_ff_gate", "w_ff_up", "w_ff_down"):
        a[name] = by_features(inp[name])
    wa = np.zeros((DEPTH, 33, 2, 512), f)
    for d in range(2):
        wa[:, 16 * d:16 * d + 16, d] = inp["gla_w_a2"][:, d]
        wa[:, 32, d] = inp["gla_b_a"][:, d]
    a["wa"] = wa
    a["cvw"] = np.ascontiguousarray(inp["conv_w_dw"][:, :, 0].reshape(DEPTH, 31, 8, 128).transpose(0, 3, 2, 1)
                                    ).reshape(DEPTH, 128, 248)
    a["pos"] = np.ascontiguousarray(inp["positions_2"][0])
    w = inp["w_in_2"]
    nq = w[:, :, 772:1284].reshape(DEPTH, 1024, 2, 4, 64).transpose(0, 1, 3, 2, 4).reshape(DEPTH, 1024, 512)
    kv = [w[:, :, 1284 + 128 * n:1412 + 128 * n] for n in range(6)]
    kc, vc, ks, vs, kw, vw = kv
    a["w_in2"] = by_features(np.concatenate(
        [w[:, :, 0:512], nq, kc, ks, kw, vc, w[:, :, 2076:2588]], 2))
    a["w_t0"] = by_tokens(np.concatenate([w[:, :, 512:768], vs, vw], 2), 512, 2)
    a["w_t1"] = by_tokens(np.concatenate([w[:, :, 2588:2844], w[:, :, 768:772], w[:, :, 2052:2076]], 2), 284, 2)
    w1 = np.stack([inp["cmp_w1_k_2"], inp["cmp_w1_v_2"]], 1)
    a["w_cmp"] = np.ascontiguousarray(
        w1.reshape(DEPTH, 2, 4, 4, 128, 256).transpose(0, 1, 2, 4, 3, 5)).reshape(DEPTH, 8, 128, 1024)
    w2k, w2v = (inp[n].reshape(DEPTH, 2, 128, 64).transpose(0, 2, 1, 3) for n in ("cmp_w2_k_2", "cmp_w2_v_2"))
    a["w2"] = np.ascontiguousarray(np.concatenate([w2k, w2k, w2v], 3)).reshape(DEPTH, 128, 384)
    cg2 = shape_constants_2()
    pe_ = np.stack([inp["cmp_pos_k_2"], inp["cmp_pos_v_2"]], 1)
    cg2[:, 2320:2384] = pe_.reshape(DEPTH, 2, 16, 128).transpose(3, 0, 1, 2).reshape(128, 64)
    cg2[:, 416:464] = np.broadcast_to(inp["b_nsa_gate_2"].reshape(1, 48), (128, 48))
    cg2[:, 2400:2408] = np.broadcast_to(inp["b_forget_2"].reshape(1, 8), (128, 8))
    a["cg2"] = cg2
    wo = inp["w_out_2"]
    mid = wo[:, 256:768].reshape(DEPTH, 2, 4, 64, 1024).transpose(0, 2, 1, 3, 4).reshape(DEPTH, 512, 1024)
    a["w_mix"] = by_features(np.concatenate([wo[:, 0:256], mid, wo[:, 768:1024]], 1))
    a["w_up"] = by_features(inp["w_up_2"])
    a["w_down"] = by_features(inp["w_down_2"])
    a["cvw2"] = np.ascontiguousarray(inp["conv_w_2"].reshape(DEPTH, 3, 44, 128).transpose(0, 3, 1, 2)
                                     ).reshape(DEPTH, 128, 132)
    return a


def kernel(**inputs):
    import concourse.bacc as _bacc
    from concourse.bass_utils import run_bass_kernel_spmd as _run

    inp = {k: np.asarray(v) for k, v in inputs.items()}
    arrays = {k + "_in": np.ascontiguousarray(v) for k, v in arrange(inp).items()}
    nc = _bacc.Bacc("TRN2", target_bir_lowering=False, num_devices=1)
    args = {}
    for name, a in arrays.items():
        args[name[:-3]] = nc.dram_tensor(name, a.shape, mybir.dt.from_np(a.dtype), kind="ExternalInput").ap()
    out = nc.dram_tensor("out", (128, 8, 256), F32, kind="ExternalOutput").ap()
    program(nc, args, out)
    r = _run(nc, [arrays], core_ids=[0])
    y = r.results[0]["out"]
    return np.ascontiguousarray(y.transpose(1, 0, 2).reshape(1024, 256).T)[None]
```

```python
from contextlib import ExitStack

import numpy as np

import concourse.bass as bass
from concourse import mybir

ALU = mybir.AluOpType
ACT = mybir.ActivationFunctionType
AXX = mybir.AxisListType.X
F32 = mybir.dt.float32
F32R = mybir.dt.float32r
BF16 = mybir.dt.bfloat16
I32 = mybir.dt.int32

P = 128
DEPTH = 2
EPS = 1e-6
ALPHA = (2.0 * DEPTH) ** 0.25
NSLOT = 6
NFF = 22
SCALE1 = 128.0 ** -0.5
SCALE2 = 0.125
MASKED = -(2.0 ** 100)

COLS = [
    ("b_ada", 48), ("q_norm", 1), ("k_norm", 1), ("gla_norm", 2), ("conv_b_dw", 8),
    ("conv_ln_g", 8), ("conv_ln_b", 8), ("ln1_g", 8), ("ln1_b", 8), ("ln2_g", 8), ("ln2_b", 8),
    ("attn_pre_norm_2", 8), ("attn_post_norm_2", 8), ("ffn_pre_norm_2", 8), ("ffn_post_norm_2", 8),
    ("conv_b_2", 44),
]
COL_AT = {}
_at = 0
for _name, _n in COLS:
    for _l in range(DEPTH):
        COL_AT[_name, _l] = _at
        _at += _n
NCOL = _at


class Engine:

    def __init__(self, name):
        self.name, self.queue, self.count, self.seen = name, [], 0, {}
        self.sem = None
        self.early = []

    def wait(self, *tokens):
        for t in tokens:
            if t is None:
                continue
            if isinstance(t, list):
                self.wait(*t)
                continue
            sem, value = t
            if self.seen.get(id(sem), 0) < value:
                self.seen[id(sem)] = value
                self.queue.append(lambda e, sem=sem, value=value: e.wait_ge(sem, value))

    def do(self, make, *tokens):
        self.wait(*tokens)
        self.count += 1
        self.queue.append(lambda e: make(e).then_inc(self.sem, 1))
        return (self.sem, self.count)

    def quiet(self, make, *tokens):
        self.wait(*tokens)
        self.queue.append(make)

    def dma(self, out, in_, sem, *tokens):
        self.wait(*tokens)
        self.queue.append(lambda e: e.dma_start(out, in_).then_inc(sem, 16))

    def at(self, place, instructions):
        self.early.append((place, instructions))

    def whole(self):
        found, at = [], 0
        for place, instructions in self.early:
            found += self.queue[at:place] + instructions
            at = place
        return found + self.queue[at:]

    def now(self):
        return (self.sem, self.count)


class Bank:
    def __init__(self, ap):
        self.ap, self.free = ap, None


def bc(ap, axis, n):
    a = ap.unsqueeze(axis)
    shape = list(a.shape)
    shape[axis] = n
    return a.to_broadcast(shape)


def program(nc, A, out):
    with ExitStack() as ctx:
        def sb(name, shape, dt=F32):
            return ctx.enter_context(nc.sbuf_tensor(name, shape, dt))

        def sem(name):
            return ctx.enter_context(nc.semaphore(name))

        pe, dve, act, pool, sp = (Engine(n) for n in ("pe", "dve", "act", "pool", "sp"))
        for e in (pe, dve, act, pool):
            e.sem = sem("s_" + e.name)
        s_const = sem("s_const")
        s_copy = sem("s_copy")
        s_out = sem("s_out")
        slot_sem = [sem(f"s_w{i}") for i in range(NSLOT)]

        def placed(name, shape):
            at = (nc.sbuf_base + 31) // 32 * 32
            return sb(name, shape), at

        def over(name, shape, at):
            return nc.alloc_sbuf_tensor_at(name, shape, F32R, offset=at)

        XT = sb("XT", [P, 8, 512])
        HT, at_ht = placed("HT", [P, 8, 512])
        MG, at_mg = placed("MG", [P, 8, 512])
        MGF = MG[:, :, :].rearrange("p a b -> p (a b)")
        RING, at_ring = placed("RING", [P, NSLOT, 1024])
        AR, at_ar = placed("AR", [P, 20480])
        CM = sb("CM", [P, 8, P])
        Z, at_z = placed("Z", [P, 7168])
        CG = Z[:, 0:5120]
        LGX = Z[:, 5120:7168].rearrange("p (k n) -> p k n", k=4)
        RINGL = over("RINGL", [P, NSLOT, 1024], at_ring)
        HTR = over("HTR", [P, 8, 512], at_ht)
        HTH = over("HTH", [P, 8, 512], at_z)
        ZR = over("ZR", [P, 7168], at_z)
        WH1 = over("WH1", [P, 3, 1024], at_z + 4 * 4096)
        MGR = over("MGR", [P, 8, 512], at_mg)
        HTH2 = over("HTH2", [P, 8, 256], at_z + 4 * 3072)
        WH0 = over("WH0", [P, 3, 1024], at_mg)
        WH2 = over("WH2", [P, 4, 1024], at_mg)
        ARR = over("ARR", [P, 20480], at_ar)
        ROPE = sb("ROPE", [P, 2, 256])
        COL = sb("COL", [P, NCOL + 2])
        MOD = sb("MOD", [P, 2, 48, 2])
        WA, at_wa = placed("WA", [P, 2, 512])
        WAR = over("WAR", [P, 2, 512], at_wa)
        CVW = sb("CVW", [P, 248])
        SM = sb("SM", [P, 320])
        ROWS = sb("ROWS", [2, 1024])
        RS, at_rs = placed("RS", [P, 3, 512])
        RSR = over("RSR", [P, 3, 512], at_rs)
        banks = [Bank(ctx.enter_context(nc.psum_tensor(f"PS{i}", [P, 512], F32))) for i in range(8)]
        turn = [0]

        in_turn = [6]

        def ps():
            b = banks[turn[0] % in_turn[0]]
            turn[0] += 1
            return b

        ONES, M1024, M256, M128, IDENT, R1, R2, ZERO = (CM[:, i, :] for i in range(8))

        def mm(out_, lhsT, rhs, start, stop, *tokens):
            pe.quiet(lambda e: e.matmul(out_, lhsT, rhs, start=start, stop=stop), *tokens)

        def mmt(out_, lhsT, rhs, start, stop, *tokens):
            return pe.do(lambda e: e.matmul(out_, lhsT, rhs, start=start, stop=stop), *tokens)

        def transpose(out_, in_, n, *tokens):
            return pe.do(lambda e: e.transpose(out_, in_, IDENT[0:n, 0:n]), *tokens)

        def tt(eng, out_, a, b, op, *tokens):
            return eng.do(lambda e: e.tensor_tensor(out_, a, b, op), *tokens)

        def ts(eng, out_, a, s1, s2, op0, op1, *tokens):
            if op1 is None:
                return eng.do(lambda e: e.tensor_scalar(out_, a, s1, None, op0), *tokens)
            return eng.do(lambda e: e.tensor_scalar(out_, a, s1, s2, op0, op1), *tokens)

        def stt(out_, a, s, b, op0, op1, *tokens):
            return dve.do(lambda e: e.scalar_tensor_tensor(out=out_, in0=a, scalar=s, in1=b, op0=op0, op1=op1),
                          *tokens)

        def copy(out_, a, *tokens):
            return dve.do(lambda e: e.tensor_copy(out_, a), *tokens)

        def recip(out_, a, *tokens):
            return dve.do(lambda e: e.reciprocal(out_, a), *tokens)

        def rmax(out_, a, *tokens):
            return dve.do(lambda e: e.tensor_reduce(out_, a, AXX, ALU.max), *tokens)

        def af(out_, a, f, *tokens, bias=0.0, scale=1.0, total=None):
            if total is not None:
                return act.do(lambda e: e.activation(out_, a, f, bias=bias, scale=scale, accum_out=total), *tokens)
            return act.do(lambda e: e.activation(out_, a, f, bias=bias, scale=scale), *tokens)

        def fence(hold_pe=True):
            now = [e.now() for e in (pe, dve, act, pool) if e.count]
            for e in (pe, dve, act, pool):
                if e is not pe or hold_pe:
                    e.wait(now)
            return now

        def col(name, l, i=0, rows=P):
            c = COL_AT[name, l] + i
            return COL[0:rows, c:c + 1]

        slot_free = [None] * NSLOT
        slot_uses = [0] * NSLOT
        nload = [0]

        slot_place = [0] * NSLOT
        sp_place = [0]

        def used_up(i):
            slot_free[i], slot_place[i] = pe.now(), len(act.queue)

        def load(src, width=1024):
            i = nload[0] % NSLOT
            nload[0] += 1
            sp_place[0] = max(sp_place[0], slot_place[i])
            slot_uses[i] += 1
            sp.dma(RING[:, i, 0:width], src, slot_sem[i], slot_free[i])
            return i, (slot_sem[i], 16 * slot_uses[i])

        def blocks(name, l, ct, kt_total=8):
            n = (kt_total + 7) // 8
            found = []
            for j in range(n):
                k = min(8, kt_total - 8 * j)
                i, t = load(A[name][l, ct, :, 8 * j * P:(8 * j + k) * P], k * P)
                found.append((i, t, 8 * j, k))
            return found

        side = [None]

        def beside(n):
            for _ in range(n if side[0] is not None else 0):
                if next(side[0], 0) == 0:
                    side[0] = None
                    break

        s_wh, s_wl = sem("s_wh"), sem("s_wl")
        uppers = {"ring": WH1, "n": 3, "floor": 0, "marks": [], "free": {}, "first": 0}
        split_at = [0]

        def split_phase(ring):
            uppers.update(ring=ring, n=ring.shape[1], floor=len(act.queue), marks=[], free={}, first=split_at[0])

        def split(slot, t, width):
            n = split_at[0]
            split_at[0] += 1
            k = n - uppers["first"]
            j = k % uppers["n"]
            uppers["marks"].append(len(act.queue))
            place = max(uppers["marks"][max(0, k - 2)] if k else uppers["floor"], sp_place[0])
            ring, free = uppers["ring"], uppers["free"].get(j)
            wait = [lambda e, t=t: e.wait_ge(*t)] + ([lambda e, f=free: e.wait_ge(*f)] if free else [])
            act.at(place, wait + [lambda e: e.activation(ring[:, j, 0:width], RING[:, slot, 0:width], ACT.Copy)
                                  .then_inc(s_wh, 1)])
            pool.wait((s_wh, n + 1))
            pool.queue.append(lambda e: e.tensor_tensor(RINGL[:, slot, 0:width], RING[:, slot, 0:width],
                                                        ring[:, j, 0:width], ALU.subtract).then_inc(s_wl, 1))
            return j, (s_wl, n + 1)

        def project(name, l, ct, src, cols, kt_total=8, width=P, after=None):
            b = ps()
            n = cols.stop - cols.start
            pe.wait(b.free, after)
            for i, t, k0, k in blocks(name, l, ct, kt_total):
                if isinstance(src, (tuple, list)):
                    u, t = split(i, t, k * P)
                    w_up, w_lo = uppers["ring"][:, u, :], RINGL[:, i, :]
                    pe.wait(t)
                    for j in range(k):
                        kt = k0 + j
                        pe.wait(src[2][kt])
                        c = slice(j * P, j * P + width)
                        o = b.ap[0:width, 0:n]
                        mm(o, w_up[:, c], src[0](kt, cols), kt == 0, False)
                        mm(o, w_up[:, c], src[1](kt, cols), False, False)
                        (mmt if j == k - 1 else mm)(o, w_lo[:, c], src[0](kt, cols), False, kt == kt_total - 1)
                    uppers["free"][u] = pe.now()
                else:
                    pe.wait(t)
                    for j in range(k):
                        kt = k0 + j
                        (mmt if j == k - 1 else mm)(
                            b.ap[0:width, 0:n], RING[:, i, j * P:j * P + width], src[:, kt, cols],
                            kt == 0, kt == kt_total - 1)
                used_up(i)
            return b, pe.now()

        def project_tok(name, l, g, tiles, width, per, emit, src=None):
            bs = [ps() for _ in tiles]
            pe.wait([b.free for b in bs])
            for q in range(8 // per):
                i, t = load(A[name][l, g * (8 // per) + q, :, 0:per * width], per * width)
                if src is not None:
                    u, t = split(i, t, per * width)
                    pe.wait(src[2])
                pe.wait(t)
                for b, tile in zip(bs, tiles):
                    for j in range(per):
                        kt = per * q + j
                        x, w = slice(tile * P, tile * P + P), slice(j * width, (j + 1) * width)
                        o = b.ap[:, 0:width]
                        last = mmt if j == per - 1 else mm
                        if src is None:
                            last(o, HT[:, kt, x], RING[:, i, w], kt == 0, kt == 7)
                        else:
                            w_up, w_lo = uppers["ring"][:, u, w], RINGL[:, i, w]
                            mm(o, src[0](kt, x), w_up, kt == 0, False)
                            mm(o, src[1](kt, x), w_up, False, False)
                            last(o, src[0](kt, x), w_lo, False, kt == 7)
                used_up(i)
                if src is not None:
                    uppers["free"][u] = pe.now()
            tok = pe.now()
            for n, b in enumerate(bs):
                b.free = emit(n, b, tok)

        def of(t, at=0, n=512):
            if len(t.shape) == 3:
                return lambda k, c: t[:, k, c]
            return lambda k, c: t[:, at + n * k + c.start:at + n * k + c.stop]

        def among(*tiles):
            return lambda k, c: tiles[k][:, c]

        def part(full, upper, lower, k, cols, *tokens):
            t = act.do(lambda e: e.activation(upper(k, cols), full(k, cols), ACT.Copy), *tokens)
            return dve.do(lambda e: e.tensor_tensor(lower(k, cols), full(k, cols), upper(k, cols), ALU.subtract), t)

        def parts(full, upper, lower, cols, *tokens):
            return upper, lower, [part(full, upper, lower, k, cols, *tokens) for k in range(8)]

        nconst = [0]

        s_more, s_last = sem("s_more"), sem("s_last")

        def const(dst, src, s=s_const):
            sp.dma(dst, src, s)
            nconst[0] += 16

        const(CM[:, :, :], A["cm"])
        const(COL[:, :], A["cols"])
        const(SM[:, 0:16], A["cc"])
        for e in (pe, dve, act, pool):
            e.wait((s_const, nconst[0]))

        late = []

        def reload(dst, src, *tokens):
            late.append((sem(f"s_late{len(late)}"), 16))
            sp_place[0] = len(act.queue)
            sp.dma(dst, src, late[-1][0], *tokens)
            return late[-1]

        XA, CA = slice(0, 256), slice(256, 512)
        BOTH = slice(0, 512)

        def silu_of(eng_out, in_, *tokens):
            return af(eng_out, in_, ACT.Silu, *tokens)

        SC = SM[:, 16:32].rearrange("p (k n) -> p k n", n=2)
        t_sc = silu_of(SC, SM[:, 0:16].rearrange("p (n k) -> p k n", n=2))

        def over_features(src, nk, mean, n, *tokens):
            b = ps()
            pe.wait(b.free, *tokens)
            for kt in range(nk):
                (mmt if kt == nk - 1 else mm)(b.ap[:, 0:n], mean, src(kt), kt == 0, kt == nk - 1)
            return b, pe.now()

        def rstd_of(b, t, n, i, *tokens):
            r = RS[:, i, 0:n]
            b.free = af(r, b.ap[:, 0:n], ACT.Sqrt, t, dve.now(), *tokens, bias=COL[:, NCOL:NCOL + 1])
            return r, recip(r, r, b.free)

        def center_scale(src, dst, sq, cols, t_in):
            n = cols.stop - cols.start
            b, t = over_features(lambda k: src[:, k, cols], 8, M1024, n, t_in)
            fill(1)
            b2 = ps()
            pe.wait(b2.free)
            for h in range(4):
                ks = slice(2 * h, 2 * h + 2)
                t1 = tt(dve, dst[:, ks, cols], src[:, ks, cols], bc(b.ap[:, 0:n], 1, 2), ALU.subtract, t)
                t2 = af(sq[:, ks, 0:n], dst[:, ks, cols], ACT.Square, t1)
                pe.wait(t2)
                for k in range(2 * h, 2 * h + 2):
                    (mmt if k % 2 else mm)(b2.ap[:, 0:n], M1024, sq[:, k, 0:n], k == 0, k == 7)
            b.free = t1
            t3 = pe.now()
            fill(1)
            r, t3 = rstd_of(b2, t3, n, 0)
            out_t = []
            for k in range(8):
                out_t.append(tt(dve, dst[:, k, cols], dst[:, k, cols], r, ALU.mult, t3))
            return out_t

        def modulate(l, cols, shift, scale, upper):
            sq = AR[:, 0:4096].rearrange("p (k n) -> p k n", k=8)
            ts_ = center_scale(XT, HT, sq, cols, None)
            toks = []
            for k in range(8):
                for s, c in ((0, XA), (1, CA)):
                    if c.start >= cols.start and c.stop <= cols.stop:
                        t = af(HT[:, k, c], HT[:, k, c], ACT.Identity, ts_[k],
                               bias=MOD[:, l, 8 * shift + k, s:s + 1], scale=MOD[:, l, 8 * scale + k, s:s + 1])
                toks.append(part(of(HT), upper, of(HTR), k, cols, t))
            return upper, of(HTR), toks

        def post(cols, g, b, l, t_in):
            sq = AR[:, 0:4096].rearrange("p (k n) -> p k n", k=8)
            ts_ = center_scale(XT, XT, sq, cols, t_in)
            for k in range(8):
                af(XT[:, k, cols], XT[:, k, cols], ACT.Identity, ts_[k],
                   bias=col(b, l, k), scale=col(g, l, k))
            return act.now()

        def residual(l, name, ct, src, cols, kt_total, gate, tmp, after):
            n = cols.stop - cols.start
            b, t = project(name, l, ct, src, cols, kt_total, after=after)
            for s, c in ((0, XA), (1, CA)):
                if c.start < cols.stop:
                    w = slice(c.start - cols.start, c.stop - cols.start)
                    t1 = af(tmp[:, w], b.ap[:, w], ACT.Copy, t, dve.now(),
                            scale=MOD[:, l, 8 * gate + ct, s:s + 1])
            b.free = t1
            return stt(XT[:, ct, cols], XT[:, ct, cols], ALPHA, tmp[:, 0:n], ALU.mult, ALU.add, t1)

        def pipe(stages, n):
            for i in range(n + len(stages) - 1):
                for s, stage in enumerate(stages):
                    if 0 <= i - s < n:
                        stage(i - s)

        def ada(l, lo, hi):
            for g in range(2 * lo, 2 * hi):
                row_out()
                row_over()
                b = banks[6 + g % 2]
                pe.wait(b.free, t_sc)
                for q in range(4):
                    i, t = load(A["w_ada"][l, 4 * g + q, :, :])
                    pe.wait(t)
                    for j in range(2):
                        kt = 2 * q + j
                        (mmt if j else mm)(b.ap[0:2, :], SC[:, kt, :], RING[:, i, 512 * j:512 * j + 512],
                                           kt == 0, kt == 7)
                    used_up(i)
                rows_in.append((l, g, b, pe.now()))
                yield

        def row_out():
            if rows_in:
                l, g, b, t = rows_in.pop(0)
                b.free = af(ROW[g % 2], b.ap[0:2, :], ACT.Copy, t, row_free[g % 2])
                rows_out.append((l, g, b.free))

        def row_over():
            while len(rows_out) > (1 if rows_in or side_pe[0] is not None else 0):
                l, g, t = rows_out.pop(0)
                b = ps()
                pe.wait(b.free, t)
                for j in range(4):
                    row_free[g % 2] = transpose(b.ap[:, 2 * j:2 * j + 2], ROW[g % 2][:, 128 * j:128 * j + 128], 2)
                c = COL_AT["b_ada", l] + 4 * g
                v = b.ap[:, 0:8].rearrange("p (c n) -> p c n", n=2)
                t = pe.now()
                m = MOD[:, l, 4 * g:4 * g + 4, :]
                b.free = tt(dve, m, v, bc(COL[:, c:c + 4], 2, 2), ALU.add, t)
                if g // 2 in (1, 4):
                    ts(dve, m, m, 1.0, None, ALU.add, None, b.free)

        rows_in, rows_out, side_pe = [], [], [None]

        def fill(n):
            for _ in range(n):
                if side_pe[0] is not None and next(side_pe[0], 0) == 0:
                    side_pe[0] = None

        def fill_all():
            fill(100)
            while rows_in or rows_out:
                row_out()
                row_over()

        ROW = [ROWS[:, 0:512], ROWS[:, 512:1024]]
        row_free = [None, None]

        def view(a, n, m, src=None):
            return (AR if src is None else src)[:, a:a + n * m].rearrange("p (k n) -> p k n", k=n)

        OG = view(0, 8, 512)
        QG = view(4096, 4, 512)
        KG = view(6144, 4, 512)
        VG = view(8192, 4, 1024)
        LGS = [LGX, view(12288, 4, 512)]
        ST = view(14336, 8, 256)
        KGT = view(16384, 2, 512)
        GLRT = AR[:, 17408:17920]
        XE = view(17920, 8, 128)
        QSTB = [view(18944, 2, 256), view(3584, 2, 256, MGF)]
        ATB = [view(19456 + 512 * i, 2, 256) for i in range(2)]
        EX = [view(1792 * i, 14, 128, MGF) for i in range(2)]
        KW = view(0, 4, 512, MGF)
        GT = MGF[:, 3584:4096]
        LM = CG[:, 0:896].rearrange("p (k n) -> p k n", k=7)
        DIAG2 = CG[:, 896:1024]
        CF = ZR[:, 1024:2816]
        CB = ZR[:, 2816:4608]
        SUMS = [ZR[:, 4608 + 128 * i:4736 + 128 * i] for i in range(4)]
        LU = [ARR[:, 16384 + 512 * i:16896 + 512 * i].rearrange("p (k n) -> p k n", k=4) for i in range(2)]
        LL = [ZR[:, 5120:7168].rearrange("p (k n) -> p k n", k=4),
              ARR[:, 12288:14336].rearrange("p (k n) -> p k n", k=4)]
        EXS, EXP = (ZR[:, 4608 + 128 * i:4736 + 128 * i].bitcast(F32) for i in (2, 3))

        QT = view(4096, 8, 512)
        KT = view(12288, 2, 512)
        VT = view(13312, 4, 256)
        PT = [view(14336 + 1024 * i, 4, 256) for i in range(3)]
        SQ = [AR[:, 17408 + 512 * i:17920 + 512 * i] for i in range(6)]

        def exact(*tokens):
            af(ZR[:, 1024:5120], CG[:, 1024:5120], ACT.Copy, *tokens)

        def gla_projections(l, qcols):
            def keep(dst, scale=1.0):
                def f(b, t):
                    b.free = af(dst, b.ap[:, 0:dst.shape[-1]], ACT.Copy, t, scale=scale)
                return f

            b = ps()
            pe.wait(b.free)
            i, t = load(A["w_glr"][l], 256)
            H = hp[0]
            u, t = split(i, t, 256)
            pe.wait(t, H[2])
            for kt in range(8):
                w = slice(kt * 32, kt * 32 + 32)
                mm(b.ap[0:32, :], uppers["ring"][:, u, w], H[0](kt, BOTH), kt == 0, False)
                mm(b.ap[0:32, :], uppers["ring"][:, u, w], H[1](kt, BOTH), False, False)
                (mmt if kt == 7 else mm)(b.ap[0:32, :], RINGL[:, i, w], H[0](kt, BOTH), False, kt == 7)
            used_up(i)
            uppers["free"][u] = pe.now()
            b.free = af(GLRT[0:32, :], b.ap[0:32, :], ACT.Copy, pe.now())
            dve.do(lambda e: e.memset(GLRT[32:33, :], 1.0))
            t_glr = [act.now(), dve.now()]
            for ct in range(4):
                keep(KG[:, ct, :])(*project("w_kg", l, ct, H, BOTH))
            t_kg = act.now()
            for g in range(2):
                def emit(n, b, tok, g=g):
                    return af(VG[:, n, g * 512:g * 512 + 512], b.ap[:, :], ACT.Copy, tok)
                project_tok("w_vg", l, g, range(4), 512, 2, emit, H)
                gla_gates(1 - g, t_glr)
            for tile in range(2):
                b = ps()
                pe.wait(b.free, t_kg)
                for h in range(4):
                    transpose(b.ap[:, h * P:h * P + P], KG[:, h, 256 + tile * P:384 + tile * P], P)
                b.free = af(KGT[:, tile, :], b.ap[:, :], ACT.Copy, pe.now())
            for ct in range(4):
                keep(QG[:, ct, qcols], SCALE1)(*project("w_qg", l, ct, H, qcols))

        def gla_gates(seq, t_in):
            LG = LGS[seq]
            g2 = (MGF[:, 3072:3584], GT)
            for tile in range(2):
                bs, ts_ = [], []
                for d in range(2):
                    b = ps()
                    q = 256 * seq + 128 * tile
                    t = mmt(b.ap[:, :], GLRT[0:33, q:q + 128], WA[0:33, d, :], True, True,
                            b.free, t_in, t_wa[0])
                    bs.append(b)
                    ts_.append(af(g2[d], b.ap[:, :], ACT.Abs, t, g_free[d]))
                for f, kw in ((ACT.Exp, dict(scale=-1.0)), (ACT.Ln, dict(bias=1.0))):
                    ts_ = [af(g2[d], g2[d], f, ts_[d], **kw) for d in range(2)]
                for d, b in enumerate(bs):
                    b.free = g_free[d] = stt(LG[:, 2 * tile + d, :], b.ap[:, :], 0.0, g2[d], ALU.min,
                                             ALU.subtract, ts_[d])

        g_free = [None, None]

        def gla_states():
            LG = LGS[1]
            for d in range(2):
                for tile in range(2):
                    b = ps()
                    far = tile == (0 if d == 0 else 1)
                    mmt(b.ap[:, :], (EXS, EXP)[d], LG[:, 2 * tile + d, :], True, not far, b.free, dve.now())
                    if far:
                        mmt(b.ap[:, :], ONES, LG[:, 2 * (1 - tile) + d, :], False, True)
                    w = KW[:, 2 * d + tile, :]
                    b.free = af(w, b.ap[:, :], ACT.Exp, pe.now(), scale=1.0 / 16)
                    tt(dve, w, w, KGT[:, tile, :], ALU.mult, act.now())
            fill(2)
            for h in range(4):
                b = ps()
                pe.wait(b.free, dve.now())
                for d in range(2):
                    for tile in range(2):
                        mmt(b.ap[:, d * 256:d * 256 + 256], KW[:, 2 * d + tile, h * P:h * P + P],
                            VG[:, 2 + tile, h * 256:h * 256 + 256], tile == 0, tile == 1)
                b.free = af(ST[:, 2 * h:2 * h + 2, :], b.ap[:, :].rearrange("p (d n) -> p d n", d=2),
                            ACT.Copy, pe.now())

        def gla_outputs(l, seq, states):
            c0 = 256 * seq
            LG = LGS[seq]
            lt, lu_free = {}, [None, None]

            def log_parts(h):
                c = slice(h * P, h * P + P)
                t = af(LU[h % 2], LG[:, :, c], ACT.Copy, dve.now() if h == 0 else None, lu_free[h % 2])
                lt[h] = [tt(dve, LL[seq][:, :, c], LG[:, :, c], LU[h % 2], ALU.subtract, t)]

            log_parts(0)
            lt[0].append(act.now())

            def weights(h):
                at = ATB[h % 2]
                QST = QSTB[h % 2]
                tx = []
                for tile in range(2):
                    b = ps()
                    pe.wait(b.free, lt[h])
                    for n, m in enumerate(SUMS):
                        g = 2 * tile + n % 2
                        mm(b.ap[:, n * P:n * P + P], LU[h % 2][:, g, :], m, True, False)
                        mmt(b.ap[:, n * P:n * P + P], LL[seq][:, g, h * P:h * P + P], m, False, True)
                    b.free = af(XE[:, 4 * tile:4 * tile + 4, :], b.ap[:, :].rearrange("p (k n) -> p k n", k=4),
                                ACT.Exp, pe.now(), xe_free[0], scale=1.0 / 16)
                tx = act.now()
                t0 = copy(SM[:, 32:33], XE[:, 0, 127:128], tx)
                t0 = copy(SM[:, 33:34], XE[:, 5, 0:1], tx)
                for tile in range(2):
                    q = QG[:, h, c0 + tile * P:c0 + tile * P + P]
                    k = KG[:, h, c0 + tile * P:c0 + tile * P + P]
                    tt(dve, XE[:, 4 * tile:4 * tile + 2, :], XE[:, 4 * tile:4 * tile + 2, :], bc(q, 1, 2),
                       ALU.mult, t0)
                    tt(dve, XE[:, 4 * tile + 2:4 * tile + 4, :], XE[:, 4 * tile + 2:4 * tile + 4, :],
                       bc(k, 1, 2), ALU.mult, t0)
                t_xe = dve.now()
                if states:
                    copy(QST[:, 0, 0:128], XE[:, 0, :], t_xe, qst_free[h % 2])
                    copy(QST[:, 1, 128:256], XE[:, 5, :])
                    ts(dve, QST[:, 0, 128:256], XE[:, 4, :], SM[:, 32:33], None, ALU.mult, None)
                    ts(dve, QST[:, 1, 0:128], XE[:, 1, :], SM[:, 33:34], None, ALU.mult, None)
                t_cross[0] = dve.now()

            def cross(h):
                at = ATB[h % 2]
                b = ps()
                mm(b.ap[:, 0:128], XE[:, 2, :], XE[:, 4, :], True, True, b.free, t_cross[0])
                xe_free[0] = mmt(b.ap[:, 128:256], XE[:, 7, :], XE[:, 1, :], True, True)
                copy(at[:, 0, 128:256], b.ap[:, 0:128], pe.now(), at_free[h % 2])
                b.free = copy(at[:, 1, 0:128], b.ap[:, 128:256])

            def levels(u):
                h, tile = u // 2, u % 2
                if tile == 0:
                    weights(h)
                q = QG[:, h, c0 + tile * P:c0 + tile * P + P]
                k = KG[:, h, c0 + tile * P:c0 + tile * P + P]
                ex = EX[tile]
                head = slice(h * P, h * P + P)
                for c in range(4):
                    n = 448
                    b = ps()
                    pe.wait(b.free)
                    for g, m in enumerate((CF, CB)):
                        m = m[:, c * n:c * n + n]
                        mm(b.ap[:, 0:n], LU[h % 2][:, 2 * tile + g, :], m, g == 0, False)
                        (mmt if g else mm)(b.ap[:, 0:n], LL[seq][:, 2 * tile + g, head], m, False, g == 1)
                    flat = MGF[:, 1792 * tile + c * n:1792 * tile + c * n + n]
                    b.free = af(flat, b.ap[:, 0:n], ACT.Exp, pe.now(), ex_free[tile], scale=1.0 / 16)
                    if c == 1:
                        tt(dve, ex[:, 0:7, :], ex[:, 0:7, :], bc(q, 1, 7), ALU.mult, act.now())
                tt(dve, ex[:, 7:14, :], ex[:, 7:14, :], bc(k, 1, 7), ALU.mult, act.now())
                gram_in[tile] = dve.now()
                if tile:
                    lu_free[h % 2] = pe.now()
                elif h < 3:
                    log_parts(h + 1)

            def grams(u):
                h, tile = u // 2, u % 2
                if tile == 0:
                    cross(h)
                at = ATB[h % 2]
                q = QG[:, h, c0 + tile * P:c0 + tile * P + P]
                k = KG[:, h, c0 + tile * P:c0 + tile * P + P]
                ex = EX[tile]
                b1, b2 = ps(), ps()
                pe.wait(b1.free, b2.free, gram_in[tile])
                for n in range(4):
                    (mmt if n == 3 else mm)(b1.ap[:, n * P:n * P + P], ex[:, 7 + n, :], ex[:, n, :], True, True)
                for n in range(4, 7):
                    mm(b2.ap[:, (n - 4) * P:(n - 3) * P], ex[:, 7 + n, :], ex[:, n, :], True, True)
                t = mmt(b2.ap[:, 384:512], k, q, True, True)
                ex_free[tile] = t
                dst = at[:, tile, tile * P:tile * P + P]
                tt(dve, dst, b2.ap[:, 384:512], DIAG2, ALU.mult, t, at_free[h % 2])
                for n in range(7):
                    src = (b1 if n < 4 else b2).ap[:, (n % 4) * P:(n % 4) * P + P]
                    mk = LM[:, n, :].bitcast(I32)
                    dve.do(lambda e, src=src, mk=mk: e.copy_predicated(dst, mk, src), dve.now())
                b1.free = b2.free = at_done[h % 2] = dve.now()

            def outputs(u):
                if u % 2:
                    values(u // 2)

            def values(h):
                at = ATB[h % 2]
                QST = QSTB[h % 2]
                b = ps()
                pe.wait(b.free, at_done[h % 2])
                for et in range(2):
                    o = b.ap[:, et * 256:et * 256 + 256]
                    e0 = h * 256 + et * P
                    mm(o, VG[:, 2 * seq, e0:e0 + P], at[:, 0, :], True, False)
                    mmt(o, VG[:, 2 * seq + 1, e0:e0 + P], at[:, 1, :], False, not states)
                    if states:
                        mm(o, ST[:, 2 * h, et * P:et * P + P], QST[:, 0, :], False, False)
                        mmt(o, ST[:, 2 * h + 1, et * P:et * P + P], QST[:, 1, :], False, True)
                at_free[h % 2] = qst_free[h % 2] = pe.now()
                o = OG[:, 2 * h:2 * h + 2, c0:c0 + 256]
                t = af(o, b.ap[:, :].rearrange("p (k n) -> p k n", k=2), ACT.Copy, pe.now())
                b.free = t

            def norm(h):
                o = OG[:, 2 * h:2 * h + 2, c0:c0 + 256]
                t = act.now()
                t = af(GT.rearrange("p (k n) -> p k n", k=2), o, ACT.Square, t, gt_free[0])
                b2, t = over_features(lambda k: GT[:, k * 256:k * 256 + 256], 2, M256, 256, t)
                gt_free[0] = t
                r, t = rstd_of(b2, t, 256, h % 3)
                for et in range(2):
                    o = OG[:, 2 * h + et, c0:c0 + 256]
                    stt(o, o, col("gla_norm", l, et), r, ALU.mult, ALU.mult, t)

            xe_free, qst_free, at_free, ex_free, gt_free = [None], [None, None], [None, None], [None, None], [None]
            gram_in, at_done, t_cross = [None, None], [None, None], [None]
            pipe([levels, grams, outputs], 8)
            gt_free[0] = pe.now()
            for h in range(4):
                norm(h)

        def att_projections(l, qcols):
            H = hp[0]
            items = [("w_k", ct, KT[:, ct, :], BOTH, "k_norm") for ct in range(2)]
            items += [("w_q", ct, QT[:, ct, qcols], qcols, "q_norm") for ct in range(8)]
            done = {}

            def raw(i):
                name, ct, dst, cols, _ = items[i]
                n = cols.stop
                b, t = project(name, l, ct, H, cols)
                t = af(dst, b.ap[:, 0:n], ACT.Copy, t)
                b.free = t
                done["raw", i] = af(SQ[i % 3][:, 0:n], dst, ACT.Square, t, done.get(("norm", i - 3)))

            def norm(i):
                _, _, dst, cols, g = items[i]
                n = cols.stop
                b, t = over_features(lambda k: SQ[i % 3][:, 0:n], 1, M128, n, done["raw", i])
                done["norm", i] = t
                r, t = rstd_of(b, t, n, i % 3)
                done["scaled", i] = stt(dst, dst, col(g, l), r, ALU.mult, ALU.mult, t)

            def rotate(i):
                dst = items[i][2][:, 0:256]
                b = ps()
                t = mmt(b.ap[:, 0:256], R1, dst, True, True, b.free, done["scaled", i])
                tmp = SQ[3 + i % 3][:, 0:256]
                b.free = tt(dve, tmp, b.ap[:, 0:256], ROPE[:, 1, :], ALU.mult, t, dve.now())
                t = tt(dve, dst, dst, ROPE[:, 0, :], ALU.mult)
                tt(dve, dst, dst, tmp, ALU.add, t)

            pipe([raw, norm, rotate], len(items))

            def emit(n, b, tok):
                return af(VT[:, n, :], b.ap[:, 0:256], ACT.Copy, tok)
            project_tok("w_v", l, 0, range(4), 256, 4, emit, H)

        def attend(q0, k0, nk):
            n = nk * P
            MXC, NMC, DEN, REC = (SM[:, 64 + 16 * i:80 + 16 * i] for i in range(4))
            done = {}
            t_in = [dve.now(), act.now()]

            def weigh(u):
                h, qt = u // 2, u % 2
                c = slice(u, u + 1)
                pq = SQ[u % 5][:, 0:n]
                b = ps()
                t = mmt(b.ap[:, 0:n], QT[:, h, q0 + qt * P:q0 + qt * P + P],
                        KT[:, h // 4, k0:k0 + n], True, True, b.free, t_in)
                t = rmax(MXC[:, c], b.ap[:, 0:n], t)
                t = ts(dve, NMC[:, c], MXC[:, c], -SCALE1, None, ALU.mult, None, t)
                b.free = t = af(pq, b.ap[:, 0:n], ACT.Exp, t, done.get(("turned", u - 5)),
                                bias=NMC[:, c], scale=SCALE1, total=DEN[:, c])
                done["exp", u] = t

            def scale(u):
                c = slice(u, u + 1)
                pq = SQ[u % 5][:, 0:n]
                t = recip(REC[:, c], DEN[:, c], done["exp", u])
                done["weighed", u] = ts(dve, pq, pq, REC[:, c], None, ALU.mult, None, t)

            def turn_over(u):
                h, qt = u // 2, u % 2
                b = ps()
                pe.wait(b.free, done["weighed", u])
                for j in range(nk):
                    t = transpose(b.ap[:, j * P:j * P + P], SQ[u % 5][:, j * P:j * P + P], P)
                done["turned", u] = t
                dst = PT[h % 3][:, 0:nk, qt * P:qt * P + P]
                src = b.ap[:, 0:n].rearrange("p (k n) -> p k n", k=nk)
                old = done.get(("values", h - 3))
                b.free = copy(dst, src, t, old) if qt else af(dst, src, ACT.Copy, t, old)
                done["pt", u] = b.free

            def values(u):
                if u % 2 == 0:
                    return
                h = u // 2
                b = ps()
                pe.wait(b.free, done["pt", u], done["pt", u - 1])
                for j in range(nk):
                    (mmt if j == nk - 1 else mm)(b.ap[:, 0:256], VT[:, k0 // P + j, (h // 4) * P:(h // 4) * P + P],
                                                 PT[h % 3][:, j, :], j == 0, j == nk - 1)
                t = done["values", h] = pe.now()
                b.free = af(QT[:, h, q0:q0 + 256], b.ap[:, 0:256], ACT.Copy, t)

            pipe([weigh, scale, lambda u: None, turn_over, values], 16)

        def merge(l, cols, branch, name, src):
            n = cols.stop
            tmp = [AR[:, 17408 + 512 * i:17408 + 512 * i + n] for i in range(2)]
            t_in = [dve.now(), act.now()]
            used = [dve.now()] * 2
            for ct in range(8):
                bg, tg = project("w_gates", l, 8 * branch + ct, hp[0], cols)
                by, ty = project(name, l, ct, src, cols, after=t_in)
                tp = tmp[ct % 2]
                bg.free = af(tp, bg.ap[:, 0:n], ACT.Sigmoid, tg, used[ct % 2])
                m = MG[:, ct, cols]
                beside(15 if branch == 0 else 1)
                if branch == 0:
                    by.free = used[ct % 2] = tt(dve, m, tp, by.ap[:, 0:n], ALU.mult, bg.free, ty)
                else:
                    by.free = tt(dve, tp, tp, by.ap[:, 0:n], ALU.mult, bg.free, ty)
                    used[ct % 2] = tt(dve, m, m, tp, ALU.add, by.free)

        def gla_gated(l, cols, qt_free):
            toks = []
            n = cols.stop
            tmp = [AR[:, 17408 + 512 * i:17408 + 512 * i + n] for i in range(2)]
            used = [dve.now()] * 2
            for ct in range(8):
                b, t = project("w_r", l, ct, hp[0], cols)
                b.free = af(tmp[ct % 2], b.ap[:, 0:n], ACT.Silu, t, used[ct % 2])
                beside(6)
                used[ct % 2] = t = tt(dve, OG[:, ct, cols], OG[:, ct, cols], tmp[ct % 2], ALU.mult, b.free)
                toks.append(part(of(OG), of(ARR, 4096), of(ARR, 0), ct, cols, t, qt_free))
            return of(ARR, 4096), of(ARR, 0), toks

        YP = AR[:, 8192:12768].rearrange("p (k s n) -> p k s n", k=8, s=2)
        ZC = view(12800, 8, 512)
        CSQ = view(8192, 8, 512)

        def glu(l, cols, qp):
            t_q = [act.now(), dve.now()]
            n = cols.stop
            ns = n // 256
            tmp = [AR[:, 17408 + 512 * i:17408 + 512 * i + n] for i in range(2)]
            used = [dve.now()] * 2
            dve.wait(act.now(), pe.now())
            dve.do(lambda e: e.memset(YP[:, :, :, 0:15], 0.0))
            t0 = dve.do(lambda e: e.memset(YP[:, :, :, 271:286], 0.0))
            for ct in range(8):
                ba, ta = project("w_glu", l, ct, hp[0], cols)
                bg, tg = project("w_glu", l, 8 + ct, hp[0], cols)
                tp = tmp[ct % 2]
                bg.free = af(tp, bg.ap[:, 0:n], ACT.Sigmoid, tg, used[ct % 2])
                v = lambda a: a.rearrange("p (s n) -> p s n", s=ns)
                ba.free = used[ct % 2] = tt(dve, YP[:, ct, 0:ns, 15:271], v(ba.ap[:, 0:n]), v(tp), ALU.mult,
                                            t0, bg.free, ta)
                t_y[ct] = ba.free
                qp[2].append(part(of(QT), *qp[0:2], ct, cols, t_q))
                if ct >= 2:
                    beside(12 if ct < 4 else 13)

        t_y = {}

        def taps(l, cols):
            ns = cols.stop // 256
            last = {}
            for cts in ((0, 1), (2, 3), (4, 5, 6, 7)):
                for tap in range(31):
                    for ct in cts:
                        z = ZC[:, ct, cols].rearrange("p (s n) -> p s n", s=ns)
                        y = YP[:, ct, 0:ns, tap:tap + 256]
                        w = CVW[:, ct * 31 + tap:ct * 31 + tap + 1]
                        if tap == 0:
                            last[ct] = ts(dve, z, y, w, col("conv_b_dw", l, ct), ALU.mult, ALU.add, t_y[ct], t_cv[0])
                        else:
                            last[ct] = stt(z, y, w, z, ALU.mult, ALU.add, last[ct])
                        yield

        def conv_norm(l, cols):
            n = cols.stop
            t_in = dve.now()
            yield
            b, t = over_features(lambda k: ZC[:, k, cols], 8, M1024, n, t_in)
            t2 = []
            for k in range(0, 8, 2):
                ks = slice(k, k + 2)
                b.free = tt(dve, ZC[:, ks, cols], ZC[:, ks, cols], bc(b.ap[:, 0:n], 1, 2), ALU.subtract, t)
                t2.append(af(CSQ[:, ks, cols], ZC[:, ks, cols], ACT.Square, b.free))
            yield
            b, t = over_features(lambda k: CSQ[:, k, cols], 8, M1024, n, t2)
            yield
            r, tr = rstd_of(b, t, n, 0)
            for k in range(8):
                t1 = tt(dve, ZC[:, k, cols], ZC[:, k, cols], r, ALU.mult, tr)
                t1 = af(ZC[:, k, cols], ZC[:, k, cols], ACT.Silu, t1,
                        bias=col("conv_ln_b", l, k), scale=col("conv_ln_g", l, k))
                cp[2].append(part(of(ZC), *cp[0:2], k, cols, t1, t))
                if k % 4 == 3:
                    yield

        cp = [of(ARR, 8192), of(ARR, 12800), []]

        FF = view(0, NFF, 512)

        def ffn(l, cols):
            n = cols.stop
            tmp = [AR[:, 12288 + 512 * i:12288 + 512 * i + n] for i in range(3)]
            used = [dve.now()] * 3
            free = [ARR[:, 11264 + 512 * i:11776 + 512 * i] for i in (0, 1, 5, 6, 7, 8, 9, 12, 13, 14, 15, 16, 17)]
            free += [MGR[:, k, :] for k in range(8)] + [RSR[:, 1, :]]
            ffp = among(*free), of(ARR), []
            for j in range(NFF):
                bg, tg = project("w_ff_gate", l, j, hp[0], cols)
                bu, tu = project("w_ff_up", l, j, hp[0], cols)
                bg.free = af(tmp[j % 3], bg.ap[:, 0:n], ACT.Silu, tg, used[j % 3])
                bu.free = used[j % 3] = tt(dve, FF[:, j, cols], tmp[j % 3], bu.ap[:, 0:n], ALU.mult, bg.free, tu)
                beside(1)
                if j:
                    ffp[2].append(part(of(FF), *ffp[0:2], j - 1, cols, ff_t))
                ff_t = bu.free
            ffp[2].append(part(of(FF), *ffp[0:2], NFF - 1, cols, ff_t))
            for ct in range(8):
                residual(l, "w_ff_down", ct, ffp, cols, NFF, 5, AR[:, 16384 + 512 * (ct % 2):16896 + 512 * (ct % 2)],
                         dve.now() if ct == 0 else None)

        def tables(now):
            posi, pf, ang, k, r = (AR[:, 512 * i + 256:512 * i + 512] for i in range(5))
            posi = posi.bitcast(I32)
            t_p = reload(posi, A["pos"].partition_broadcast(P), now)
            yield
            t = copy(pf, posi, t_p)
            yield
            t_a = t = ts(dve, ang, pf, COL[:, NCOL + 1:NCOL + 2], None, ALU.mult, None, t)
            yield
            big = 1.5 * 2.0 ** 23
            c1 = 6.28125
            c2 = float(np.round(1.9353071795864769e-3 * 2.0 ** 20) / 2.0 ** 20)
            c3 = 1.9353071795864769e-3 - c2
            for n, shift in ((1, 0.0), (0, 0.25)):
                t = ts(dve, k, ang, 1.0 / (2.0 * np.pi), shift, ALU.mult, ALU.add, t_a, t)
                yield
                t = ts(dve, k, k, big, None, ALU.add, None, t)
                yield
                t = ts(dve, k, k, -big, None, ALU.add, None, t)
                yield
                t = stt(r, k, -c1, ang, ALU.mult, ALU.add, t)
                yield
                t = stt(r, k, -c2, r, ALU.mult, ALU.add, t)
                yield
                t = stt(r, k, -c3, r, ALU.mult, ALU.add, t)
                yield
                t = ts(dve, r, r, float(2.0 * np.pi * shift), 3.1415925, ALU.add, ALU.min, t)
                yield
                t = ts(dve, r, r, -3.1415925, None, ALU.max, None, t)
                t = af(ROPE[:, n, :], r, ACT.Sin, t)
                yield

        t_wa, t_cv, hp = [None], [None], [None]
        t_cg = None
        side_pe[0] = ada(0, 0, 2)
        fill(3)
        nconst[0] = 0
        const(XT[:, :, 0:256], A["x"], s_more)
        const(XT[:, :, 256:512], A["ctx"], s_more)
        fill_all()
        for e in (pe, dve, act, pool):
            e.wait((s_more, nconst[0]))
        const(CG[:, :], A["cg"], s_last)
        const(ROPE[:, :, :], A["rope1"], s_last)
        for l in range(DEPTH):
            last = l == DEPTH - 1
            cols = XA if last else BOTH
            now = [e.now() for e in (pe, dve, act, pool)]
            t_wa[0] = reload(WA[0:33, :, :], A["wa"][l], now)
            t_cv[0] = reload(CVW[:, :], A["cvw"][l], now)
            if l == 0:
                split_phase(WH0)
                hp[0] = modulate(l, BOTH, 0, 1, of(ARR))
                for e in (pe, dve, act, pool):
                    e.wait((s_last, 32))
                exact()
                side_pe[0] = ada(l, 2, 6)
            gla_projections(l, cols)
            t_ht = pe.now()
            fence(False)
            pe.wait(dve.now())
            for e in (pe, dve):
                e.wait(t_cg)
            gla_states()
            for k in range(8):
                tt(pool, HT[:, k, :], ARR[:, 512 * k:512 * k + 512], HTR[:, k, :], ALU.add, t_ht)
            fence()
            if not last:
                gla_outputs(l, 1, False)
                fence()
            fill(1)
            gla_outputs(l, 0, True)
            fence(False)
            split_phase(WH1)
            hp[0] = parts(of(HT), of(HTH), of(HTR), BOTH)
            fill(1)
            att_projections(l, cols)
            fill(1)
            fence(False)
            if not last:
                attend(256, 256, 2)
                fill(1)
                fence(False)
            attend(0, 0, 4)
            fence(False)
            free = [ARR[:, a:a + 512] for a in (16896, 18432, 18944, 19456, 19968)]
            free += [RSR[:, 1, :], RSR[:, 2, :], WAR[:, 0, :]]
            qp = among(*free), of(ARR, 4096), []
            side[0] = taps(l, cols)
            glu(l, cols, qp)
            merge(l, cols, 0, "w_att_o", qp)
            op = gla_gated(l, cols, pe.now())
            beside(1000)
            cp[2] = []
            side[0] = conv_norm(l, cols)
            merge(l, cols, 1, "w_gla_o", op)
            beside(1000)
            fill_all()
            merge(l, cols, 2, "w_conv_o", cp)
            fence()
            mp = parts(of(MG), of(HTR), of(MGR), cols)
            for ct in range(8):
                residual(l, "w_out", ct, mp, cols, 8, 2, AR[:, 16384 + 512 * (ct % 2):16896 + 512 * (ct % 2)], None)
            fence()
            if not last:
                side_pe[0] = ada(l + 1, 0, 6)
            post(cols, "ln1_g", "ln1_b", l, None)
            fence()
            hp[0] = modulate(l, cols, 3, 4, of(HTH))
            if last:
                side[0] = tables([e.now() for e in (pe, dve, act, pool)])
            ffn(l, cols)
            beside(1000)
            now = fence()
            t_cg = reload(CG, A["cg"], now) if not last else reload(CG[:, 0:3072], A["cg2"], now)
            post(cols, "ln2_g", "ln2_b", l, None)
            if not last:
                fence()
                fill_all()
                exact(t_cg)
                split_phase(WH0)
                hp[0] = modulate(l + 1, BOTH, 0, 1, of(ARR))

        in_turn[0] = 8
        X = slice(0, 256)
        QK = view(0, 16, 256)
        VX = AR[:, 4096:5632].rearrange("p (t h n) -> p t h n", t=2, h=6)
        TK = AR[:, 7168:8192].rearrange("p (a g n) -> p a g n", a=2, g=2)
        XW = AR[:, 8192:9152].rearrange("p (a k g n) -> p a k g n", a=2, k=16, g=2)
        HID = AR[:, 9152:9272].rearrange("p (a j n) -> p a j n", a=2, j=2)
        KCMP = AR[:, 9280:9296]
        VC = AR[0:15, 9296:9424]
        W2 = AR[:, 9600:9984].rearrange("p (j n) -> p j n", j=2)
        MIX = view(10240, 8, 256)
        PB = [AR[:, 12288 + 384 * i:12672 + 384 * i] for i in range(4)]
        PQ = [AR[:, 13824 + 384 * i:14208 + 384 * i] for i in range(4)]
        GQ = AR[:, 15360:15408].rearrange("p (t n) -> p t n", t=2)
        PC = AR[:, 15424:15664].rearrange("p (u q n) -> p u q n", u=8, q=2)
        PCT = AR[0:15, 15872:17920].rearrange("p (u n) -> p u n", u=8)
        TB = [AR[:, 17920 + 512 * i:18432 + 512 * i] for i in range(4)]
        CT8 = AR[0:4, 20224:20480]
        CNT = CG[:, 0:384]
        C01 = CG[:, 384:414].rearrange("p (q n) -> p q n", q=2)
        BNG = CG[:, 416:464].rearrange("p (l n) -> p l n", l=2)
        TRI = CG[:, 2176:2304]
        POSE = CG[:, 2320:2384].rearrange("p (l a k) -> p l a k", l=2, a=2)
        BFG = CG[:, 2400:2408].rearrange("p (l h) -> p l h", l=2)
        CBF = CG[:, 2560:3072].bitcast(BF16)
        IDB, MQ = CBF[:, 0:128], CBF[:, 128:512]
        DQ, CQM = CBF[:, 512:896], CBF[:, 896:1024]
        LFT = SM[:, 272:296].rearrange("p (a t h) -> p a t h", a=3, t=2)
        MX, NMX, DN, RC = (SM[:, 32 + 48 * i:80 + 48 * i].rearrange("p (u q) -> p u q", q=2) for i in range(4))
        CM_ = [SM[:, 224 + 16 * i:240 + 16 * i].rearrange("p (u q) -> p u q", q=2) for i in range(3)]


        def normed(l, name, at, toks):
            sq = view(at, 8, 256)
            b = ps()
            pe.wait(b.free)
            for k in range(8):
                t = af(sq[:, k, :], XT[:, k, X], ACT.Square, toks[k])
                t = mmt(b.ap[:, 0:256], M1024, sq[:, k, :], k == 0, k == 7, t)
            r, t = rstd_of(b, t, 256, 0)
            found = []
            for k in range(8):
                t1 = stt(HT[:, k, X], XT[:, k, X], col(name, l, k), r, ALU.mult, ALU.mult, t)
                if k:
                    found.append(part(of(HT), of(HTH2), of(HTR), k - 1, X, t0))
                t0 = t1
            found.append(part(of(HT), of(HTH2), of(HTR), 7, X, t0))
            return of(HTH2), of(HTR), found

        qk_t = {}

        def projections2(l):
            rope = {4, 5, 6, 7, 8, 9, 10, 12, 13, 14, 15}
            done = {}

            def raw(i):
                b, t = project("w_in2", l, i, hp[0], X)
                b.free = done[i] = qk_t[i] = af(QK[:, i, :], b.ap[:, 0:256], ACT.Copy, t)

            def rotate(i):
                if i not in rope:
                    return
                dst = QK[:, i, :]
                b = ps()
                t = mmt(b.ap[:, 0:256], R2, dst, True, True, b.free, done[i])
                tmp = TB[i % 2][:, 0:256]
                b.free = tt(dve, tmp, b.ap[:, 0:256], ROPE[:, 1, :], ALU.mult, t, dve.now())
                t = tt(dve, dst, dst, ROPE[:, 0, :], ALU.mult)
                qk_t[i] = tt(dve, dst, dst, tmp, ALU.add, t)

            def emit(n, b, tok, first):
                if first:
                    return af(VX[:, n, 0:4, :], b.ap[:, 0:512].rearrange("p (h n) -> p h n", h=4), ACT.Copy, tok)
                t = af(VX[:, n, 4:6, :], b.ap[:, 0:256].rearrange("p (h n) -> p h n", h=2), ACT.Copy, tok)
                t = tt(dve, LFT[:, 0, n, :], b.ap[:, 256:260], BFG[:, l, :], ALU.add, t)
                t = tt(dve, GQ[:, n, :], b.ap[:, 260:284], BNG[:, l, :], ALU.add, t)
                af(GQ[:, n, :], GQ[:, n, :], ACT.Sigmoid, t)
                return t
            project_tok("w_t1", l, 0, range(2), 284, 2, lambda n, b, tok: emit(n, b, tok, False), hp[0])
            project_tok("w_t0", l, 0, range(2), 512, 2, lambda n, b, tok: emit(n, b, tok, True), hp[0])
            t = af(LFT[:, 1], LFT[:, 0], ACT.Abs, dve.now())
            t = af(LFT[:, 1], LFT[:, 1], ACT.Exp, t, scale=-1.0)
            t = af(LFT[:, 1], LFT[:, 1], ACT.Ln, t, bias=1.0)
            t_lf = stt(LFT[:, 2], LFT[:, 0], 0.0, LFT[:, 1], ALU.min, ALU.subtract, t)
            lf = LFT[:, 2]
            for i in range(17):
                if i < 16:
                    raw(i)
                if i:
                    rotate(i - 1)
                if i == 3:
                    b = ps()
                    mm(b.ap[0:4, 0:128], lf[:, 0, :], TRI, True, True, b.free, t_lf)
                    mm(b.ap[0:4, 128:256], lf[:, 0, :], ONES, True, False)
                    mmt(b.ap[0:4, 128:256], lf[:, 1, :], TRI, False, True)
                    b.free = af(CT8, b.ap[0:4, 0:256], ACT.Copy, pe.now(), scale=-8.0)

        def compress(l, t_w2):
            dve.wait(qk_t[8], qk_t[11])
            for a, tile in ((0, 8), (1, 11)):
                for g in range(2):
                    src = QK[64 * g:64 * g + 64, tile, :]
                    copy(TK[0:64, a, g, :], src)
                    copy(TK[64:128, a, g, 0:255], src[:, 1:256])
            t = dve.now()
            for a in range(2):
                for g in range(2):
                    for h in range(2):
                        v = TK[:, a, g, 16 * h:16 * h + 240].rearrange("p (n k t) -> p k n t", k=8, t=2)[:, :, :, 0]
                        tt(dve, XW[:, a, 8 * h:8 * h + 8, g, :], v, bc(POSE[:, l, a, 8 * h:8 * h + 8], 2, 15),
                           ALU.add, t)
            t = dve.now()
            yield
            bs = []
            for a in range(2):
                b = [ps(), ps()]
                bs.append(b)
                pe.wait(b[0].free, b[1].free, t)
                for c in range(4):
                    i, tw = load(A["w_cmp"][l, 4 * a + c], 1024)
                    pe.wait(tw)
                    for k in range(4):
                        for j in range(2):
                            (mmt if k == 3 else mm)(
                                b[j].ap[:, 0:30], RING[:, i, 256 * k + 128 * j:256 * k + 128 * j + 128],
                                XW[:, a, 4 * c + k, :, :], c == 0 and k == 0, c == 3 and k == 3)
                    used_up(i)
            t = pe.now()
            for a in range(2):
                for j in range(2):
                    bs[a][j].free = af(HID[:, a, j, :], bs[a][j].ap[:, 0:30], ACT.Gelu_apprx_tanh, t)
            t = act.now()
            yield
            b = ps()
            pe.wait(b.free, t, t_w2)
            for j in range(2):
                (mmt if j else mm)(b.ap[:, 0:30], W2[:, j, 0:128], HID[:, 0, j, :], j == 0, j == 1)
            af(KCMP[0:64, 0:15], b.ap[0:64, 0:15], ACT.Copy, pe.now())
            b.free = af(KCMP[64:128, 0:15], b.ap[64:128, 15:30], ACT.Copy)
            b = ps()
            pe.wait(b.free)
            for g in range(2):
                for j in range(2):
                    mmt(b.ap[0:15, 64 * g:64 * g + 64], HID[:, 1, j, 15 * g:15 * g + 15], W2[:, j, 128:192],
                        j == 0, j == 1)
            b.free = t_kv[0] = af(VC, b.ap[0:15, 0:128], ACT.Copy, pe.now())

        t_kv = [None]

        ONE = (True, True)
        UNITS = [("fox", h % 2, h // 2, 2 + h // 2, h // 2, h // 2, None, ONE) for h in range(4)]
        UNITS += [("dil", h % 2, 12 + h // 2, 14 + h // 2, 4 + h // 2, 6 + h // 2, None, ONE) for h in range(4)]
        for i in range(4):
            for g in range(2):
                UNITS += [("sel", g, 4 + i, 9, 2, 2 + i, 1, (False, False)),
                          ("win", g, 4 + i, 10, 3, 2 + i, 2, (False, True))]

        def attention2(compressing):
            done = {}

            def weigh(u):
                kind, par, q, k, v, o, br, _ = UNITS[u]
                r = slice(64 * par, 64 * par + 64)
                pq = PQ[u % 4]
                b = ps()
                mm(b.ap[:, 0:384], IDB, DQ if kind == "dil" else MQ, True, False, b.free, qk_t[q], qk_t[k])
                if kind == "fox":
                    one = IDENT[0:4, u:u + 1].to_broadcast([4, P])
                    mm(b.ap[:, 0:128], one, CT8[:, 0:128], False, False)
                    mm(b.ap[:, 128:384], one, CT8[:, 0:256], False, False)
                mm(b.ap[:, 0:128], QK[r, q, 0:128], QK[r, k, 0:128], False, False)
                t = mmt(b.ap[:, 128:384], QK[r, q, 128:256], QK[r, k, 0:256], False, True)
                parts = ((0, slice(0, 128)), (1, slice(128, 384)))
                for qt, w in parts:
                    rmax(MX[:, u, qt:qt + 1], b.ap[:, w], t)
                t = ts(dve, NMX[:, u, :], MX[:, u, :], -SCALE2, None, ALU.mult, None, dve.now())
                for qt, w in parts:
                    b.free = t = af(pq[:, w], b.ap[:, w], ACT.Exp, t, done.get(("turned", u - 4)),
                                    bias=NMX[:, u, qt:qt + 1], scale=SCALE2, total=DN[:, u, qt:qt + 1])
                if kind == "dil":
                    for qt, w in parts:
                        x, c, d = pq[:, w], CNT[:, w], DN[:, u, qt:qt + 1]
                        t = dve.do(lambda e, x=x, c=c, d=d: e.scalar_tensor_tensor(
                            out=x, in0=x, scalar=1.0, in1=c, op0=ALU.mult, op1=ALU.mult, accum_out=d), b.free)
                done["exp", u] = t

            def scale(u):
                kind, par, q, k, v, o, br, _ = UNITS[u]
                pq = PQ[u % 4]
                parts = ((0, slice(0, 128)), (1, slice(128, 384)))
                t = recip(RC[:, u, :], DN[:, u, :], done["exp", u])
                if br is not None:
                    h = 4 * par + (o - 2)
                    t = tt(dve, RC[:, u, :], RC[:, u, :], GQ[:, :, 3 * h + br], ALU.mult, t)
                for qt, w in parts:
                    done["weighed", u] = ts(dve, pq[:, w], pq[:, w], RC[:, u, qt:qt + 1], None, ALU.mult, None, t)

            def turn_over(u):
                b = ps()
                pe.wait(b.free, done["weighed", u])
                for c, d in ((0, 0), (128, 128), (256, 256)):
                    t = transpose(b.ap[:, d:d + P], PQ[u % 4][:, c:c + P], P)
                done["turned", u] = t
                old = done.get(("values", u - 4))
                b.free = done["pb", u] = (copy(PB[u % 4], b.ap[:, 0:384], t, old) if u % 2 else
                                          af(PB[u % 4], b.ap[:, 0:384], ACT.Copy, t, old))

            def values(u):
                kind, par, q, k, v, o, br, (first, last) = UNITS[u]
                pt = PB[u % 4]
                b = banks[6 + o % 2]
                out_ = b.ap[:, 256 * par:256 * par + 256]
                pe.wait(b.free, done["pb", u])
                if kind == "sel":
                    mm(out_, VC, PCT[:, 2 * (o - 2) + par, :], True, False, t_cmp[0])
                mm(out_, VX[:, 0, v, :], pt[:, 0:256], first, False)
                t = done["values", u] = mmt(out_[:, 128:256], VX[:, 1, v, :], pt[:, 256:384], False, last)
                if last and par:
                    af(MIX[0:64, o, :], b.ap[0:64, 0:256], ACT.Copy, t)
                    b.free = af(MIX[64:128, o, :], b.ap[64:128, 256:512], ACT.Copy, t)

            t_cmp, t_pc = [None], [None]

            def compressed():
                m, d, r = CM_
                for par in range(2):
                    rows = slice(64 * par, 64 * par + 64)
                    b = ps()
                    mm(b.ap[:, 0:128], IDB, CQM, True, False, b.free, t_kv[0], [qk_t[i] for i in range(4, 8)])
                    for i in range(4):
                        for qt in range(2):
                            c = 32 * i + 16 * qt
                            mmt(b.ap[:, c:c + 15], QK[rows, 4 + i, 128 * qt:128 * qt + 128], KCMP[rows, 0:15], False,
                                i == 3 and qt == 1)
                    src = b.ap[:, 0:128].rearrange("p (u q n) -> p u q n", u=4, q=2)[:, :, :, 0:15]
                    pc = PC.rearrange("p (u two) q n -> p two u q n", two=2)[:, par]
                    b.free = dve.do(lambda e, pc=pc, src=src: e.tensor_copy(pc, src), pe.now())
                flat = PC.rearrange("p u q n -> p (u q) n")
                fm, fd, fr = (x.rearrange("p u q -> p (u q)") for x in (m, d, r))
                t = rmax(fm, flat, dve.now())
                t = tt(dve, flat, flat, bc(fm, 2, 15), ALU.subtract, t)
                t = af(flat, flat, ACT.Exp, t, scale=SCALE2)
                t = tt(dve, PC, PC, bc(C01, 1, 8), ALU.mult, t)
                t = dve.do(lambda e: e.tensor_reduce(fd, flat, AXX, ALU.add), t)
                t = ts(dve, fd, fd, 1e-30, None, ALU.max, None, t)
                t = recip(fr, fd, t)
                for u in range(8):
                    h = 4 * (u % 2) + u // 2
                    tt(dve, r[:, u, :], r[:, u, :], GQ[:, :, 3 * h], ALU.mult, t)
                t_pc[0] = tt(dve, flat, flat, bc(fr, 2, 15), ALU.mult, dve.now())

            def compressed_over():
                t = t_pc[0]
                for i in range(4):
                    b = ps()
                    pe.wait(b.free, t)
                    for j in range(4):
                        u, qt = 2 * i + j // 2, j % 2
                        transpose(b.ap[0:15, j * P:j * P + P], PC[:, u, qt, :], P)
                    b.free = t_cmp[0] = af(PCT[:, 2 * i:2 * i + 2, :],
                                           b.ap[0:15, :].rearrange("p (u n) -> p u n", u=2), ACT.Copy, pe.now())

            in_turn[0] = 6
            steps = [weigh, scale, lambda u: None, turn_over, values]
            for i in range(24 + len(steps) - 1):
                if i in (1, 3):
                    next(compressing, None)
                if i == 5:
                    compressed()
                if i == 8:
                    compressed_over()
                for n, f in enumerate(steps):
                    if 0 <= i - n < 24:
                        f(i - n)
            in_turn[0] = 8

        def mix_out(l, name, src, kt_total, norm, at):
            f = view(12288, 8, 256)
            sq = view(at, 8, 256)
            in_turn[0] = 7
            bm = banks[7]
            pe.wait(bm.free)
            t_sq = []
            for ct in range(9):
                if ct < 8:
                    b, t = project(name, l, ct, src, X, kt_total)
                    af(f[:, ct, :], b.ap[:, 0:256], ACT.Copy, t)
                    b.free = af(sq[:, ct, :], b.ap[:, 0:256], ACT.Square, t)
                    t_sq.append(b.free)
                if ct:
                    t = mmt(bm.ap[:, 0:256], M1024, sq[:, ct - 1, :], ct == 1, ct == 8, t_sq[ct - 1])
            in_turn[0] = 8
            r, t = rstd_of(bm, t, 256, 0)
            toks = []
            for k in range(8):
                t1 = stt(f[:, k, :], f[:, k, :], col(norm, l, k), r, ALU.mult, ALU.mult, t)
                if k:
                    toks.append(tt(dve, XT[:, k - 1, X], XT[:, k - 1, X], f[:, k - 1, :], ALU.add, t0))
                t0 = t1
            toks.append(tt(dve, XT[:, 7, X], XT[:, 7, X], f[:, 7, :], ALU.add, t0))
            return toks

        def ffn2(l):
            ffv = view(0, NFF, 256)
            ts_ = {}
            fp = of(ARR, 5632, 256), of(ARR, 0, 256), []

            def one(j):
                b, t = project("w_up", l, j, hp[0], X)
                tp = TB[(j // NFF + 2 * (j % NFF)) % 4][:, 0:256]
                w = [CVW[:, 44 * n + j:44 * n + j + 1] for n in range(3)]
                t = af(tp, b.ap[:, 0:256], ACT.Identity, t, ts_.get((j % NFF) - 2), t_cv[0],
                       bias=col("conv_b_2", l, j), scale=w[2])
                t = stt(tp[:, 1:256], b.ap[:, 0:255], w[1], tp[:, 1:256], ALU.mult, ALU.add, t)
                b.free = stt(tp[:, 2:256], b.ap[:, 0:254], w[0], tp[:, 2:256], ALU.mult, ALU.add, t)
                return tp, b.free

            for j in range(NFF):
                ta, t1 = one(j)
                tb, t2 = one(j + NFF)
                t1 = af(ta, ta, ACT.Silu, t1)
                if j:
                    fp[2].append(part(of(ffv), *fp[0:2], j - 1, X, ts_[j - 1]))
                ts_[j] = tt(dve, ffv[:, j, :], ta, tb, ALU.mult, t1, t2)
            fp[2].append(part(of(ffv), *fp[0:2], NFF - 1, X, ts_[NFF - 1]))
            return mix_out(l, "w_down", fp, NFF, "ffn_post_norm_2", 14336)

        fence()
        for e in (pe, dve, act, pool):
            e.wait(t_cg)
        split_phase(WH2)
        xt = [None] * 8
        for l in range(DEPTH):
            now = [e.now() for e in (pe, dve, act, pool)]
            t_cv[0] = reload(CVW[:, 0:132], A["cvw2"][l], now)
            t_w2 = reload(AR[:, 9600:9984], A["w2"][l], now)
            hp[0] = normed(l, "attn_pre_norm_2", 14336, xt)
            projections2(l)
            compressing = compress(l, t_w2)
            next(compressing)
            attention2(compressing)
            fence()
            mp = parts(of(MIX), of(ARR, 14336, 256), of(ARR, 10240, 256), X)
            xt = mix_out(l, "w_mix", mp, 8, "attn_post_norm_2", 18432)
            hp[0] = normed(l, "ffn_pre_norm_2", 18432, xt)
            xt = ffn2(l)
        sp.dma(out, XT[:, :, X], s_out, dve.now())
        sp.queue.append(lambda e: e.wait_ge(s_out, 16))

        sp.wait(late, [e.now() for e in (pe, dve, act, pool) if e.count])
        sp.wait([(slot_sem[i], 16 * slot_uses[i]) for i in range(NSLOT)])

        block = ctx.enter_context(nc.Block())

        def run(queue, e):
            for f in queue.whole():
                f(e)

        @block.sync
        def _(e):
            run(sp, e)

        @block.tensor
        def _(e):
            run(pe, e)

        @block.vector
        def _(e):
            run(dve, e)

        @block.scalar
        def _(e):
            run(act, e)

        @block.gpsimd
        def _(e):
            run(pool, e)


def shape_constants():
    f = np.float32
    i = np.arange(128)
    cm = np.zeros((128, 8, 128), f)
    cm[:, 0] = 1.0
    cm[:, 1] = 1.0 / 1024
    cm[:, 2] = 1.0 / 256
    cm[:, 3] = 1.0 / 128
    cm[:, 4] = np.eye(128)
    for m in range(0, 128, 2):
        cm[m + 1, 5, m] = -1.0
        cm[m, 5, m + 1] = 1.0
    for h in (0, 64):
        for d in range(8):
            cm[h + d + 8, 6, h + d] = -1.0
            cm[h + d, 6, h + d + 8] = 1.0
    s, t = i[:, None], i[None, :]
    cg = np.zeros((128, 5120), f)
    for n, m in enumerate((64, 32, 16, 8, 4, 2, 1)):
        mid = (i // (2 * m)) * 2 * m + m
        same = (s // (2 * m)) == (t // (2 * m))
        up_s, up_t = s >= mid[:, None], t >= mid[None, :]
        cg[:, 128 * n:128 * n + 128] = same & (up_s != up_t)
        md = mid[None, :]
        qf = up_t & (s >= md) & (s <= t)
        qb = ~up_t & (s >= t) & (s < md)
        kf = ~up_t & (s > t) & (s < md)
        kb = up_t & (s >= md) & (s < t)
        for base, q, k in ((1024, qf, kf), (2816, qb, kb)):
            cg[:, base + 128 * n:base + 128 * n + 128] = q
            cg[:, base + 896 + 128 * n:base + 1024 + 128 * n] = k
    cg[:, 896:1024] = 2.0 * np.eye(128)
    for n, m in enumerate((s <= t, s >= t, s > t, s < t)):
        cg[:, 4608 + 128 * n:4736 + 128 * n] = m
    pos = np.arange(256)
    inv = (np.float32(10000.0) ** (-np.arange(0, 64, 2, dtype=f) / f(64))).astype(f)
    ang = np.concatenate([(pos // 64).astype(f)[:, None] * inv, (pos % 64).astype(f)[:, None] * inv], 1)
    rope1 = np.stack([np.repeat(np.cos(ang).T, 2, 0), np.repeat(np.sin(ang).T, 2, 0)], 1).astype(f)
    return cm, cg, rope1


def shape_constants_2():
    f = np.float32
    i = np.arange(128)
    s, t = i[:, None], i[None, :]
    c = np.zeros((128, 3072), f)
    k, q = s, t
    off = lambda k0, q0: (q0 + q) - (k0 + k)

    def count(o):
        ok = o >= 0
        return (ok & (o <= 128)).astype(f) + (ok & (o % 4 == 0)) + (ok & (o % 16 == 0))
    parts = ((0, 0), (128, 0), (128, 128))
    for n, (q0, k0) in enumerate(parts):
        c[:, 128 * n:128 * n + 128] = count(off(k0, q0)).T
    ends = np.arange(15) * 16 + 31
    seen = ends[:, None] <= np.arange(256)[None, :]
    c[:, 384:399] = seen[:, 0:128].T
    c[:, 399:414] = seen[:, 128:256].T
    c[:, 2176:2304] = s <= t
    b = np.zeros((128, 1024), f)
    b[:, 0:128] = np.eye(128)
    for n, (q0, k0) in enumerate(parts):
        b[:, 128 + 128 * n:256 + 128 * n] = np.where(off(k0, q0).T >= 0, 0.0, MASKED)
        b[:, 512 + 128 * n:640 + 128 * n] = np.where(count(off(k0, q0)).T > 0, 0.0, MASKED)
    for u in range(4):
        for qt in range(2):
            a = 896 + 32 * u + 16 * qt
            b[:, a:a + 15] = np.where(seen[:, 128 * qt:128 * qt + 128].T, 0.0, MASKED)
    c[:, 2560:3072] = (b.view(np.uint32) >> 16).astype(np.uint16).view(f)
    return c


def by_features(w):
    n, k, c = w.shape
    return np.ascontiguousarray(
        w.reshape(n, k // 128, 128, c // 128, 128).transpose(0, 3, 2, 1, 4)).reshape(n, c // 128, 128, k)


def by_tokens(w, width, per):
    n, k, c = w.shape
    return np.ascontiguousarray(
        w.reshape(n, 8 // per, per, 128, c // width, width).transpose(0, 4, 1, 3, 2, 5)
    ).reshape(n, c // width * (8 // per), 128, per * width)


def narrow(w):
    n, k, c = w.shape
    return np.ascontiguousarray(w.reshape(n, 8, 128, c).transpose(0, 2, 1, 3)).reshape(n, 128, 8 * c)


def columns(v):
    return v.reshape(-1, 128).T


def arrange(inp):
    f = np.float32
    a = {}
    a["cm"], a["cg"], a["rope1"] = shape_constants()
    i = np.arange(128)
    inv = (f(500000.0) ** (f(-2.0) * np.arange(8, dtype=f) / f(16))).astype(f)
    inv = np.where(i % 64 < 16, inv[i % 8], 0.0).astype(f)[:, None]
    a["cols"] = np.concatenate([columns(inp[name][l]) for name, _ in COLS for l in range(DEPTH)]
                               + [np.full((128, 1), EPS, f), inv], 1)
    feat = lambda x: np.ascontiguousarray(x[0].T.reshape(8, 128, 256).transpose(1, 0, 2))
    a["x"], a["ctx"] = feat(inp["x"]), feat(inp["ctx"])
    a["cc"] = np.concatenate([columns(inp["c"][0]), columns(inp["c_ctx"])], 1)
    a["w_ada"] = by_tokens(inp["w_ada"], 512, 2)
    w = inp["w_in"]
    cut = lambda lo, n: w[:, :, lo:lo + n]
    a["w_k"] = by_features(cut(0, 256))
    a["w_v"] = by_tokens(cut(256, 256), 256, 4)
    a["w_kg"] = by_features(cut(512, 512))
    a["w_vg"] = by_tokens(cut(1024, 1024), 512, 2)
    a["w_glr"] = narrow(cut(2048, 32))
    a["w_q"] = by_features(cut(2080, 1024))
    a["w_qg"] = by_features(cut(3104, 512))
    a["w_r"] = by_features(cut(3616, 1024))
    a["w_glu"] = by_features(cut(4640, 2048))
    a["w_gates"] = by_features(cut(6688, 3072))
    for name in ("w_att_o", "w_gla_o", "w_conv_o", "w_out", "w_ff_gate", "w_ff_up", "w_ff_down"):
        a[name] = by_features(inp[name])
    wa = np.zeros((DEPTH, 33, 2, 512), f)
    for d in range(2):
        wa[:, 16 * d:16 * d + 16, d] = inp["gla_w_a2"][:, d]
        wa[:, 32, d] = inp["gla_b_a"][:, d]
    a["wa"] = wa
    a["cvw"] = np.ascontiguousarray(inp["conv_w_dw"][:, :, 0].reshape(DEPTH, 31, 8, 128).transpose(0, 3, 2, 1)
                                    ).reshape(DEPTH, 128, 248)
    a["pos"] = np.ascontiguousarray(inp["positions_2"][0])
    w = inp["w_in_2"]
    nq = w[:, :, 772:1284].reshape(DEPTH, 1024, 2, 4, 64).transpose(0, 1, 3, 2, 4).reshape(DEPTH, 1024, 512)
    kv = [w[:, :, 1284 + 128 * n:1412 + 128 * n] for n in range(6)]
    kc, vc, ks, vs, kw, vw = kv
    a["w_in2"] = by_features(np.concatenate(
        [w[:, :, 0:512], nq, kc, ks, kw, vc, w[:, :, 2076:2588]], 2))
    a["w_t0"] = by_tokens(np.concatenate([w[:, :, 512:768], vs, vw], 2), 512, 2)
    a["w_t1"] = by_tokens(np.concatenate([w[:, :, 2588:2844], w[:, :, 768:772], w[:, :, 2052:2076]], 2), 284, 2)
    w1 = np.stack([inp["cmp_w1_k_2"], inp["cmp_w1_v_2"]], 1)
    a["w_cmp"] = np.ascontiguousarray(
        w1.reshape(DEPTH, 2, 4, 4, 128, 256).transpose(0, 1, 2, 4, 3, 5)).reshape(DEPTH, 8, 128, 1024)
    w2k, w2v = (inp[n].reshape(DEPTH, 2, 128, 64).transpose(0, 2, 1, 3) for n in ("cmp_w2_k_2", "cmp_w2_v_2"))
    a["w2"] = np.ascontiguousarray(np.concatenate([w2k, w2k, w2v], 3)).reshape(DEPTH, 128, 384)
    cg2 = shape_constants_2()
    pe_ = np.stack([inp["cmp_pos_k_2"], inp["cmp_pos_v_2"]], 1)
    cg2[:, 2320:2384] = pe_.reshape(DEPTH, 2, 16, 128).transpose(3, 0, 1, 2).reshape(128, 64)
    cg2[:, 416:464] = np.broadcast_to(inp["b_nsa_gate_2"].reshape(1, 48), (128, 48))
    cg2[:, 2400:2408] = np.broadcast_to(inp["b_forget_2"].reshape(1, 8), (128, 8))
    a["cg2"] = cg2
    wo = inp["w_out_2"]
    mid = wo[:, 256:768].reshape(DEPTH, 2, 4, 64, 1024).transpose(0, 2, 1, 3, 4).reshape(DEPTH, 512, 1024)
    a["w_mix"] = by_features(np.concatenate([wo[:, 0:256], mid, wo[:, 768:1024]], 1))
    a["w_up"] = by_features(inp["w_up_2"])
    a["w_down"] = by_features(inp["w_down_2"])
    a["cvw2"] = np.ascontiguousarray(inp["conv_w_2"].reshape(DEPTH, 3, 44, 128).transpose(0, 3, 1, 2)
                                     ).reshape(DEPTH, 128, 132)
    return a


def kernel(**inputs):
    import concourse.bacc as _bacc
    from concourse.bass_utils import run_bass_kernel_spmd as _run

    inp = {k: np.asarray(v) for k, v in inputs.items()}
    arrays = {k + "_in": np.ascontiguousarray(v) for k, v in arrange(inp).items()}
    nc = _bacc.Bacc("TRN2", target_bir_lowering=False, num_devices=1)
    args = {}
    for name, a in arrays.items():
        args[name[:-3]] = nc.dram_tensor(name, a.shape, mybir.dt.from_np(a.dtype), kind="ExternalInput").ap()
    out = nc.dram_tensor("out", (128, 8, 256), F32, kind="ExternalOutput").ap()
    program(nc, args, out)
    r = _run(nc, [arrays], core_ids=[0])
    y = r.results[0]["out"]
    return np.ascontiguousarray(y.transpose(1, 0, 2).reshape(1024, 256).T)[None]
```
